# Optimizing a Trainium2 kernel written in Bass

```python
import numpy as np
import jax
import jax.numpy as jnp
from jax import lax
import jax, jax.numpy as jnp

D_MODEL = 1024
BATCH = 1
SEQ = 256
DEPTH = 1

MIX = D_MODEL // 2
GM_CHUNK = 128
GM_GROUPS = 4
GM_GW = MIX // GM_GROUPS
CONV_WIDTH = 4
LRU_BLOCKS = 8
LRU_BW = MIX // LRU_BLOCKS
LRU_C = 8.0
N_HEADS = 8
HEAD_DIM = MIX // N_HEADS
N_KV = 2
HPG = N_HEADS // N_KV
CMP_LEN = 32
CMP_STRIDE = 16
SLC_LEN = 64
SLC_TOPN = 8
WIN = 512
Q_BLOCK = 128
NSA_Q = N_HEADS * HEAD_DIM
NSA_KV = N_KV * HEAD_DIM
POOL_WINDOWS = (2, 4, 8, 16)
POOL_GROUPS = len(POOL_WINDOWS)
POOL_GW = MIX // POOL_GROUPS
N_BRANCH = 4
N_GROUPS = 4
EXPERTS_PER_GROUP = 4
N_EXPERTS = N_GROUPS * EXPERTS_PER_GROUP
EXPERT_TOPK = 2
D_EXPERT = D_MODEL // 2

EPS = 1e-6
NEG_INF = -1e30
FORCE_SCORE = 1e6

IN_SPLITS = (MIX, MIX, MIX, MIX, NSA_Q, 6 * NSA_KV, 3 * N_HEADS, MIX, N_BRANCH * D_MODEL)
N_IN = sum(IN_SPLITS)


def rms_norm(x, g):
    xf = x.astype(jnp.float32)
    y = xf * lax.rsqrt(jnp.mean(xf * xf, axis=-1, keepdims=True) + EPS)
    return (y * g.astype(jnp.float32)).astype(x.dtype)

def gmlp_mixer(u, v, v_norm_g, ws, bs):
    B, S, _ = u.shape
    nc = S // GM_CHUNK
    u = jax.nn.gelu(u)
    v = rms_norm(jax.nn.gelu(v), v_norm_g).reshape(B, nc, GM_CHUNK, GM_GROUPS, GM_GW)
    causal = jnp.tril(jnp.ones((GM_CHUNK, GM_CHUNK), dtype=bool))
    w = jnp.where(causal[None], ws, 0.0)
    mixed = jnp.einsum('gts,bnsgc->bntgc', w, v) + bs.T[:, :, None]
    return u * mixed.reshape(B, S, MIX)

def rglru_mixer(gate_in, x_in, conv_w, conv_b, wa, ba, wx, bx, lam):
    B, S, C = x_in.shape
    f32 = jnp.float32
    xp = jnp.pad(x_in, ((0, 0), (CONV_WIDTH - 1, 0), (0, 0)))
    xc = conv_b + sum(xp[:, k:k + S] * conv_w[k] for k in range(CONV_WIDTH))
    xb = xc.reshape(B, S, LRU_BLOCKS, LRU_BW)
    r = jax.nn.sigmoid(jnp.einsum('bshi,hij->bshj', xb, wa).reshape(B, S, C) + ba)
    i = jax.nn.sigmoid(jnp.einsum('bshi,hij->bshj', xb, wx).reshape(B, S, C) + bx)
    log_a = -LRU_C * r.astype(f32) * jax.nn.softplus(-lam.astype(f32))
    a = jnp.exp(log_a)
    b = jnp.sqrt(-jnp.expm1(2.0 * log_a)) * (i * xc).astype(f32)

    def combine(c1, c2):
        a1, b1 = c1
        a2, b2 = c2
        return a1 * a2, a2 * b1 + b2

    _, h = lax.associative_scan(combine, (a, b), axis=1)
    return jax.nn.gelu(gate_in) * h.astype(x_in.dtype)

def _gather_blocks(blocks, idx):
    return blocks[idx].reshape(idx.shape[0], -1, blocks.shape[-1])

_gather_bg = jax.vmap(jax.vmap(_gather_blocks))

def nsa_mixer(q, kv, gate_logits, cmp_pe, cmp_w1, cmp_w2):
    B, S, _ = q.shape
    f32 = jnp.float32
    scale = HEAD_DIM ** -0.5
    t_pos = jnp.arange(S)
    qh = q.reshape(B, S, N_KV, HPG, HEAD_DIM).transpose(0, 2, 3, 1, 4)
    kv = kv.reshape(B, S, 6, N_KV, HEAD_DIM).transpose(2, 0, 3, 1, 4)

    n_sub = CMP_LEN // CMP_STRIDE
    n_chunk = S // CMP_STRIDE
    n_cmp = n_chunk - n_sub + 1
    chunks = kv[0:2].reshape(2, B, N_KV, n_chunk, CMP_STRIDE, HEAD_DIM)
    blocks = jnp.concatenate([chunks[:, :, :, j:j + n_cmp] for j in range(n_sub)], axis=4)
    blocks = blocks + cmp_pe[:, None, None, None]
    flat = blocks.reshape(2, B, N_KV, n_cmp, CMP_LEN * HEAD_DIM)
    hid = jax.nn.gelu(jnp.einsum('cbgnf,cgfe->cbgne', flat, cmp_w1))
    kvc = jnp.einsum('cbgne,cged->cbgnd', hid, cmp_w2)
    k_c, v_c = kvc[0], kvc[1]
    cmp_end = jnp.arange(n_cmp) * CMP_STRIDE + (CMP_LEN - 1)
    cmp_mask = cmp_end[None, :] <= t_pos[:, None]
    s_c = jnp.einsum('bgjsd,bgnd->bgjsn', qh, k_c).astype(f32) * scale
    p_c = jax.nn.softmax(jnp.where(cmp_mask, s_c, NEG_INF), axis=-1)
    p_c = jnp.where(jnp.any(cmp_mask, axis=-1)[:, None], p_c, 0.0)
    o_cmp = jnp.einsum('bgjsn,bgnd->bgjsd', p_c.astype(q.dtype), v_c)

    n_slc = S // SLC_LEN
    topn = min(SLC_TOPN, n_slc)
    c_start = np.arange(n_cmp) * CMP_STRIDE
    s_start = np.arange(n_slc) * SLC_LEN
    overlap = ((c_start[:, None] <= s_start[None, :] + SLC_LEN - 1)
               & (c_start[:, None] + CMP_LEN - 1 >= s_start[None, :])).astype(np.float32)
    imp = jnp.einsum('bgjsn,nm->bgsm', p_c, jnp.asarray(overlap))
    blk = jnp.arange(n_slc)
    cur = t_pos // SLC_LEN
    causal_blk = blk[None, :] * SLC_LEN <= t_pos[:, None]
    forced = (blk[None, :] == 0) | (blk[None, :] == cur[:, None]) | (blk[None, :] == cur[:, None] - 1)
    score = jnp.where(forced, FORCE_SCORE, jnp.where(causal_blk, imp, -1.0))
    top_val, top_idx = lax.top_k(score, topn)
    top_ok = top_val >= 0.0

    nq = S // Q_BLOCK
    ks_blk = kv[2].reshape(B, N_KV, n_slc, SLC_LEN, HEAD_DIM)
    vs_blk = kv[3].reshape(B, N_KV, n_slc, SLC_LEN, HEAD_DIM)

    def slc_block(args):
        q_b, idx_b, ok_b, t_b = args
        k_sel = _gather_bg(ks_blk, idx_b)
        v_sel = _gather_bg(vs_blk, idx_b)
        k_pos = idx_b[..., None] * SLC_LEN + jnp.arange(SLC_LEN)
        ok = (ok_b[..., None] & (k_pos <= t_b[:, None, None])).reshape(B, N_KV, Q_BLOCK, -1)
        s = jnp.einsum('bgjqd,bgqkd->bgjqk', q_b, k_sel).astype(f32) * scale
        p = jax.nn.softmax(jnp.where(ok[:, :, None], s, NEG_INF), axis=-1)
        return jnp.einsum('bgjqk,bgqkd->bgjqd', p.astype(q_b.dtype), v_sel)

    q_blocks = qh.reshape(B, N_KV, HPG, nq, Q_BLOCK, HEAD_DIM).transpose(3, 0, 1, 2, 4, 5)
    idx_blocks = top_idx.reshape(B, N_KV, nq, Q_BLOCK, topn).transpose(2, 0, 1, 3, 4)
    ok_blocks = top_ok.reshape(B, N_KV, nq, Q_BLOCK, topn).transpose(2, 0, 1, 3, 4)
    o_slc = lax.map(slc_block, (q_blocks, idx_blocks, ok_blocks, t_pos.reshape(nq, Q_BLOCK)))
    o_slc = o_slc.transpose(1, 2, 3, 0, 4, 5).reshape(B, N_KV, HPG, S, HEAD_DIM)

    n_pad = WIN // Q_BLOCK
    band_len = Q_BLOCK * (n_pad + 1)
    kw = jnp.pad(kv[4], ((0, 0), (0, 0), (WIN, 0), (0, 0))).reshape(B, N_KV, nq + n_pad, Q_BLOCK, HEAD_DIM)
    vw = jnp.pad(kv[5], ((0, 0), (0, 0), (WIN, 0), (0, 0))).reshape(B, N_KV, nq + n_pad, Q_BLOCK, HEAD_DIM)
    band_k = jnp.concatenate([kw[:, :, j:j + nq] for j in range(n_pad + 1)], axis=3)
    band_v = jnp.concatenate([vw[:, :, j:j + nq] for j in range(n_pad + 1)], axis=3)
    qb = qh.reshape(B, N_KV, HPG, nq, Q_BLOCK, HEAD_DIM)
    s_w = jnp.einsum('bgjiqd,bgikd->bgjiqk', qb, band_k).astype(f32) * scale
    q_idx = jnp.arange(Q_BLOCK)
    k_idx = jnp.arange(band_len)
    delta = WIN + q_idx[:, None] - k_idx[None, :]
    k_abs = (jnp.arange(nq)[:, None] - n_pad) * Q_BLOCK + k_idx[None, :]
    win_mask = ((delta >= 0) & (delta < WIN))[None] & (k_abs >= 0)[:, None, :]
    p_w = jax.nn.softmax(jnp.where(win_mask, s_w, NEG_INF), axis=-1)
    o_win = jnp.einsum('bgjiqk,bgikd->bgjiqd', p_w.astype(q.dtype), band_v).reshape(B, N_KV, HPG, S, HEAD_DIM)

    g = jax.nn.sigmoid(gate_logits.reshape(B, S, N_KV, HPG, 3).transpose(4, 0, 2, 3, 1))[..., None]
    o = g[0] * o_cmp + g[1] * o_slc + g[2] * o_win
    return o.transpose(0, 3, 1, 2, 4).reshape(B, S, NSA_Q)

def pool_mixer(xd, pool_w, pool_scale):
    B, S, C = xd.shape
    f32 = jnp.float32
    xf = xd.astype(f32)
    csum = jnp.pad(lax.cumsum(xf, axis=1), ((0, 0), (1, 0), (0, 0)))
    t = jnp.arange(S)
    outs = []
    for gi, w in enumerate(POOL_WINDOWS):
        c = csum[:, :, gi * POOL_GW:(gi + 1) * POOL_GW]
        lower = jnp.pad(c[:, :S + 1 - w], ((0, 0), (w - 1, 0), (0, 0)))
        cnt = jnp.minimum(t + 1, w).astype(f32)[None, :, None]
        outs.append((c[:, 1:] - lower) / cnt - xf[:, :, gi * POOL_GW:(gi + 1) * POOL_GW])
    pooled = jnp.stack(outs, axis=2).astype(xd.dtype)
    mixed = jnp.einsum('bsgi,gij->bsgj', pooled, pool_w).reshape(B, S, C)
    return mixed * pool_scale

def hybrid_mixer(h, w_in, gm_norm_g, gm_ws, gm_b, conv_w, conv_b, lru_wa, lru_ba, lru_wx,
                 lru_bx, lru_lambda, cmp_pe, cmp_w1, cmp_w2, pool_w, pool_scale, w_branch, w_out):
    B, S, _ = h.shape
    proj = h @ w_in
    cuts = np.cumsum(IN_SPLITS)[:-1].tolist()
    u, v, gate_b, rec_b, q, kv, nsa_g, xd, mg = jnp.split(proj, cuts, axis=-1)
    y_a = gmlp_mixer(u, v, gm_norm_g, gm_ws, gm_b)
    y_b = rglru_mixer(gate_b, rec_b, conv_w, conv_b, lru_wa, lru_ba, lru_wx, lru_bx, lru_lambda)
    y_c = nsa_mixer(q, kv, nsa_g, cmp_pe, cmp_w1, cmp_w2)
    y_d = pool_mixer(xd, pool_w, pool_scale)
    ys = jnp.stack([y_a, y_b, y_c, y_d])
    branch = jnp.einsum('nbsc,ncd->bsnd', ys, w_branch)
    gates = jax.nn.sigmoid(mg.reshape(B, S, N_BRANCH, D_MODEL))
    merged = jnp.sum(gates * branch, axis=2)
    return merged @ w_out

def hier_moe(h, wr_g, br_g, wr_e, br_e, w_gate, w_up, w_down):
    B, S, D = h.shape
    f32 = jnp.float32
    t = h.reshape(-1, D)
    T = t.shape[0]
    grp_p = jax.nn.softmax((t @ wr_g + br_g).astype(f32), axis=-1)
    grp_w, grp_idx = lax.top_k(grp_p, 1)
    exp_logits = (t @ wr_e + br_e).astype(f32).reshape(T, N_GROUPS, EXPERTS_PER_GROUP)
    in_grp = jnp.einsum('tge,tg->te', exp_logits, jax.nn.one_hot(grp_idx[:, 0], N_GROUPS, dtype=f32))
    top_l, top_e = lax.top_k(in_grp, EXPERT_TOPK)
    top_w = jax.nn.softmax(top_l, axis=-1) * grp_w
    expert_id = grp_idx * EXPERTS_PER_GROUP + top_e
    combine = jnp.sum(jax.nn.one_hot(expert_id, N_EXPERTS, dtype=f32) * top_w[..., None], axis=1)
    hid = jax.nn.silu(jnp.einsum('td,edf->etf', t, w_gate)) * jnp.einsum('td,edf->etf', t, w_up)
    hid = hid * combine.T[:, :, None].astype(hid.dtype)
    out = jnp.einsum('etf,efd->td', hid, w_down)
    return out.reshape(B, S, D)

def first_inputs(seed: int = 0) -> dict:
    key = jax.random.key(seed)
    ks = iter(jax.random.split(key, 40))
    f32 = jnp.float32
    L = DEPTH

    def nrm(shape, scale):
        return jax.random.normal(next(ks), shape, f32) * scale

    def gain(shape):
        return 1.0 + 0.02 * jax.random.normal(next(ks), shape, f32)

    a_c = jax.random.uniform(next(ks), (L, MIX), f32, minval=0.9, maxval=0.999)
    a0 = a_c ** (1.0 / LRU_C)
    lru_lambda = jnp.log(a0) - jnp.log1p(-a0)
    return {
        'x': nrm((BATCH, SEQ, D_MODEL), 1.0),
        'norm1_g': gain((L, D_MODEL)),
        'w_in': nrm((L, D_MODEL, N_IN), D_MODEL ** -0.5),
        'gm_norm_g': gain((L, MIX)),
        'gm_ws': nrm((L, GM_GROUPS, GM_CHUNK, GM_CHUNK), GM_CHUNK ** -0.5),
        'gm_b': gain((L, GM_GROUPS, GM_CHUNK)),
        'conv_w': nrm((L, CONV_WIDTH, MIX), CONV_WIDTH ** -0.5),
        'conv_b': nrm((L, MIX), 0.02),
        'lru_wa': nrm((L, LRU_BLOCKS, LRU_BW, LRU_BW), LRU_BW ** -0.5),
        'lru_ba': nrm((L, MIX), 0.02),
        'lru_wx': nrm((L, LRU_BLOCKS, LRU_BW, LRU_BW), LRU_BW ** -0.5),
        'lru_bx': nrm((L, MIX), 0.02),
        'lru_lambda': lru_lambda,
        'cmp_pe': nrm((L, 2, CMP_LEN, HEAD_DIM), 0.02),
        'cmp_w1': nrm((L, 2, N_KV, CMP_LEN * HEAD_DIM, HEAD_DIM), (CMP_LEN * HEAD_DIM) ** -0.5),
        'cmp_w2': nrm((L, 2, N_KV, HEAD_DIM, HEAD_DIM), HEAD_DIM ** -0.5),
        'pool_w': nrm((L, POOL_GROUPS, POOL_GW, POOL_GW), POOL_GW ** -0.5),
        'pool_scale': gain((L, MIX)),
        'w_branch': nrm((L, N_BRANCH, MIX, D_MODEL), MIX ** -0.5),
        'w_out': nrm((L, D_MODEL, D_MODEL), D_MODEL ** -0.5),
        'norm2_g': gain((L, D_MODEL)),
        'router_w_group': nrm((L, D_MODEL, N_GROUPS), D_MODEL ** -0.5),
        'router_b_group': nrm((L, N_GROUPS), 0.01),
        'router_w_expert': nrm((L, D_MODEL, N_EXPERTS), D_MODEL ** -0.5),
        'router_b_expert': nrm((L, N_EXPERTS), 0.01),
        'moe_w_gate': nrm((L, N_EXPERTS, D_MODEL, D_EXPERT), D_MODEL ** -0.5),
        'moe_w_up': nrm((L, N_EXPERTS, D_MODEL, D_EXPERT), D_MODEL ** -0.5),
        'moe_w_down': nrm((L, N_EXPERTS, D_EXPERT, D_MODEL), D_EXPERT ** -0.5),
        'final_norm_g': gain((D_MODEL,)),
    }

def first_block(x, norm1_g, w_in, gm_norm_g, gm_ws, gm_b, conv_w, conv_b, lru_wa, lru_ba, lru_wx,
              lru_bx, lru_lambda, cmp_pe, cmp_w1, cmp_w2, pool_w, pool_scale, w_branch, w_out,
              norm2_g, router_w_group, router_b_group, router_w_expert, router_b_expert,
              moe_w_gate, moe_w_up, moe_w_down, final_norm_g):
    h = x
    for l in range(DEPTH):
        h = h + hybrid_mixer(rms_norm(h, norm1_g[l]), w_in[l], gm_norm_g[l], gm_ws[l], gm_b[l],
                             conv_w[l], conv_b[l], lru_wa[l], lru_ba[l], lru_wx[l], lru_bx[l],
                             lru_lambda[l], cmp_pe[l], cmp_w1[l], cmp_w2[l], pool_w[l],
                             pool_scale[l], w_branch[l], w_out[l])
        h = h + hier_moe(rms_norm(h, norm2_g[l]), router_w_group[l], router_b_group[l],
                         router_w_expert[l], router_b_expert[l], moe_w_gate[l], moe_w_up[l],
                         moe_w_down[l])
    return rms_norm(h, final_norm_g)


DEPTH_2 = 2

CHUNK = 64
HEAD_DIM_2 = 64
NORM_EPS = 1e-6
D_RWKV = D_MODEL // 2
N_RWKV_HEADS = D_RWKV // HEAD_DIM_2
D_CONV = D_MODEL // 2
CONV_WIDTH_2 = 31
LORA_DECAY = 64
LORA_ICLR = 64
LORA_GATE = 128
GN_EPS = 1e-5 * HEAD_DIM_2
CONV_LN_EPS = 1e-5
COLS_RWKV = 3 * D_RWKV + LORA_DECAY + LORA_ICLR + LORA_GATE
COLS_A = COLS_RWKV + 2 * D_CONV
N_FOX_HEADS = D_MODEL // HEAD_DIM_2
D_FOX = N_FOX_HEADS * HEAD_DIM_2
COLS_C = 4 * D_FOX + N_FOX_HEADS
D_FF = 2816
N_A_LAYERS = (DEPTH_2 + 1) // 2
N_C_LAYERS = DEPTH_2 // 2


def rms_norm_2(x, g):
    xf = x.astype(jnp.float32)
    y = xf * lax.rsqrt(jnp.mean(xf * xf, axis=-1, keepdims=True) + NORM_EPS)
    return (y * g.astype(jnp.float32)).astype(x.dtype)

def layer_norm(x, g, b, eps):
    xf = x.astype(jnp.float32)
    mu = jnp.mean(xf, axis=-1, keepdims=True)
    xc = xf - mu
    y = xc * lax.rsqrt(jnp.mean(xc * xc, axis=-1, keepdims=True) + eps)
    return (y * g.astype(jnp.float32) + b.astype(jnp.float32)).astype(x.dtype)

def swiglu(x, w_gate, w_up, w_down):
    return (jax.nn.silu(x @ w_gate) * (x @ w_up)) @ w_down

def split_cols(t, sizes):
    out, start = [], 0
    for s in sizes:
        out.append(t[..., start:start + s])
        start += s
    return out

def rwkv7_scan(r, w, k, v, kk, a):
    b, _, h, n = r.shape

    def step(state, inp):
        r_t, w_t, k_t, v_t, kk_t, a_t = inp
        s_kk = jnp.einsum('bhvk,bhk->bhv', state, kk_t)
        state = (state * w_t[:, :, None, :]
                 - s_kk[..., None] * (kk_t * a_t)[:, :, None, :]
                 + v_t[..., None] * k_t[:, :, None, :])
        y_t = jnp.einsum('bhvk,bhk->bhv', state, r_t)
        return state, y_t

    xs = tuple(jnp.moveaxis(t, 1, 0) for t in (r, w, k, v, kk, a))
    s0 = jnp.zeros((b, h, n, n), jnp.float32)
    _, ys = lax.scan(step, s0, xs)
    return jnp.moveaxis(ys, 0, 1)

def mixer_ab(h, w_in, shift_mu, decay_up, decay_base, iclr_up, iclr_base, gate_up,
             k_k, k_a, r_k, lnx_g, lnx_b, conv_w, conv_b, conv_ln_g, conv_ln_b, w_out):
    b, t, _ = h.shape
    f32 = jnp.float32
    proj = h @ w_in
    p = proj[..., :COLS_RWKV]
    p_prev = jnp.pad(p, ((0, 0), (1, 0), (0, 0)))[:, :-1]
    p = p + shift_mu * (p_prev - p)
    r, k, v, d_w, d_a, d_g = split_cols(p, [D_RWKV, D_RWKV, D_RWKV, LORA_DECAY, LORA_ICLR, LORA_GATE])
    w_log = -jax.nn.softplus(-(decay_base + jnp.tanh(d_w) @ decay_up)) - 0.5
    decay = jnp.exp(-jnp.exp(w_log.astype(f32)))
    a = jax.nn.sigmoid(iclr_base + d_a @ iclr_up).astype(f32)
    g = jax.nn.sigmoid(d_g) @ gate_up
    r = r.astype(f32)
    k = k.astype(f32)
    v = v.astype(f32)
    kk = (k * k_k.astype(f32)).reshape(b, t, N_RWKV_HEADS, HEAD_DIM_2)
    kk = kk * lax.rsqrt(jnp.maximum(jnp.sum(kk * kk, axis=-1, keepdims=True), 1e-24))
    k = k * (1.0 + (a - 1.0) * k_a.astype(f32))
    hs = lambda z: z.reshape(b, t, N_RWKV_HEADS, HEAD_DIM_2)
    rh, kh, vh = hs(r), hs(k), hs(v)
    y = rwkv7_scan(rh, hs(decay), kh, vh, kk, hs(a))
    mu = jnp.mean(y, axis=-1, keepdims=True)
    yc = y - mu
    y = yc * lax.rsqrt(jnp.mean(yc * yc, axis=-1, keepdims=True) + GN_EPS)
    y = y.reshape(b, t, D_RWKV) * lnx_g.astype(f32) + lnx_b.astype(f32)
    bonus = jnp.sum(rh * kh * r_k.astype(f32), axis=-1, keepdims=True) * vh
    y_a = ((y + bonus.reshape(b, t, D_RWKV)) * g.astype(f32)).astype(h.dtype)
    c_val, c_gate = split_cols(proj[..., COLS_RWKV:], [D_CONV, D_CONV])
    glu = c_val * jax.nn.sigmoid(c_gate)
    conv = lax.conv_general_dilated(
        glu, conv_w[:, None, :], window_strides=(1,), padding=[(CONV_WIDTH_2 - 1, 0)],
        dimension_numbers=('NWC', 'WIO', 'NWC'), feature_group_count=D_CONV) + conv_b
    y_b = jax.nn.silu(layer_norm(conv, conv_ln_g, conv_ln_b, CONV_LN_EPS))
    return jnp.concatenate([y_a, y_b], axis=-1) @ w_out

def mixer_c(h, w_in, forget_bias, q_norm_g, k_norm_g, w_out):
    b, t, _ = h.shape
    f32 = jnp.float32
    proj = h @ w_in
    q, k, v, gate, f_logit = split_cols(proj, [D_FOX, D_FOX, D_FOX, D_FOX, N_FOX_HEADS])
    q = rms_norm_2(q.reshape(b, t, N_FOX_HEADS, HEAD_DIM_2), q_norm_g) * (HEAD_DIM_2 ** -0.5)
    k = rms_norm_2(k.reshape(b, t, N_FOX_HEADS, HEAD_DIM_2), k_norm_g)
    v = v.reshape(b, t, N_FOX_HEADS, HEAD_DIM_2)
    log_f = jax.nn.log_sigmoid((f_logit + forget_bias).astype(f32))
    cum = jnp.transpose(jnp.cumsum(log_f, axis=1), (0, 2, 1))
    outs = []
    for blk in range(t // Q_BLOCK):
        q0 = blk * Q_BLOCK
        k_end = q0 + Q_BLOCK
        s = jnp.einsum('bqhd,bkhd->bhqk', q[:, q0:k_end], k[:, :k_end],
                       preferred_element_type=f32)
        s = s + cum[:, :, q0:k_end, None] - cum[:, :, None, :k_end]
        q_pos = q0 + jnp.arange(Q_BLOCK)
        mask = q_pos[:, None] >= jnp.arange(k_end)[None, :]
        prob = jax.nn.softmax(jnp.where(mask, s, -jnp.inf), axis=-1)
        outs.append(jnp.einsum('bhqk,bkhd->bqhd', prob.astype(v.dtype), v[:, :k_end]))
    o = jnp.concatenate(outs, axis=1).reshape(b, t, D_FOX)
    o = o * jax.nn.sigmoid(gate)
    return o @ w_out

def second_inputs(seed: int = 0) -> dict:
    key = jax.random.key(seed)
    ks = list(jax.random.split(key, 40))

    def nrm(i, shape, scale):
        return scale * jax.random.normal(ks[i], shape, jnp.float32)

    def uni(i, shape, lo, hi):
        return jax.random.uniform(ks[i], shape, jnp.float32, minval=lo, maxval=hi)

    na, nc = N_A_LAYERS, N_C_LAYERS
    return {
        "x": nrm(0, (BATCH, SEQ, D_MODEL), 1.0),
        "norm_gains": 1.0 + nrm(1, (DEPTH_2, 6, D_MODEL), 0.02),
        "ffn_w_gate": nrm(2, (DEPTH_2, 2, D_MODEL, D_FF), D_MODEL ** -0.5),
        "ffn_w_up": nrm(3, (DEPTH_2, 2, D_MODEL, D_FF), D_MODEL ** -0.5),
        "ffn_w_down": nrm(4, (DEPTH_2, 2, D_FF, D_MODEL), D_FF ** -0.5),
        "a_w_in": nrm(5, (na, D_MODEL, COLS_A), D_MODEL ** -0.5),
        "a_shift_mu": uni(6, (na, COLS_RWKV), 0.0, 1.0),
        "a_decay_up": nrm(7, (na, LORA_DECAY, D_RWKV), 0.1),
        "a_decay_base": uni(8, (na, D_RWKV), -6.0, 1.0),
        "a_iclr_up": nrm(9, (na, LORA_ICLR, D_RWKV), 0.5 * LORA_ICLR ** -0.5),
        "a_iclr_base": nrm(10, (na, D_RWKV), 0.5),
        "a_gate_up": nrm(11, (na, LORA_GATE, D_RWKV), LORA_GATE ** -0.5),
        "a_k_k": 0.85 + nrm(12, (na, D_RWKV), 0.05),
        "a_k_a": 1.0 + nrm(13, (na, D_RWKV), 0.05),
        "a_r_k": nrm(14, (na, N_RWKV_HEADS, HEAD_DIM_2), 0.1),
        "a_lnx_g": 1.0 + nrm(15, (na, D_RWKV), 0.02),
        "a_lnx_b": nrm(16, (na, D_RWKV), 0.02),
        "b_conv_w": nrm(17, (na, CONV_WIDTH_2, D_CONV), CONV_WIDTH_2 ** -0.5),
        "b_conv_b": nrm(18, (na, D_CONV), 0.02),
        "b_ln_g": 1.0 + nrm(19, (na, D_CONV), 0.02),
        "b_ln_b": nrm(20, (na, D_CONV), 0.02),
        "ab_w_out": nrm(21, (na, D_RWKV + D_CONV, D_MODEL), (D_RWKV + D_CONV) ** -0.5),
        "c_w_in": nrm(22, (nc, D_MODEL, COLS_C), D_MODEL ** -0.5),
        "c_forget_bias": 2.0 + nrm(23, (nc, N_FOX_HEADS), 0.5),
        "c_q_norm_g": 1.0 + nrm(24, (nc, HEAD_DIM_2), 0.02),
        "c_k_norm_g": 1.0 + nrm(25, (nc, HEAD_DIM_2), 0.02),
        "c_w_out": nrm(26, (nc, D_FOX, D_MODEL), D_FOX ** -0.5),
    }

def second_block(x, norm_gains, ffn_w_gate, ffn_w_up, ffn_w_down,
              a_w_in, a_shift_mu, a_decay_up, a_decay_base, a_iclr_up, a_iclr_base, a_gate_up,
              a_k_k, a_k_a, a_r_k, a_lnx_g, a_lnx_b,
              b_conv_w, b_conv_b, b_ln_g, b_ln_b, ab_w_out,
              c_w_in, c_forget_bias, c_q_norm_g, c_k_norm_g, c_w_out):
    for layer in range(DEPTH_2):
        g = norm_gains[layer]
        f = swiglu(rms_norm_2(x, g[0]), ffn_w_gate[layer, 0], ffn_w_up[layer, 0], ffn_w_down[layer, 0])
        x = x + 0.5 * rms_norm_2(f, g[1])
        h = rms_norm_2(x, g[2])
        i = layer // 2
        if layer % 2 == 0:
            m = mixer_ab(h, a_w_in[i], a_shift_mu[i], a_decay_up[i], a_decay_base[i],
                         a_iclr_up[i], a_iclr_base[i], a_gate_up[i], a_k_k[i], a_k_a[i],
                         a_r_k[i], a_lnx_g[i], a_lnx_b[i], b_conv_w[i], b_conv_b[i],
                         b_ln_g[i], b_ln_b[i], ab_w_out[i])
        else:
            m = mixer_c(h, c_w_in[i], c_forget_bias[i], c_q_norm_g[i], c_k_norm_g[i], c_w_out[i])
        x = x + rms_norm_2(m, g[3])
        f = swiglu(rms_norm_2(x, g[4]), ffn_w_gate[layer, 1], ffn_w_up[layer, 1], ffn_w_down[layer, 1])
        x = x + 0.5 * rms_norm_2(f, g[5])
    return x


def setup_inputs(seed=0):
    out = dict(first_inputs(seed))
    for name, value in second_inputs(seed + 1).items():
        if name != "x":
            out[name + "_2"] = value
    return out


def reference(
    x, norm1_g, w_in, gm_norm_g, gm_ws, gm_b, conv_w, conv_b, lru_wa, lru_ba, lru_wx, lru_bx,
    lru_lambda, cmp_pe, cmp_w1, cmp_w2, pool_w, pool_scale, w_branch, w_out, norm2_g,
    router_w_group, router_b_group, router_w_expert, router_b_expert, moe_w_gate, moe_w_up,
    moe_w_down, final_norm_g, norm_gains_2, ffn_w_gate_2, ffn_w_up_2, ffn_w_down_2, a_w_in_2,
    a_shift_mu_2, a_decay_up_2, a_decay_base_2, a_iclr_up_2, a_iclr_base_2, a_gate_up_2,
    a_k_k_2, a_k_a_2, a_r_k_2, a_lnx_g_2, a_lnx_b_2, b_conv_w_2, b_conv_b_2, b_ln_g_2, b_ln_b_2,
    ab_w_out_2, c_w_in_2, c_forget_bias_2, c_q_norm_g_2, c_k_norm_g_2, c_w_out_2,
):
    x = first_block(
        x, norm1_g, w_in, gm_norm_g, gm_ws, gm_b, conv_w, conv_b, lru_wa, lru_ba, lru_wx,
        lru_bx, lru_lambda, cmp_pe, cmp_w1, cmp_w2, pool_w, pool_scale, w_branch, w_out,
        norm2_g, router_w_group, router_b_group, router_w_expert, router_b_expert, moe_w_gate,
        moe_w_up, moe_w_down, final_norm_g,
    )
    return second_block(
        x, norm_gains_2, ffn_w_gate_2, ffn_w_up_2, ffn_w_down_2, a_w_in_2, a_shift_mu_2,
        a_decay_up_2, a_decay_base_2, a_iclr_up_2, a_iclr_base_2, a_gate_up_2, a_k_k_2, a_k_a_2,
        a_r_k_2, a_lnx_g_2, a_lnx_b_2, b_conv_w_2, b_conv_b_2, b_ln_g_2, b_ln_b_2, ab_w_out_2,
        c_w_in_2, c_forget_bias_2, c_q_norm_g_2, c_k_norm_g_2, c_w_out_2,
    )


_drawn_inputs = setup_inputs


def setup_inputs(seed=0):
    import zlib

    import numpy as np

    out = dict(_drawn_inputs(seed))
    spreads = {}
    factors = {'gm_norm_g': 8.0,
     'gm_b': 2.703,
     'lru_ba': 8.0,
     'lru_bx': 8.0,
     'cmp_pe': 8.0,
     'pool_scale': 2.914,
     'router_b_expert': 4.842,
     'a_lnx_g_2': 4.844,
     'a_lnx_b_2': 3.607,
     'b_ln_g_2': 3.477,
     'b_ln_b_2': 3.665,
     'c_q_norm_g_2': 7.591,
     'c_k_norm_g_2': 8.0,
     'router_b_group': 8.0}
    for name, (base, spread) in spreads.items():
        noise = np.random.default_rng([zlib.crc32(name.encode()), seed]).standard_normal(out[name].shape)
        drawn = base * np.exp(spread * noise) if base else spread * noise
        out[name] = jnp.asarray(drawn.astype(out[name].dtype))
    for name, factor in factors.items():
        out[name] = (out[name] * factor).astype(out[name].dtype)
    return out
```

```python
import numpy as np
import concourse.bass as bass
from concourse import mybir
from contextlib import ExitStack

FP32 = mybir.dt.float32
BF16 = mybir.dt.bfloat16
ACT = mybir.ActivationFunctionType
ALU = mybir.AluOpType
AX = mybir.AxisListType

P = 128
D = 1024
T = 256
KD = D // P
MIX = 512
MT = MIX // P
TT = T // P
UNIT = 2048
UC = UNIT // KD
RING = 6
N_EXP = 16
D_EXP = 512
D_FF = 2816
N_HEADS, N_TYPES = 8, 3
N_CMP = 15
N_FOX = 16
N_RW = 8
HD = 64
CONV_A = 4
CONV_B = 31
WINDOWS = (2, 4, 8, 16)
NEG = -1e30
EPS = 1e-6
GN_EPS = 1e-5 * HD
LN_EPS = 1e-5
ARENA = 26520
SIDES_2 = ["n3", "n4", "n5", "gu0", "gu1", "kk0", "kk1", "bo0", "bo1", "ln1", "ln2", "n6", "n7", "n8", "n9", "n10", "n11"]\
    + [f"hs{n}" for n in range(8)] + ["f"] + [f"cb{n}" for n in range(8)] + ["n12", "n13", "n14"]
SCALE = HD ** -0.5
MOE_STEPS = N_EXP * D_EXP // UC
FFN_STEPS = D_FF // UC


def offsets(parts):
    at, table = 0, {}
    for name, width in parts:
        table[name] = (at, width)
        at += width
    return table, at


SMALL_1 = [("n1", KD), ("n2", KD), ("nf", KD), ("gm_g", MT), ("conv_w", CONV_A * MT), ("conv_b", MT),
           ("ba", MT), ("bx", MT), ("lam", MT), ("pool_s", MT), ("pe", 64), ("gm_wT", MIX), ("wa", MIX),
           ("wx", MIX), ("pool_w", MIX), ("cw2", 128), ("w_gate", KD * 24), ("w_route", KD * 20),
           ("gm_b", MIX), ("b_route", 20)]
SMALL_2 = [("n", 12 * KD), ("mu", 14), ("d_base", MT), ("i_base", MT), ("k_k", MT), ("k_a", MT),
           ("r_k", MT), ("lnx_g", MT), ("lnx_b", MT), ("conv_w", CONV_B * MT), ("conv_b", MT),
           ("ln_g", MT), ("ln_b", MT), ("qg", 1), ("kg", 1), ("fb", 1), ("lora", MIX), ("gate_up", MIX),
           ("w_f", KD * N_FOX)]
LEVELS = [1 << n for n in range(7)]
N_INV = 4 * (len(LEVELS) - 1)
CONSTS = [("ident", P), ("mask3", 3 * P), ("head1", P), ("cmp_add", 2 * 16), ("cmp_01", 2 * 16),
          ("level", len(LEVELS) * P), ("s_le_t", P), ("gram", 4 * P), ("level_t", P), ("pool_n", 4 * 16),
          ("keep", T), ("ones", P), ("eps", 4)]
OFF_1, W_1 = offsets(SMALL_1)
OFF_2, W_2 = offsets(SMALL_2)
OFF_C, W_C = offsets(CONSTS)


def constants():
    c = np.zeros((P, W_C), np.float32)

    def put(name, value):
        a, w = OFF_C[name]
        c[:, a:a + w] = np.asarray(value, np.float32).reshape(P, w)
    i = np.arange(P)
    put("ident", np.eye(P))
    diag = np.where(i[None, :] <= i[:, None], 0.0, NEG)
    put("mask3", np.concatenate([diag, np.zeros((P, P)), diag], 1))
    put("head1", i[:, None] // HD == i[None, :] // HD)
    t = (np.arange(TT)[None, :, None] * P + i[:, None, None])
    seen = (np.arange(16)[None, None, :] * 16 + 31 <= t) & (np.arange(16) < N_CMP)
    put("cmp_add", np.where(seen, 0.0, NEG))
    put("cmp_01", seen)
    put("level", np.stack([(i[:, None] // (2 * b) == i[None, :] // (2 * b)) & (i[:, None] // b < i[None, :] // b)
                           for b in LEVELS], 1))
    put("s_le_t", i[:, None] <= i[None, :])
    first = (i[:, None] // 2 == i[None, :] // 2) & (i[:, None] < i[None, :])
    put("gram", np.stack([i[:, None] < i[None, :], i[:, None] <= i[None, :], -1.0 * first, -1.0 * (i[:, None] <= i[None, :])], 1))
    put("level_t", -1.0 * first.T)
    put("pool_n", np.broadcast_to(np.stack([1.0 / np.minimum(np.arange(16) + 1, w) for w in WINDOWS])[None], (P, 4, 16)))
    put("keep", np.broadcast_to((np.arange(T) % P != 0)[None], (P, T)))
    put("ones", np.ones((P, P)))
    put("eps", np.broadcast_to(np.array([EPS, GN_EPS, LN_EPS, 0.0])[None], (P, 4)))
    return c


PROJ_1 = 31
BRANCH = 8
SQUARE = 4
PROJ_AB = 11
PROJ_C = 16
AB_ORDER = [6, 0, 1, 2, 3, 4, 5, 9, 10, 7, 8]


def column_units(w):
    return w.reshape(KD, P, -1, UC).transpose(2, 1, 0, 3).reshape(-1, P, UNIT)


def row_units(w):
    return w.reshape(-1, 2, P, D).transpose(0, 2, 1, 3).reshape(-1, P, UNIT)


def gated_units(gate, up, down):
    g, u, d = column_units(gate), column_units(up), row_units(down)
    order = [g[0], u[0]]
    for n in range(1, len(g)):
        order += [g[n], u[n], d[n - 1]]
    return order + [d[-1]]


def cols(v):
    return v.reshape(-1, P).T


def pack(parts, given):
    out = np.zeros((P, sum(w for _, w in parts)), np.float32)
    table, _ = offsets(parts)
    for name, (a, w) in table.items():
        v = given[name]
        v = v.reshape(v.shape[0], w)
        out[:v.shape[0], a:a + w] = v
    return out


def block_diagonal(w):
    out = np.zeros((P, MT, P), np.float32)
    for b in range(8):
        h = b % 2
        out[HD * h:HD * h + HD, b // 2, HD * h:HD * h + HD] = w[b]
    return out


def lay_out(a):
    a = {k: np.asarray(v) for k, v in a.items()}
    w_in = a["w_in"][0]
    first = np.concatenate([w_in[:, :3328], w_in[:, 3352:]], 1)
    units = list(column_units(first))
    wb = a["w_branch"][0]
    for n in range(4):
        units += list(wb[n].reshape(MT, P, 2, 512).transpose(2, 1, 0, 3).reshape(2, P, UNIT))
    units += list(column_units(a["w_out"][0]))
    gate = np.concatenate(list(a["moe_w_gate"][0]), 1)
    up = np.concatenate(list(a["moe_w_up"][0]), 1)
    down = a["moe_w_down"][0].reshape(-1, D)
    units += gated_units(gate, up, down)
    fg, fu, fd = a["ffn_w_gate_2"], a["ffn_w_up_2"], a["ffn_w_down_2"]
    units += gated_units(fg[0, 0], fu[0, 0], fd[0, 0])
    ab = column_units(a["a_w_in_2"][0])
    units += [ab[n] for n in AB_ORDER]
    units += list(column_units(a["ab_w_out_2"][0]))
    units += gated_units(fg[0, 1], fu[0, 1], fd[0, 1])
    units += gated_units(fg[1, 0], fu[1, 0], fd[1, 0])
    units += list(column_units(a["c_w_in_2"][0][:, :4096]))
    units += list(column_units(a["c_w_out_2"][0]))
    units += gated_units(fg[1, 1], fu[1, 1], fd[1, 1])
    pe = a["cmp_pe"][0].transpose(0, 2, 1)
    rows = lambda w: w.reshape(KD, P, -1).transpose(1, 0, 2)
    every = lambda v: np.broadcast_to(v.reshape(1, -1), (P, v.size))
    small_1 = pack(SMALL_1, {
        "n1": cols(a["norm1_g"][0]), "n2": cols(a["norm2_g"][0]), "nf": cols(a["final_norm_g"]),
        "gm_g": cols(a["gm_norm_g"][0]), "conv_w": cols(a["conv_w"][0].reshape(-1)), "conv_b": cols(a["conv_b"][0]),
        "ba": cols(a["lru_ba"][0]), "bx": cols(a["lru_bx"][0]), "lam": cols(a["lru_lambda"][0]),
        "pool_s": cols(a["pool_scale"][0]), "pe": np.concatenate([pe, pe], 1).transpose(1, 0, 2),
        "gm_wT": a["gm_ws"][0].transpose(2, 0, 1), "wa": block_diagonal(a["lru_wa"][0]),
        "wx": block_diagonal(a["lru_wx"][0]), "pool_w": a["pool_w"][0].transpose(1, 0, 2),
        "cw2": a["cmp_w2"][0].transpose(1, 2, 0, 3).reshape(P, 128), "w_gate": rows(w_in[:, 3328:3352]),
        "w_route": rows(np.concatenate([a["router_w_group"][0], a["router_w_expert"][0]], 1)),
        "gm_b": every(a["gm_b"][0]),
        "b_route": every(np.concatenate([a["router_b_group"][0], a["router_b_expert"][0]]))})
    cmp_w1 = a["cmp_w1"][0].reshape(2, 2, 32, HD, HD).transpose(1, 3, 0, 2, 4).reshape(P, 2 * 32 * HD)
    two = lambda v: np.concatenate([v, v]).reshape(P, 1)
    small_2 = pack(SMALL_2, {
        "n": cols(a["norm_gains_2"].reshape(-1)), "mu": cols(a["a_shift_mu_2"][0]),
        "d_base": cols(a["a_decay_base_2"][0]), "i_base": cols(a["a_iclr_base_2"][0]),
        "k_k": cols(a["a_k_k_2"][0]), "k_a": cols(a["a_k_a_2"][0]), "r_k": cols(a["a_r_k_2"][0].reshape(-1)),
        "lnx_g": cols(a["a_lnx_g_2"][0]), "lnx_b": cols(a["a_lnx_b_2"][0]),
        "conv_w": cols(a["b_conv_w_2"][0].reshape(-1)), "conv_b": cols(a["b_conv_b_2"][0]),
        "ln_g": cols(a["b_ln_g_2"][0]), "ln_b": cols(a["b_ln_b_2"][0]), "qg": two(a["c_q_norm_g_2"][0]),
        "kg": two(a["c_k_norm_g_2"][0]), "fb": a["c_forget_bias_2"][0].reshape(N_FOX, 1),
        "lora": np.concatenate([a["a_decay_up_2"][0], a["a_iclr_up_2"][0]], 0), "gate_up": a["a_gate_up_2"][0],
        "w_f": rows(a["c_w_in_2"][0][:, 4096:])})
    return {"x_t": np.ascontiguousarray(a["x"][0].T), "stream": np.stack(units), "small_1": small_1,
            "cmp_w1": np.ascontiguousarray(cmp_w1), "small_2": small_2, "consts": constants()}


def build(nc, x_t, stream, small_1, cmp_w1, small_2, consts, out):
    n_units = stream.shape[0]
    assert n_units % RING == 0
    with ExitStack() as ctx:
        def sb(name, shape, dt=FP32):
            return ctx.enter_context(nc.sbuf_tensor(name, shape, dt))

        sems = {}

        def S(name):
            if name not in sems:
                sems[name] = ctx.enter_context(nc.semaphore("s_" + name))
            return sems[name]

        ring = sb("ring", [P, RING, UNIT])
        con = sb("con", [P, W_C])
        sm1 = sb("sm1", [P, W_1])
        sm2 = sb("sm2", [P, W_2])
        X = sb("X", [P, KD, T])
        H = sb("H", [P, KD, T])
        SQ = sb("SQ", [P, KD, T])
        rstd = sb("rstd", [P, T])
        zeros = sb("zeros", [P, 512], BF16)
        tiny = sb("tiny", [P, 256])
        arena = sb("arena", [P, ARENA])
        bank = [ctx.enter_context(nc.psum_tensor(f"bank{n}", [P, 512], FP32)) for n in range(8)]

        def C(name, *dims):
            a, w = OFF_C[name]
            return con[:, a:a + w]

        def P1(name):
            a, w = OFF_1[name]
            return sm1[:, a:a + w]

        def P2(name):
            a, w = OFF_2[name]
            return sm2[:, a:a + w]

        def tiles(ap, n):
            return ap.rearrange("p (m t) -> p m t", m=n)

        class Carve:

            def __init__(self, at=0):
                self.at = at

            def __call__(self, width):
                a = self.at
                self.at += width
                assert self.at <= ARENA, self.at
                return arena[:, a:a + width]

        cut = Carve()
        u = tiles(cut(MT * T), MT)
        gate = tiles(cut(MT * T), MT)
        yc = tiles(cut(MT * T), MT)
        yd = tiles(cut(MT * T), MT)
        mg = tiles(cut(4 * KD * T), 4 * KD)
        after_mg = cut.at
        q1 = tiles(cut(MT * T), MT)
        xd = tiles(cut(MT * (16 + T)), MT)
        rec = tiles(cut(MT * 260), MT)
        kvc = tiles(cut(2 * T), 2)
        kd = tiles(cut(4 * T), 4)
        vn = tiles(cut(2 * TT * P), 2)
        v1 = tiles(cut(TT * MIX), TT)
        cw1_flat = cut(2 * 32 * HD)
        cw1 = cw1_flat.rearrange("p (c l e) -> p c l e", c=2, l=32)
        xc, th_r, th_i, e_b = (tiles(cw1_flat[:, n * 1024:(n + 1) * 1024], MT) for n in range(4))
        att_sp = cut(4 * 384)
        att_s, att_p = tiles(att_sp[:, 0:768], 2), tiles(att_sp[:, 768:1536], 2)
        att_t = tiles(cut(2 * 384), 2)
        p_cmp = cut(2 * P)
        kpe = att_sp[:, 0:2 * 32 * 16].rearrange("p (c l n) -> p c l n", c=2, l=32)
        late = arena[:, after_mg - 16 * T:after_mg]
        win_a, win_b = (tiles(late[:, n * MT * (16 + T):(n + 1) * MT * (16 + T)], MT) for n in range(2))
        hid_c = cut(2 * 16).rearrange("p (c n) -> p c n", c=2)
        k_c = cut(2 * 16).rearrange("p (g n) -> p g n", g=2)
        v_c = cut(2 * HD)
        gates3 = tiles(cut(TT * 24), TT)
        v_junk = SQ[:, 4:8, :].rearrange("p k t -> p (k t)")
        first_cols = tiles(cut(4 * 16), 4)
        junk = cut(T)
        comb_all = mg[:, 0:N_EXP, :]
        cut = Carve(after_mg)
        sil = [tiles(cut(2 * T), 2) for _ in range(2)]
        hid = [tiles(cut(2 * T), 2) for _ in range(2)]
        route = cut(512)
        route_pick = tiles(route[:, 112:144], 2)
        gsum, rt_w2 = route[:, 56:64], route[:, 286:288]

        cut = Carve()
        kkt, qt, kh, bh = (tiles(cut(MT * T), MT) for _ in range(4))
        bon, gup = (tiles(cut(MT * T), MT) for _ in range(2))
        glu = tiles(cut(MT * 288), MT)
        cacc, ctmp = (tiles(cut(MT * T), MT) for _ in range(2))
        phase = cut.at
        pr = tiles(cut(14 * 260), 14)
        pp = tiles(cut(14 * T), 14)
        cv, cg = (tiles(cut(MT * T), MT) for _ in range(2))
        lw, cum_l, rate, e_l, e_p, e_n, kk = (tiles(cut(MT * T), MT) for _ in range(7))
        cut = Carve(phase)
        N_MAT = 2 * N_RW
        gram = cut(N_MAT * 4 * P).rearrange("p (i a t) -> p i a t", i=N_MAT, a=4)
        mat_w_at = cut.at + N_MAT * P
        mat_y, mat_w, mat_m = (tiles(cut(N_MAT * P), N_MAT) for _ in range(3))
        mat_q = tiles(cut(2 * 4 * P), 2)
        rw_r, rw_u = mat_q[:, 0, :], mat_q[:, 1, :]
        rw_y = tiles(cut(TT * MIX), TT)
        sq_flat = SQ[:, :, :].rearrange("p k t -> p (k t)")
        v_tok = tiles(sq_flat[:, 0:2 * MIX], TT)
        kh_tok, bh_tok = sq_flat[:, 2 * MIX:3 * MIX], sq_flat[:, 3 * MIX:4 * MIX]
        state = tiles(cut(MIX), MT)
        cut = Carve()
        fq = tiles(cut(2 * KD * T), 2 * KD)
        f_sq, f_rs = (tiles(cut(2 * 2 * T), 2) for _ in range(2))
        f_v = tiles(cut(TT * D), TT)
        f_gate = tiles(cut(KD * T), KD)
        f_cum = tiles(cut(N_FOX * T), N_FOX)
        f_mc = tiles(cut(2 * 384), 2)
        fat_s, fat_p, fat_t = (tiles(cut(2 * 384), 2) for _ in range(3))
        f_o = tiles(cut(KD * T), KD)
        fz, fa, fe, fl, fc, fm = (cut(T) for _ in range(6))

        def small(at, width):
            return tiny[:, at:at + width]
        v_ss, v_rstd = small(0, 2), small(4, 2)
        neg_max, row_sum, inv_sum = small(8, 4), small(12, 4), small(16, 4)
        hb_a, hb_x, lam_t, lam_z, lam_l, lam_c = (small(20 + 4 * n, 4) for n in range(6))
        lam_d, lam_e = small(44, 4), small(48, 4)
        hd_base, hi_base, e_last = small(52, 4), small(56, 4), small(60, 4)
        gn_sum, gn_rs = small(64, 16), small(80, 16)
        e_mean = arena[:, mat_w_at:mat_w_at + T]
        half_gain, qg8 = small(96, KD), small(104, 1)

        GROUPS = (["u0", "u1", "v0", "v1", "ga0", "ga1", "re0", "re1", "q0", "q1", "kvc", "ks", "vs", "kw", "vw",
                   "g24", "xd0", "xd1"] + [f"mg{n}" for n in range(16)])
        GI = {name: n for n, name in enumerate(GROUPS)}
        PARTS = ["ks", "kw", "g24"]
        FULL, unit = {}, 0
        for name in GROUPS:
            if name in PARTS:
                FULL[name] = ("part_full", PARTS.index(name) + 1)
            else:
                unit += 1
                FULL[name] = ("unit_used", unit)
        assert unit == PROJ_1
        for kind, order in (("ab", AB_ORDER), ("c", range(PROJ_C))):
            for place, n in enumerate(order):
                GI[f"{kind}{n}"] = len(GI)
                FULL[f"{kind}{n}"] = (kind, place + 1)
        SIDES = ["norm0", "gm0", "gm1", "hid", "kvc2", "wa0", "wa1", "wx0", "wx1", "po0", "po1",
                 "norm1", "route"] + [f"comb{n}" for n in range(8)] + ["norm2"] + SIDES_2
        SI = {name: n for n, name in enumerate(SIDES)}
        N_SLOTS = N_HEADS * N_TYPES
        D_UNITS = {"branch": PROJ_1, "w_out": PROJ_1 + BRANCH, "moe": PROJ_1 + BRANCH + SQUARE}
        at = D_UNITS["moe"] + 3 * MOE_STEPS
        for name, size in (("ffn0", 3 * FFN_STEPS), ("ab", PROJ_AB), ("ab_out", SQUARE), ("ffn1", 3 * FFN_STEPS),
                           ("ffn2", 3 * FFN_STEPS), ("c", PROJ_C), ("c_out", SQUARE), ("ffn3", 3 * FFN_STEPS)):
            D_UNITS[name] = at
            at += size
        assert at == n_units
        for name in GI:
            if FULL[name][0] in ("ab", "c"):
                FULL[name] = ("unit_used", D_UNITS[FULL[name][0]] + FULL[name][1])
        STEP0 = {"moe": 0}
        for n in range(4):
            STEP0[f"ffn{n}"] = MOE_STEPS + n * FFN_STEPS
        SQ0 = {"w_out": 0, "ab_out": SQUARE, "c_out": 2 * SQUARE}

        def fox_schedule(run_slot, run_gate):
            for n in range(N_FOX + 2):
                if n < 4:
                    run_gate(n)
                run_slot(n)

        def up_count(name, s):
            return s * 3 + (D_UNITS[name] + 1)

        def down_count(name, s):
            return s * 3 + (D_UNITS[name] + 5)

        def schedule(run_slot, run_mg):
            for j in range(16):
                run_mg(j)
                if j >= 3:
                    for n in (2 * (j - 3), 2 * (j - 3) + 1):
                        run_slot(n)

        block = ctx.enter_context(nc.Block())

        @block.sync
        def _(sp):
            sp.dma_start(X[:, :, :], x_t.rearrange("(k p) t -> p k t", p=P)).then_inc(S("x"), 16)
            def load(s, unit):
                sp.dma_start(ring[:, s, :], unit.rearrange("a p n -> (a p) n")).then_inc(S(f"unit{s}"), 16)
            load(0, stream[0:1, :, :])
            sp.dma_start(con[:, :], consts).then_inc(S("con"), 16)
            sp.dma_start(sm1[:, :], small_1).then_inc(S("sm1"), 16)
            for s in range(1, RING):
                load(s, stream[s:s + 1, :, :])
            sp.dma_start(cw1_flat, cmp_w1).then_inc(S("cw1"), 16)
            sp.dma_start(sm2[:, :], small_2).then_inc(S("sm2"), 16)
            with sp.Fori(0, n_units // RING - 1) as i:
                for s in range(RING):
                    sp.wait_ge(S("unit_used"), i * RING + s + 1)
                    load(s, stream[bass.ds(i * RING + (RING + s), 1), :, :])
            sp.wait_ge(S("out"), 1)
            sp.dma_start(out.rearrange("(k p) t -> p k t", p=P), X[:, :, :]).then_inc(S("stored"), 16)
            sp.wait_ge(S("stored"), 16)

        @block.gpsimd
        def _(pool):
            chain = [0]

            def link(ins):
                chain[0] += 1
                ins.then_inc(S("pool_chain"), 1)
                pool.wait_ge(S("pool_chain"), chain[0])
            for part in (zeros[:, :], p_cmp, v_c, xd[:, :, 0:16], win_a[:, :, :], win_b[:, :, :]):
                link(pool.memset(part, 0.0))
            pool.memset(rec[:, :, 0:3], 0.0).then_inc(S("zeroed"), 1)
            pool.wait_ge(S("zeroed"), 1)
            pool.wait_ge(S("con"), 16)
            pool.wait_ge(S("proj_free"), GI["xd1"] + 1)
            link(pool.tensor_tensor(win_a[:, :, 1:16 + T], xd[:, :, 1:16 + T], xd[:, :, 0:15 + T], ALU.add))
            src, dst = win_a, win_b
            for m, w in enumerate(WINDOWS):
                if m < MT - 1:
                    link(pool.tensor_tensor(dst[:, m + 1:, w:16 + T], src[:, m + 1:, w:16 + T],
                                            src[:, m + 1:, 0:16 + T - w], ALU.add))
                first = C("pool_n").rearrange("p (m t) -> p m t", m=4)[:, m, :]
                link(pool.tensor_tensor(first_cols[:, m, :], src[:, m, 16:32], first, ALU.mult))
                link(pool.tensor_scalar(src[:, m, 16:16 + T], src[:, m, 16:16 + T], 1.0 / w, None, ALU.mult))
                link(pool.tensor_copy(src[:, m, 16:32], first_cols[:, m, :]))
                pool.tensor_tensor(xd[:, m, 16:16 + T], src[:, m, 16:16 + T], xd[:, m, 16:16 + T], ALU.subtract)\
                    .then_inc(S("pooled"), 1)
                src, dst = dst, src

            pool.wait_ge(S("added"), 1)
            link(pool.memset(pr[:, :, 0:1], 0.0))
            pool.memset(glu[:, :, 0:CONV_B - 1], 0.0).then_inc(S("zeroed_2"), 1)
            pool.wait_ge(S("sm2"), 16)
            pool.wait_ge(S("glu"), MT)
            for k in range(CONV_B):
                dst = ctmp if k else cacc
                for m in range(MT):
                    w = P2("conv_w")[:, MT * k + m:MT * k + m + 1]
                    ins = pool.tensor_scalar(dst[:, m, :], glu[:, m, k:k + T], w, None, ALU.mult)
                link(ins)
                if k:
                    ins = pool.tensor_tensor(cacc[:, :, :], cacc[:, :, :], ctmp[:, :, :], ALU.add)
                    if k < CONV_B - 1:
                        link(ins)
            ins.then_inc(S("conv_2"), 1)
            for h in range(N_FOX):
                b = h % 2
                pool.wait_ge(S("side_free"), SI[f"cb{h // 2}"] + 1)
                if h >= 2:
                    pool.wait_ge(S("fsc_free"), h - 1)
                m = C("mask3")
                pool.tensor_tensor(f_mc[:, b, 0:P], m[:, 0:P], f_cum[:, h, 0:P], ALU.add)
                pool.tensor_tensor(f_mc[:, b, P:3 * P], m[:, P:3 * P], f_cum[:, h, :], ALU.add)\
                    .then_inc(S("mc"), 1)

        @block.scalar
        def _(act):
            chain = [0]

            def link(ins):
                chain[0] += 1
                ins.then_inc(S("act_chain"), 1)
                act.wait_ge(S("act_chain"), chain[0])

            def squares(n):
                act.activation(SQ[:, :, :], X[:, :, :], ACT.Square).then_inc(S("squares"), 1)

            def evac(name, dst, func, scale=1.0):
                n = GI[name]
                act.wait_ge(S(FULL[name][0]), FULL[name][1])
                src = bank[5 + n % 2][:, 0:dst.free_size()]
                if len(dst.shape) == 3:
                    src = tiles(src, dst.shape[1])
                act.activation(dst, src, func, scale=scale).then_inc(S("proj_free"), 1)

            def root_mean(name, scale=1.0 / D, eps=0, width=T):
                act.wait_ge(S("side_full"), SI[name] + 1)
                act.activation(rstd[:, 0:width], bank[7][:, 0:width], ACT.Sqrt, bias=C("eps")[:, eps:eps + 1], scale=scale)\
                   .then_inc(S("side_free"), 1)

            act.wait_ge(S("x"), 16)
            squares(0)
            act.wait_ge(S("con"), 16)
            root_mean("norm0")
            gelu = ACT.Gelu_apprx_tanh
            for n in range(2):
                evac(f"u{n}", u[:, 2 * n:2 * n + 2, :], gelu)
            for n in range(2):
                evac(f"v{n}", v1[:, :, n * UC:(n + 1) * UC], gelu)
            for n in range(2):
                evac(f"ga{n}", gate[:, 2 * n:2 * n + 2, :], gelu)
            act.wait_ge(S("zeroed"), 1)
            for n in range(2):
                evac(f"re{n}", rec[:, 2 * n:2 * n + 2, 3:3 + T], ACT.Copy)
            for n in range(2):
                evac(f"q{n}", q1[:, 2 * n:2 * n + 2, :], ACT.Copy)
            evac("kvc", kvc[:, :, :], ACT.Copy)
            for n, (k, v) in enumerate((("ks", "vs"), ("kw", "vw"))):
                evac(k, kd[:, 2 * n:2 * n + 2, :], ACT.Copy)
                evac(v, vn[:, n, :].rearrange("p (t d) -> p t d", t=TT), ACT.Copy)
            evac("g24", gates3[:, :, :], ACT.Tanh, scale=0.5)
            for n in range(2):
                evac(f"xd{n}", xd[:, 2 * n:2 * n + 2, 16:16 + T], ACT.Copy)
            act.wait_ge(S("proj_free"), GI["v1"] + 1)
            for t in range(TT):
                link(act.activation(tiles(v_junk, 2)[:, t, :], v1[:, t, :], ACT.Square, accum_out=v_ss[:, t:t + 1]))
            act.wait_ge(S("con"), 16)
            act.activation(v_rstd, v_ss, ACT.Sqrt, bias=C("eps")[:, 0:1], scale=1.0 / MIX).then_inc(S("v_sums"), 1)

            def exp(n):
                act.wait_ge(S("max_ok"), n + 1)
                b = n % 2
                if n >= 2:
                    act.wait_ge(S("pt_full"), n - 1)
                for t in range(TT):
                    if n % 3 == 0:
                        dst, src = p_cmp[:, t * P:t * P + N_CMP], att_s[:, b, t * 16:t * 16 + N_CMP]
                    else:
                        a, z = (0, P) if t == 0 else (P, 3 * P)
                        dst, src = att_p[:, b, a:z], att_s[:, b, a:z]
                    act.activation(dst, src, ACT.Exp, bias=neg_max[:, 2 * b + t:2 * b + t + 1],
                                   accum_out=row_sum[:, 2 * b + t:2 * b + t + 1]).then_inc(S("exp_done"), 1)

            def weights_out(n):
                act.wait_ge(S("pt_full"), n + 1)
                if n >= 2:
                    act.wait_ge(S("pv_done"), n - 1)
                w = 2 * P if n % 3 == 0 else 3 * P
                act.activation(att_t[:, n % 2, 0:w], bank[2 + n % 2][:, 0:w], ACT.Copy).then_inc(S("pt_free"), 1)

            def run_mg(j):
                if j == 8:
                    act.wait_ge(S("pooled"), MT)
                evac(f"mg{j}", mg[:, 2 * j:2 * j + 2, :], ACT.Tanh, scale=0.5)
                if j == 1:
                    act.wait_ge(S("side_full"), SI["hid"] + 1)
                    act.activation(hid_c[:, :, 0:N_CMP], tiles(bank[7][:, 0:32], 2)[:, :, 0:N_CMP], gelu).then_inc(S("side_free"), 1)
                if j == 2:
                    act.wait_ge(S("lam_abs"), 1)
                    act.activation(lam_z, lam_t, ACT.Exp, scale=-1.0).then_inc(S("lam_z"), 1)
                    act.wait_ge(S("lam_u"), 1)
                    act.activation(lam_l, lam_t, ACT.Ln).then_inc(S("lam_l"), 1)
                if j in (7, 8, 9, 10):
                    name, dst, bias = (("wa0", th_r, hb_a), ("wa1", th_r, hb_a), ("wx0", th_i, hb_x),
                                       ("wx1", th_i, hb_x))[j - 7]
                    act.wait_ge(S("side_full"), SI[name] + 1)
                    for t in range(2):
                        m = 2 * (j % 2 == 0) + t
                        ins = act.activation(dst[:, m, :], bank[7][:, t * T:(t + 1) * T], ACT.Tanh,
                                             bias=bias[:, m:m + 1], scale=0.5)
                    ins.then_inc(S("side_free"), 1)
                if j in (11, 12):
                    name = f"po{j - 11}"
                    act.wait_ge(S("side_full"), SI[name] + 1)
                    for t in range(2):
                        m = 2 * (j - 11) + t
                        ins = act.activation(yd[:, m, :], bank[7][:, t * T:(t + 1) * T], ACT.Copy,
                                             scale=P1("pool_s")[:, m:m + 1])
                    ins.then_inc(S("side_free"), 1)
                if j == 13:
                    act.wait_ge(S("log_a"), 1)
                    act.activation(th_i[:, :, :], th_r[:, :, :], ACT.Tanh).then_inc(S("tanh_l"), 1)
                    act.activation(th_r[:, :, :], th_r[:, :, :], ACT.Exp).then_inc(S("decay"), 1)
                if j == 15:
                    act.wait_ge(S("e_ok"), 1)
                    act.activation(e_b[:, :, :], e_b[:, :, :], ACT.Sqrt).then_inc(S("e_root"), 1)

            def run_slot(n):
                if n < N_SLOTS:
                    exp(n)
                if 1 <= n <= N_SLOTS:
                    weights_out(n - 1)

            schedule(run_slot, run_mg)

            act.wait_ge(S("res_done"), SQ0["w_out"] + SQUARE)
            squares(1)
            root_mean("norm1")

            act.wait_ge(S("rt_1"), 1)
            act.activation(gsum, gsum, ACT.Exp).then_inc(S("rt_e"), 1)
            act.wait_ge(S("rt_2"), 1)
            act.activation(rt_w2, rt_w2, ACT.Exp).then_inc(S("rt_e"), 1)

            def silu_steps(name, steps):
                def step(parity, count):
                    act.wait_ge(S("unit_used"), count)
                    act.activation(sil[parity], tiles(bank[4 + 2 * parity][:, :], 2), ACT.Silu)\
                       .then_inc(S("silu_done"), 1)
                step(0, D_UNITS[name] + 2)
                with act.Fori(0, (steps - 1) // 2) as i:
                    step(1, up_count(name, i * 2 + 1))
                    step(0, up_count(name, i * 2 + 2))
                if steps % 2 == 0:
                    step(1, up_count(name, steps - 1))

            silu_steps("moe", MOE_STEPS)
            act.wait_ge(S("out_1"), 1)
            squares(2)
            root_mean("norm2")

            def pre_norm(n):
                if n > 3:
                    act.wait_ge(S("added"), (n - 3) // 2)
                else:
                    act.wait_ge(S("normed"), 3 * KD)
                squares(n)
                root_mean(f"n{n}")

            def post_norm(n, full):
                for b in range(4):
                    act.wait_ge(S("unit_used"), full[b])
                    ins = act.activation(SQ[:, 2 * b:2 * b + 2, :], tiles(bank[b][:, :], 2), ACT.Square)
                ins.then_inc(S("squares"), 1)
                root_mean(f"n{n}")

            def ffn(n, first):
                pre_norm(first)
                silu_steps(f"ffn{n}", FFN_STEPS)
                post_norm(first + 1, [D_UNITS[f"ffn{n}"] + 3 * FFN_STEPS] * 4)

            def squares_out(name):
                return [D_UNITS[name] + b + 1 for b in range(4)]

            ffn(0, 3)
            pre_norm(5)
            act.wait_ge(S("zeroed_2"), 1)
            evac("ab6", pr[:, 12:14, 1:1 + T], ACT.Copy)
            act.wait_ge(S("shifted"), 1)
            act.activation(pp[0:HD, 12, :], pp[0:HD, 12, :], ACT.Tanh).then_inc(S("lora_in"), 1)
            act.activation(pp[:, 13, :], pp[:, 13, :], ACT.Tanh, scale=0.5).then_inc(S("lora_in"), 1)
            for n in range(2):
                evac(f"ab{n}", pr[:, 2 * n:2 * n + 2, 1:1 + T], ACT.Copy)
            act.wait_ge(S("half_bias"), 1)
            act.wait_ge(S("lora_full"), 1)
            for m in range(MT):
                act.activation(lw[:, m, :], bank[m // 2][:, (m % 2) * T:(m % 2 + 1) * T], ACT.Tanh,
                               bias=hd_base[:, m:m + 1], scale=0.5).then_inc(S("lora_out"), 1)
            for m in range(MT):
                act.activation(rate[:, m, :], bank[2 + m // 2][:, (m % 2) * T:(m % 2 + 1) * T], ACT.Tanh,
                               bias=hi_base[:, m:m + 1], scale=0.5).then_inc(S("lora_out"), 1)
            for n in range(2, 6):
                evac(f"ab{n}", pr[:, 2 * n:2 * n + 2, 1:1 + T], ACT.Copy)
            for n in range(2):
                act.wait_ge(S("side_full"), SI[f"gu{n}"] + 1)
                act.activation(gup[:, 2 * n:2 * n + 2, :], tiles(bank[7][:, :], 2), ACT.Copy).then_inc(S("side_free"), 1)
            for n in range(2):
                evac(f"ab{9 + n}", cg[:, 2 * n:2 * n + 2, :], ACT.Tanh, scale=0.5)
            act.wait_ge(S("kk_max"), 1)
            act.activation(e_l[:, :, :], e_l[:, :, :], ACT.Sqrt).then_inc(S("kk_root"), 1)
            act.wait_ge(S("logs"), 1)
            act.activation(e_p[:, :, :], e_p[:, :, :], ACT.Exp).then_inc(S("exps"), 1)
            act.activation(e_n[:, :, :], cum_l[:, :, :], ACT.Exp, scale=-1.0).then_inc(S("exps"), 1)
            act.wait_ge(S("kk_used"), 1)
            act.activation(e_l[:, :, :], cum_l[:, :, :], ACT.Exp).then_inc(S("exps"), 1)
            for n in range(2):
                evac(f"ab{7 + n}", cv[:, 2 * n:2 * n + 2, :], ACT.Copy)
            act.wait_ge(S("turned"), 1)
            for c in range(TT):
                act.activation(v_tok[:, c, :], bank[c][:, :], ACT.Copy)
            act.activation(kh_tok, bank[2][:, :], ACT.Copy)
            act.activation(bh_tok, bank[3][:, :], ACT.Copy, scale=-1.0).then_inc(S("tok_ok"), 1)
            for g in range(4):
                act.wait_ge(S("y_full"), g + 1)
                act.activation(mat_y[:, 4 * g:4 * g + 4, :], tiles(bank[5 + g % 2][:, :], 4), ACT.Copy)\
                   .then_inc(S("y_free"), 1)
            for c in range(TT):
                act.wait_ge(S("rw_full"), 3 * c + 1)
                act.activation(rw_r, bank[4 * c][:, :], ACT.Copy).then_inc(S("rw_r"), 1)
                act.wait_ge(S("rw_full"), 3 * c + 2)
                act.activation(rw_u, bank[4 * c + 1][:, :], ACT.Copy).then_inc(S("rw_u"), 1)
            act.wait_ge(S("gn_var"), 1)
            act.activation(gn_rs, gn_sum, ACT.Sqrt, bias=C("eps")[:, 1:2], scale=1.0 / HD).then_inc(S("gn_root"), 1)
            act.wait_ge(S("y_turned"), 1)
            for m in range(MT):
                act.activation(H[:, m, :], bank[m // 2][:, (m % 2) * T:(m % 2 + 1) * T], ACT.Identity,
                               bias=P2("lnx_b")[:, m:m + 1], scale=P2("lnx_g")[:, m:m + 1]).then_inc(S("gn_out"), 1)
            act.wait_ge(S("side_full"), SI["ln1"] + 1)
            act.activation(e_mean, bank[7][:, 0:T], ACT.Copy, scale=1.0 / MIX).then_inc(S("side_free"), 1)
            act.wait_ge(S("ln_centered"), 1)
            act.activation(ctmp[:, :, :], cacc[:, :, :], ACT.Square).then_inc(S("ln_sq"), 1)
            root_mean("ln2", scale=1.0 / MIX, eps=2)
            act.wait_ge(S("ln_scaled"), 1)
            for m in range(MT):
                act.activation(H[:, MT + m, :], cacc[:, m, :], ACT.Silu, bias=P2("ln_b")[:, m:m + 1],
                               scale=P2("ln_g")[:, m:m + 1]).then_inc(S("y_conv"), 1)
            post_norm(6, squares_out("ab_out"))
            ffn(1, 7)
            ffn(2, 9)
            pre_norm(11)

            def head_norm(n):
                act.wait_ge(S("side_full"), SI[f"hs{n}"] + 1)
                if n >= 2:
                    act.wait_ge(S("hn_done"), n - 1)
                act.activation(f_rs[:, n % 2, :], bank[7][:, :], ACT.Sqrt, bias=C("eps")[:, 0:1], scale=1.0 / HD)\
                   .then_inc(S("side_free"), 1)

            for n in range(8):
                act.wait_ge(S(FULL[f"c{n}"][0]), FULL[f"c{n}"][1])
                if n >= 2:
                    act.wait_ge(S("side_full"), SI[f"hs{n - 2}"] + 1)
                act.activation(f_sq[:, n % 2, :], bank[5 + GI[f"c{n}"] % 2][:, :], ACT.Square).then_inc(S("f_sq"), 1)
                evac(f"c{n}", fq[:, 2 * n:2 * n + 2, :], ACT.Copy)
                if n:
                    head_norm(n - 1)
            head_norm(7)
            for n in range(4):
                evac(f"c{8 + n}", f_v[:, :, n * UC:(n + 1) * UC], ACT.Copy)
            act.wait_ge(S("f_abs"), 1)
            act.activation(fe[0:N_FOX, :], fa[0:N_FOX, :], ACT.Exp, scale=-1.0).then_inc(S("f_exp"), 1)
            act.wait_ge(S("f_one"), 1)
            act.activation(fl[0:N_FOX, :], fa[0:N_FOX, :], ACT.Ln).then_inc(S("f_log"), 1)
            for n in range(8):
                act.wait_ge(S("side_full"), SI[f"cb{n}"] + 1)
                act.activation(f_cum[:, 2 * n:2 * n + 2, :], tiles(bank[7][:, :], 2), ACT.Copy).then_inc(S("side_free"), 1)

            def fox_slot(n):
                if n < N_FOX:
                    b = n % 2
                    act.wait_ge(S("fmax_ok"), n + 1)
                    if n >= 2:
                        act.wait_ge(S("fpt_full"), n - 1)
                    for t, (a, z) in enumerate(((0, P), (P, 3 * P))):
                        act.activation(fat_p[:, b, a:z], fat_s[:, b, a:z], ACT.Exp,
                                       bias=neg_max[:, 2 * b + t:2 * b + t + 1],
                                       accum_out=row_sum[:, 2 * b + t:2 * b + t + 1]).then_inc(S("fexp_done"), 1)
                if 1 <= n <= N_FOX:
                    act.wait_ge(S("fpt_full"), n)
                    if n >= 3:
                        act.wait_ge(S("fpv_done"), n - 2)
                    act.activation(fat_t[:, (n - 1) % 2, :], bank[2 + (n - 1) % 2][:, 0:384], ACT.Copy)\
                       .then_inc(S("fpt_free"), 1)

            fox_schedule(fox_slot, lambda j: evac(f"c{12 + j}", f_gate[:, 2 * j:2 * j + 2, :], ACT.Tanh, scale=0.5))
            post_norm(12, squares_out("c_out"))
            ffn(3, 13)

        @block.vector
        def _(dve):
            chain = [0]

            def link(ins):
                chain[0] += 1
                ins.then_inc(S("dve_chain"), 1)
                dve.wait_ge(S("dve_chain"), chain[0])

            def norm(n, side, gain, dst):
                dve.wait_ge(S("side_free"), SI[side] + 1)
                link(dve.reciprocal(rstd[:, :], rstd[:, :]))
                for k in range(KD):
                    dve.scalar_tensor_tensor(dst[:, k, :], X[:, k, :], gain[:, k:k + 1], rstd[:, :], ALU.mult,
                                             ALU.mult).then_inc(S("normed"), 1)

            dve.memset(small(110, 1), 0.0).then_inc(S("hid_done"), 1)
            dve.wait_ge(S("con"), 16)
            dve.wait_ge(S("sm1"), 16)
            dve.wait_ge(S("x"), 16)
            norm(0, "norm0", P1("n1"), H)
            gm_w = tiles(P1("gm_wT"), 4)
            link(dve.tensor_tensor(gm_w, gm_w, C("s_le_t").unsqueeze(1).to_broadcast([P, 4, P]), ALU.mult))
            link(dve.tensor_scalar(hb_a, P1("ba"), 0.5, None, ALU.mult))
            link(dve.tensor_scalar(hb_x, P1("bx"), 0.5, None, ALU.mult))
            link(dve.tensor_scalar(lam_d, P1("lam"), -1.0, None, ALU.mult))
            dve.tensor_tensor(lam_t, lam_d, P1("lam"), ALU.max).then_inc(S("lam_abs"), 1)
            dve.wait_ge(S("proj_free"), GI["kvc"] + 1)
            for c in range(2):
                by16 = kvc[:, c, :].rearrange("p (n l) -> p l n", l=16)
                for half in range(2):
                    pe_c = P1("pe")[:, c * 32 + half * 16:c * 32 + half * 16 + 16]
                    ins = dve.tensor_tensor(kpe[:, c, half * 16:half * 16 + 16, 0:N_CMP],
                                            by16[:, :, half:half + N_CMP],
                                            pe_c.unsqueeze(2).to_broadcast([P, 16, N_CMP]), ALU.add)
            ins.then_inc(S("kpe"), 1)
            dve.wait_ge(S("v_sums"), 1)
            link(dve.reciprocal(v_rstd, v_rstd))
            for t in range(TT):
                dve.tensor_scalar(v1[:, t, :], v1[:, t, :], v_rstd[:, t:t + 1], None, ALU.mult)\
                   .then_inc(S("v_normed"), 1)
            dve.wait_ge(S("proj_free"), GI["g24"] + 1)
            link(dve.tensor_scalar(gates3[:, :, :], gates3[:, :, :], 0.5, 0.5, ALU.mult, ALU.add))

            def gmlp(pair):
                dve.wait_ge(S("side_full"), SI[f"gm{pair}"] + 1)
                for t in range(2):
                    g = 2 * pair + t
                    bias = P1("gm_b")[:, g * P:(g + 1) * P].unsqueeze(1).to_broadcast([P, 2, P])
                    link(dve.scalar_tensor_tensor(tiles(SQ[:, 2 + t, :], 2), tiles(bank[7][:, t * T:(t + 1) * T], 2),
                                                  P1("gm_g")[:, g:g + 1], bias, ALU.mult, ALU.add))
                    ins = dve.tensor_tensor(u[:, g, :], u[:, g, :], SQ[:, 2 + t, :], ALU.mult)
                    if t == 0:
                        link(ins)
                ins.then_inc(S("side_free"), 1)

            def compressed():
                dve.wait_ge(S("side_full"), SI["kvc2"] + 1)
                dve.wait_ge(S("zeroed"), 1)
                for g, ps in enumerate((bank[7], bank[4])):
                    dve.tensor_copy(k_c[:, g, 0:N_CMP], ps[:, g * 16:g * 16 + N_CMP])
                    ins = dve.tensor_copy(v_c[0:N_CMP, g * HD:(g + 1) * HD], ps[0:N_CMP, P + g * HD:P + (g + 1) * HD])
                ins.then_inc(S("side_free"), 1)

            def soft_1(n):
                b = n % 2
                dve.wait_ge(S("sc_full"), n + 1)
                if n >= 2:
                    dve.wait_ge(S("exp_done"), 2 * (n - 1))
                if n % 3 == 0:
                    s = tiles(att_s[:, b, 0:32], 2)[:, :, 0:N_CMP]
                    ins = dve.scalar_tensor_tensor(s, tiles(bank[b][:, 0:32], 2)[:, :, 0:N_CMP], SCALE,
                                                   tiles(C("cmp_add"), 2)[:, :, 0:N_CMP], ALU.mult, ALU.add)
                    ins.then_inc(S("sc_free"), 1)
                    dve.wait_ge(S("sc_free"), n + 1)
                    link(dve.tensor_reduce(neg_max[:, 2 * b:2 * b + 2], s, AX.X, ALU.max))
                else:
                    dve.scalar_tensor_tensor(att_s[:, b, :], bank[b][:, 0:384], SCALE, C("mask3"), ALU.mult, ALU.add)\
                       .then_inc(S("sc_free"), 1)
                    dve.wait_ge(S("sc_free"), n + 1)
                    dve.tensor_reduce(neg_max[:, 2 * b:2 * b + 1], att_s[:, b, 0:P], AX.X, ALU.max)
                    link(dve.tensor_reduce(neg_max[:, 2 * b + 1:2 * b + 2], att_s[:, b, P:3 * P], AX.X, ALU.max))
                dve.tensor_scalar(neg_max[:, 2 * b:2 * b + 2], neg_max[:, 2 * b:2 * b + 2], -1.0, None, ALU.mult)\
                   .then_inc(S("max_ok"), 1)

            def soft_2(n):
                b, h, kind = n % 2, n // 3, n % 3
                dve.wait_ge(S("exp_done"), 2 * (n + 1))
                inv = inv_sum[:, 2 * b:2 * b + 2]
                link(dve.reciprocal(inv, row_sum[:, 2 * b:2 * b + 2]))
                link(dve.tensor_tensor(inv, inv, gates3[:, :, 3 * h + kind], ALU.mult))
                for t in range(TT):
                    i = inv[:, t:t + 1]
                    if kind == 0:
                        w = p_cmp[:, t * P:t * P + N_CMP]
                        ins = dve.scalar_tensor_tensor(w, w, i, tiles(C("cmp_01"), 2)[:, t, 0:N_CMP], ALU.mult, ALU.mult)
                    else:
                        a, z = (0, P) if t == 0 else (P, 3 * P)
                        ins = dve.tensor_scalar(att_p[:, b, a:z], att_p[:, b, a:z], i, None, ALU.mult)
                ins.then_inc(S("p_ok"), 1)

            def conv(m):
                w = P1("conv_w")
                link(dve.tensor_scalar(xc[:, m, :], rec[:, m, 0:T], w[:, m:m + 1], P1("conv_b")[:, m:m + 1],
                                       ALU.mult, ALU.add))
                for k in range(1, CONV_A):
                    ins = dve.scalar_tensor_tensor(xc[:, m, :], rec[:, m, k:k + T], w[:, MT * k + m:MT * k + m + 1],
                                                   xc[:, m, :], ALU.mult, ALU.add)
                    if k < CONV_A - 1:
                        link(ins)
                ins.then_inc(S("xc"), 1)

            def lam_1():
                dve.wait_ge(S("lam_z"), 1)
                dve.tensor_scalar(lam_t, lam_z, 1.0, None, ALU.add).then_inc(S("lam_u"), 1)

            def lam_2():
                dve.wait_ge(S("lam_l"), 1)
                link(dve.tensor_scalar(lam_d, lam_t, -1.0, None, ALU.add))
                link(dve.tensor_scalar(lam_e, lam_d, 0.0, None, ALU.is_equal))
                link(dve.tensor_tensor(lam_d, lam_d, lam_e, ALU.add))
                link(dve.reciprocal(lam_d, lam_d))
                link(dve.tensor_tensor(lam_c, lam_l, lam_d, ALU.mult))
                link(dve.tensor_tensor(lam_c, lam_c, lam_e, ALU.add))
                link(dve.tensor_tensor(lam_c, lam_c, lam_z, ALU.mult))
                link(dve.tensor_scalar(lam_d, P1("lam"), -1.0, 0.0, ALU.mult, ALU.max))
                link(dve.tensor_tensor(lam_c, lam_c, lam_d, ALU.add))
                link(dve.tensor_scalar(lam_c, lam_c, -4.0, None, ALU.mult))

            def recur_1():
                dve.wait_ge(S("side_free"), SI["wx1"] + 1)
                link(dve.scalar_tensor_tensor(xc[:, :, :], th_i[:, :, :], 1.0, xc[:, :, :], ALU.add, ALU.mult))
                for m in range(MT):
                    ins = dve.tensor_scalar(th_r[:, m, :], th_r[:, m, :], 1.0, lam_c[:, m:m + 1], ALU.add, ALU.mult)
                ins.then_inc(S("log_a"), 1)

            def recur_2():
                dve.wait_ge(S("decay"), 1)
                link(dve.tensor_scalar(e_b[:, :, :], th_i[:, :, :], -1.0, 1.0, ALU.mult, ALU.add))
                link(dve.reciprocal(e_b[:, :, :], e_b[:, :, :]))
                dve.scalar_tensor_tensor(e_b[:, :, :], th_i[:, :, :], -2.0, e_b[:, :, :], ALU.mult, ALU.mult)\
                   .then_inc(S("e_ok"), 1)

            def recur_3():
                dve.wait_ge(S("e_root"), 1)
                link(dve.scalar_tensor_tensor(xc[:, :, :], e_b[:, :, :], 0.5, xc[:, :, :], ALU.mult, ALU.mult))
                for m in range(MT):
                    ins = dve.tensor_tensor_scan(e_b[:, m, :], th_r[:, m, :], xc[:, m, :], 0.0, ALU.mult, ALU.add)
                link(ins)
                dve.tensor_tensor(gate[:, :, :], gate[:, :, :], e_b[:, :, :], ALU.mult).then_inc(S("y_b"), 1)

            def run_mg(j):
                if j < 2:
                    gmlp(j)
                if j == 2:
                    compressed()
                    lam_1()
                if j == 3:
                    lam_2()
                if 3 <= j <= 6:
                    conv(j - 3)
                if j == 12:
                    recur_1()
                if j == 14:
                    recur_2()
                if j == 15:
                    recur_3()

            def run_slot(n):
                if n < N_SLOTS:
                    soft_1(n)
                if 1 <= n <= N_SLOTS:
                    soft_2(n - 1)
                if n >= 2 and (n - 2) % 6 == 5:
                    p = (n - 2) // 6
                    dve.wait_ge(S("pv_done"), 6 * (p + 1))
                    dve.tensor_copy(yc[:, p, :], bank[4][:, (p % 2) * T:(p % 2) * T + T]).then_inc(S("o_free"), 1)

            schedule(run_slot, run_mg)

            for n in range(4):
                for half in range(2):
                    unit = 2 * n + half
                    dve.wait_ge(S("unit_used"), D_UNITS["branch"] + unit + 1)
                    for b in range(2):
                        d0 = 4 * half + 2 * b
                        dst = SQ if n == 0 else H
                        ins = dve.scalar_tensor_tensor(dst[:, d0:d0 + 2, :], mg[:, KD * n + d0:KD * n + d0 + 2, :], 1.0,
                                                       tiles(bank[2 * half + b][:, :], 2), ALU.add, ALU.mult)
                        ins.then_inc(S("br_free"), 1)
                        if n:
                            dve.wait_ge(S("br_free"), 2 * unit + b + 1)
                            link(dve.tensor_tensor(SQ[:, d0:d0 + 2, :], SQ[:, d0:d0 + 2, :], H[:, d0:d0 + 2, :], ALU.add))
            dve.tensor_scalar(H[:, :, :], SQ[:, :, :], 0.5, None, ALU.mult).then_inc(S("merged"), 1)

            def add_square(name, dst, src=None):
                for n in range(SQUARE):
                    dve.wait_ge(S("unit_used"), D_UNITS[name] + n + 1)
                    d = dst[:, 2 * n:2 * n + 2, :]
                    ps = tiles(bank[n][:, :], 2)
                    ins = dve.tensor_tensor(d, ps, src[:, 2 * n:2 * n + 2, :], ALU.add) if src is not None \
                        else dve.tensor_copy(d, ps)
                    ins.then_inc(S("res_done"), 1)

            add_square("w_out", X, X)
            norm(1, "norm1", P1("n2"), H)

            dve.wait_ge(S("side_full"), SI["route"] + 1)
            lg = tiles(route[:, 0:40], 2)
            dve.tensor_tensor(lg, tiles(bank[7][:, 0:40], 2), P1("b_route").unsqueeze(1).to_broadcast([P, 2, 20]),
                              ALU.add).then_inc(S("side_free"), 1)
            dve.wait_ge(S("side_free"), SI["route"] + 1)
            gl, el = lg[:, :, 0:4], lg[:, :, 4:20]
            gmax, ge, gw = route[:, 40:42], route[:, 48:56], route[:, 64:66]
            one_g, pick, in_g, o1, o2, rest = (tiles(route[:, 80 + 32 * n:80 + 32 * n + w], 2) for n, w in
                                               enumerate((8, 32, 8, 8, 8, 8)))
            m1, m2, w1, w2 = route[:, 280:282], route[:, 282:284], route[:, 284:286], rt_w2

            def bc(x, n):
                return x.unsqueeze(2).to_broadcast([P, 2, n])

            def first_of(dst, src, top, tmp):
                link(dve.tensor_tensor(dst, src, bc(top, 4), ALU.is_equal))
                for k in range(1, 4):
                    link(dve.tensor_reduce(tmp, dst[:, :, 0:k], AX.X, ALU.max))
                    link(dve.tensor_scalar(tmp, tmp, -1.0, 1.0, ALU.mult, ALU.add))
                    link(dve.tensor_tensor(dst[:, :, k], dst[:, :, k], tmp, ALU.mult))
            t2 = route[:, 290:292]
            link(dve.tensor_reduce(gmax, gl, AX.X, ALU.max))
            link(dve.tensor_tensor(tiles(ge, 2), gl, bc(gmax, 4), ALU.subtract))
            first_of(one_g, gl, gmax, t2)
            dve.tensor_copy(gsum, ge).then_inc(S("rt_1"), 1)
            dve.wait_ge(S("rt_1"), 1)
            el4 = route[:, 0:40].rearrange("p (t c) -> p t c", t=2)[:, :, 4:20]
            for t in range(2):
                e_t = el4[:, t, :].rearrange("p (g e) -> p g e", g=4)
                link(dve.tensor_tensor(pick[:, t, :].rearrange("p (g e) -> p g e", g=4), e_t,
                                       one_g[:, t, :].unsqueeze(2).to_broadcast([P, 4, 4]), ALU.mult))
                link(dve.tensor_reduce(in_g[:, t, :], pick[:, t, :].rearrange("p (g e) -> p e g", g=4), AX.X, ALU.add))
            link(dve.tensor_reduce(m1, in_g, AX.X, ALU.max))
            first_of(o1, in_g, m1, t2)
            link(dve.scalar_tensor_tensor(rest, o1, 2.0 * NEG, in_g, ALU.mult, ALU.add))
            link(dve.tensor_reduce(m2, rest, AX.X, ALU.max))
            first_of(o2, rest, m2, t2)
            dve.tensor_tensor(w2, m2, m1, ALU.subtract).then_inc(S("rt_2"), 1)
            dve.wait_ge(S("rt_e"), 2)
            link(dve.tensor_reduce(gw, tiles(gsum, 2), AX.X, ALU.add))
            link(dve.tensor_scalar(w1, w2, 1.0, None, ALU.add))
            link(dve.tensor_tensor(w1, w1, gw, ALU.mult))
            link(dve.reciprocal(w1, w1))
            link(dve.tensor_tensor(w2, w2, w1, ALU.mult))
            link(dve.tensor_tensor(o1, o1, bc(w1, 4), ALU.mult))
            link(dve.tensor_tensor(o2, o2, bc(w2, 4), ALU.mult))
            link(dve.tensor_tensor(o1, o1, o2, ALU.add))
            for t in range(2):
                ins = dve.tensor_tensor(pick[:, t, :].rearrange("p (g e) -> p g e", g=4),
                                        one_g[:, t, :].unsqueeze(2).to_broadcast([P, 4, 4]),
                                        o1[:, t, :].unsqueeze(1).to_broadcast([P, 4, 4]), ALU.mult)
                ins.then_inc(S("combine"), 1)
            for n in range(8):
                dve.wait_ge(S("side_full"), SI[f"comb{n}"] + 1)
                dve.tensor_copy(comb_all[:, 2 * n:2 * n + 2, :], tiles(bank[7][:, :], 2)).then_inc(S("side_free"), 1)
            dve.wait_ge(S("side_free"), SI["comb7"] + 1)

            def hid_steps(name, steps, experts=False):
                s0 = STEP0[name]

                def step(parity, s, expert=None):
                    dve.wait_ge(S("silu_done"), s + (s0 + 1))
                    if not isinstance(s, int) or s >= 1:
                        dve.wait_ge(S("unit_used"), s * 3 + (D_UNITS[name] - 1))
                    up = tiles(bank[5 + 2 * parity][:, :], 2)
                    if not experts:
                        dve.tensor_tensor(hid[parity], sil[parity], up, ALU.mult).then_inc(S("hid_done"), 1)
                        return
                    dve.tensor_tensor(sil[parity], sil[parity], up, ALU.mult).then_inc(S("half_hid"), 1)
                    dve.wait_ge(S("half_hid"), s + 1)
                    dve.tensor_tensor(hid[parity], sil[parity], comb_all[:, expert, :].to_broadcast([P, 2, T]),
                                      ALU.mult).then_inc(S("hid_done"), 1)
                step(0, 0, slice(0, 1))
                with dve.Fori(0, (steps - 1) // 2) as i:
                    step(1, i * 2 + 1, bass.ds(i, 1))
                    step(0, i * 2 + 2, bass.ds(i + 1, 1))
                if steps % 2 == 0:
                    step(1, steps - 1, slice(N_EXP - 1, N_EXP))

            hid_steps("moe", MOE_STEPS, experts=True)
            dve.wait_ge(S("unit_used"), D_UNITS["moe"] + 3 * MOE_STEPS)
            for b in range(4):
                ins = dve.tensor_tensor(X[:, 2 * b:2 * b + 2, :], tiles(bank[b][:, :], 2), X[:, 2 * b:2 * b + 2, :], ALU.add)
            ins.then_inc(S("out_1"), 1)
            dve.wait_ge(S("out_1"), 1)
            norm(2, "norm2", P1("nf"), X)

            def add_normed(n, gain_index, half):
                gain = P2("n")[:, gain_index * KD:(gain_index + 1) * KD]
                if half:
                    link(dve.tensor_scalar(half_gain, gain, 0.5, None, ALU.mult))
                    gain = half_gain
                dve.wait_ge(S("side_free"), SI[f"n{n}"] + 1)
                link(dve.reciprocal(rstd[:, :], rstd[:, :]))
                for k in range(KD):
                    ins = dve.scalar_tensor_tensor(SQ[:, k, :], bank[k // 2][:, (k % 2) * T:(k % 2 + 1) * T],
                                                   gain[:, k:k + 1], rstd[:, :], ALU.mult, ALU.mult)
                link(ins)
                dve.tensor_tensor(X[:, :, :], X[:, :, :], SQ[:, :, :], ALU.add).then_inc(S("added"), 1)
                dve.wait_ge(S("added"), (n - 2) // 2)

            def pre_norm(n, gain_index):
                norm(n, f"n{n}", P2("n")[:, gain_index * KD:(gain_index + 1) * KD], H)

            def ffn(n, first, layer, place):
                pre_norm(first, 6 * layer + place)
                hid_steps(f"ffn{n}", FFN_STEPS)
                add_normed(first + 1, 6 * layer + place + 1, True)

            dve.wait_ge(S("normed"), 3 * KD)
            dve.wait_ge(S("sm2"), 16)
            ffn(0, 3, 0, 0)
            pre_norm(5, 2)

            def shift(n):
                dve.wait_ge(S("proj_free"), GI[f"ab{n}"] + 1)
                two = slice(2 * n, 2 * n + 2)
                link(dve.tensor_tensor(pp[:, two, :], pr[:, two, 0:T], pr[:, two, 1:1 + T], ALU.subtract))
                for m in range(2 * n, 2 * n + 2):
                    ins = dve.scalar_tensor_tensor(pp[:, m, :], pp[:, m, :], P2("mu")[:, m:m + 1], pr[:, m, 1:1 + T],
                                                   ALU.mult, ALU.add)
                return ins

            link(dve.tensor_scalar(hd_base, P2("d_base"), 0.5, None, ALU.mult))
            dve.tensor_scalar(hi_base, P2("i_base"), 0.5, None, ALU.mult).then_inc(S("half_bias"), 1)
            shift(6).then_inc(S("shifted"), 1)
            dve.wait_ge(S("lora_in"), 2)
            dve.tensor_scalar(pp[:, 13, :], pp[:, 13, :], 0.5, 0.5, ALU.mult, ALU.add).then_inc(S("gate_in"), 1)
            for n in range(2):
                link(shift(n))
            dve.wait_ge(S("lora_out"), MT)
            c_log = -0.5 * float(np.exp(-0.5))
            link(dve.tensor_scalar(lw[:, :, :], lw[:, :, :], 1.0, c_log, ALU.add, ALU.mult))
            for m in range(MT):
                ins = dve.tensor_tensor_scan(cum_l[:, m, :], C("keep"), lw[:, m, :], 0.0, ALU.mult, ALU.add)
            link(ins)
            dve.tensor_tensor(e_p[:, :, :], cum_l[:, :, :], lw[:, :, :], ALU.subtract).then_inc(S("logs"), 1)
            dve.wait_ge(S("lora_out"), 2 * MT)
            link(dve.tensor_scalar(rate[:, :, :], rate[:, :, :], 0.5, 0.5, ALU.mult, ALU.add))
            for n in range(2, 4):
                link(shift(n))
            r, k, v = pp[:, 0:4, :], pp[:, 4:8, :], pp[:, 8:12, :]
            for m in range(MT):
                ins = dve.tensor_scalar(kk[:, m, :], k[:, m, :], P2("k_k")[:, m:m + 1], None, ALU.mult)
            link(ins)
            dve.tensor_tensor(kkt[:, :, :], kk[:, :, :], kk[:, :, :], ALU.mult).then_inc(S("kk_sq"), 1)
            for m in range(MT):
                ins = dve.tensor_scalar(bh[:, m, :], rate[:, m, :], 1.0, P2("k_a")[:, m:m + 1], ALU.subtract, ALU.mult)
            link(ins)
            link(dve.scalar_tensor_tensor(k, bh[:, :, :], 1.0, k, ALU.add, ALU.mult))
            for m in range(MT):
                ins = dve.scalar_tensor_tensor(qt[:, m, :], r[:, m, :], P2("r_k")[:, m:m + 1], k[:, m, :], ALU.mult,
                                               ALU.mult)
            ins.then_inc(S("bonus_in"), 1)
            for n in range(4, 6):
                link(shift(n))
            for n in range(2):
                dve.wait_ge(S("side_full"), SI[f"kk{n}"] + 1)
                dve.tensor_scalar(e_l[:, 2 * n:2 * n + 2, :], tiles(bank[7][:, :], 2), 1e-24, None, ALU.max)\
                   .then_inc(S("side_free"), 1)
            dve.wait_ge(S("side_free"), SI["kk1"] + 1)
            dve.tensor_copy(half_gain, half_gain).then_inc(S("kk_max"), 1)
            dve.wait_ge(S("kk_root"), 1)
            link(dve.reciprocal(e_l[:, :, :], e_l[:, :, :]))
            dve.tensor_tensor(kk[:, :, :], kk[:, :, :], e_l[:, :, :], ALU.mult).then_inc(S("kk_used"), 1)
            dve.wait_ge(S("kk_used"), 1)
            for n in range(2):
                dve.wait_ge(S("side_full"), SI[f"bo{n}"] + 1)
                dve.tensor_tensor(bon[:, 2 * n:2 * n + 2, :], tiles(bank[7][:, :], 2), v[:, 2 * n:2 * n + 2, :], ALU.mult)\
                   .then_inc(S("side_free"), 1)
            dve.wait_ge(S("exps"), 2)
            link(dve.tensor_tensor(kkt[:, :, :], kk[:, :, :], e_p[:, :, :], ALU.mult))
            link(dve.tensor_tensor(kh[:, :, :], k, e_n[:, :, :], ALU.mult))
            link(dve.tensor_tensor(bh[:, :, :], kk[:, :, :], rate[:, :, :], ALU.mult))
            link(dve.tensor_tensor(bh[:, :, :], bh[:, :, :], e_n[:, :, :], ALU.mult))
            dve.wait_ge(S("exps"), 3)
            link(dve.tensor_copy(e_last, e_l[:, :, P - 1]))
            dve.tensor_tensor(qt[:, :, :], r, e_l[:, :, :], ALU.mult).then_inc(S("factors"), 1)
            dve.wait_ge(S("zeroed_2"), 1)
            dve.wait_ge(S("proj_free"), GI["ab8"] + 1)
            for m in range(MT):
                dve.scalar_tensor_tensor(glu[:, m, CONV_B - 1:CONV_B - 1 + T], cg[:, m, :], 1.0, cv[:, m, :], ALU.add,
                                         ALU.mult).then_inc(S("glu"), 1)
            dve.wait_ge(S("glu"), MT)
            dve.wait_ge(S("tok_ok"), 1)
            for c in range(TT):
                for p in range(4):
                    for par in range(2):
                        job = 8 * c + 2 * p + par
                        dve.wait_ge(S("gram_full"), job + 1)
                        dve.tensor_tensor(gram[:, 8 * c + 4 * par + p, :, :], tiles(bank[par + 2 * (p % 2)][:, :], 4),
                                          tiles(C("gram"), 4), ALU.mult).then_inc(S("gram_free"), 1)
            dve.wait_ge(S("gram_free"), N_MAT)
            ident4 = C("ident").unsqueeze(1).to_broadcast([P, 4, P])
            for g in range(4):
                four = slice(4 * g, 4 * g + 4)
                dve.wait_ge(S("y_free"), g + 1)
                link(dve.tensor_tensor(mat_w[:, four, :], mat_y[:, four, :],
                                       C("level_t").unsqueeze(1).to_broadcast([P, 4, P]), ALU.mult))
                link(dve.tensor_tensor(mat_w[:, four, :], mat_w[:, four, :], ident4, ALU.add))
                dve.tensor_tensor(mat_m[:, four, :], gram[:, four, 2, :], ident4, ALU.add).then_inc(S("mat_ok"), 1)
            dve.wait_ge(S("mat_ok"), 4)

            def q_out(n):
                level = C("level")[:, (n // 4 + 1) * P:(n // 4 + 2) * P].unsqueeze(1).to_broadcast([P, 4, P])
                dve.wait_ge(S("q_full"), n + 1)
                if n >= 2:
                    dve.wait_ge(S("mw_full"), n - 1)
                dve.tensor_tensor(tiles(mat_q[:, n % 2, :], 4), tiles(bank[n % 2][:, :], 4), level, ALU.mult)\
                   .then_inc(S("q_ok"), 1)

            def mw_out(n):
                four = slice(4 * (n % 4), 4 * (n % 4) + 4)
                dve.wait_ge(S("mw_full"), n + 1)
                if n < N_INV - 4:
                    dve.tensor_tensor(mat_w[:, four, :], mat_w[:, four, :], tiles(bank[5 + n % 2][:, :], 4), ALU.subtract)
                dve.tensor_tensor(mat_m[:, four, :], mat_m[:, four, :], tiles(bank[2 + n % 2][:, :], 4), ALU.subtract)\
                   .then_inc(S("mw_ok"), 1)

            for n in range(N_INV + 1):
                if n < N_INV:
                    q_out(n)
                if n:
                    mw_out(n - 1)
            dve.wait_ge(S("mw_ok"), N_INV)
            dve.wait_ge(S("rw_full"), 3)
            for m in range(MT):
                ins = dve.scalar_tensor_tensor(state[:, m, :], bank[3][:, m * P:(m + 1) * P], e_last[:, m:m + 1],
                                               C("head1"), ALU.mult, ALU.mult)
            ins.then_inc(S("state"), 1)
            dve.tensor_copy(rw_y[:, 0, :], bank[2][:, :]).then_inc(S("gn_in"), 1)
            dve.wait_ge(S("rw_full"), 6)
            dve.tensor_copy(rw_y[:, 1, :], bank[6][:, :]).then_inc(S("gn_in"), 1)
            dve.wait_ge(S("gn_in"), 2)
            yh = rw_y[:, :, :].rearrange("p c (h v) -> p (c h) v", v=HD)
            ysq = arena[:, phase:phase + TT * MIX].rearrange("p (h v) -> p h v", v=HD)
            link(dve.tensor_reduce(gn_sum, yh, AX.X, ALU.add))
            link(dve.tensor_scalar(gn_sum, gn_sum, 1.0 / HD, None, ALU.mult))
            link(dve.tensor_tensor(yh, yh, gn_sum.unsqueeze(2).to_broadcast([P, 16, HD]), ALU.subtract))
            link(dve.tensor_tensor(ysq, yh, yh, ALU.mult))
            dve.tensor_reduce(gn_sum, ysq, AX.X, ALU.add).then_inc(S("gn_var"), 1)
            dve.wait_ge(S("gn_root"), 1)
            link(dve.reciprocal(gn_rs, gn_rs))
            dve.tensor_tensor(yh, yh, gn_rs.unsqueeze(2).to_broadcast([P, 16, HD]), ALU.mult).then_inc(S("gn_y"), 1)
            dve.wait_ge(S("gn_out"), MT)
            link(dve.tensor_tensor(H[:, 0:MT, :], H[:, 0:MT, :], bon[:, :, :], ALU.add))
            dve.tensor_tensor(H[:, 0:MT, :], H[:, 0:MT, :], gup[:, :, :], ALU.mult).then_inc(S("y_rw"), 1)
            dve.wait_ge(S("conv_2"), 1)
            for m in range(MT):
                ins = dve.tensor_scalar(cacc[:, m, :], cacc[:, m, :], 0.5, P2("conv_b")[:, m:m + 1], ALU.mult, ALU.add)
            ins.then_inc(S("ln_in"), 1)
            dve.wait_ge(S("side_free"), SI["ln1"] + 1)
            dve.tensor_tensor(cacc[:, :, :], cacc[:, :, :], e_mean.unsqueeze(1).to_broadcast([P, MT, T]), ALU.subtract)\
               .then_inc(S("ln_centered"), 1)
            dve.wait_ge(S("side_free"), SI["ln2"] + 1)
            link(dve.reciprocal(rstd[:, :], rstd[:, :]))
            dve.tensor_tensor(cacc[:, :, :], cacc[:, :, :], rstd[:, :].unsqueeze(1).to_broadcast([P, MT, T]), ALU.mult)\
               .then_inc(S("ln_scaled"), 1)
            add_normed(6, 3, False)
            ffn(1, 7, 0, 4)
            ffn(2, 9, 1, 0)

            pre_norm(11, 8)
            link(dve.tensor_scalar(qg8, P2("qg"), SCALE, None, ALU.mult))

            def head_norm(n):
                dve.wait_ge(S("side_free"), SI[f"hs{n}"] + 1)
                link(dve.reciprocal(f_rs[:, n % 2, :], f_rs[:, n % 2, :]))
                gain = qg8 if n < 4 else P2("kg")
                dve.wait_ge(S("proj_free"), GI[f"c{n}"] + 1)
                dve.scalar_tensor_tensor(fq[:, 2 * n:2 * n + 2, :], fq[:, 2 * n:2 * n + 2, :], gain[:, 0:1],
                                         tiles(f_rs[:, n % 2, :], 2), ALU.mult, ALU.mult).then_inc(S("hn_done"), 1)

            for n in range(8):
                head_norm(n)
            s = slice(0, N_FOX)
            dve.wait_ge(S("side_full"), SI["f"] + 1)
            dve.tensor_scalar(fz[s, :], bank[7][s, 0:T], P2("fb")[s, :], None, ALU.add).then_inc(S("side_free"), 1)
            dve.wait_ge(S("side_free"), SI["f"] + 1)
            link(dve.tensor_scalar(fa[s, :], fz[s, :], -1.0, None, ALU.mult))
            dve.tensor_tensor(fa[s, :], fa[s, :], fz[s, :], ALU.max).then_inc(S("f_abs"), 1)
            link(dve.tensor_scalar(fm[s, :], fz[s, :], -1.0, 0.0, ALU.mult, ALU.max))
            dve.wait_ge(S("f_exp"), 1)
            dve.tensor_scalar(fa[s, :], fe[s, :], 1.0, None, ALU.add).then_inc(S("f_one"), 1)
            dve.wait_ge(S("f_one"), 1)
            link(dve.tensor_scalar(fz[s, :], fa[s, :], -1.0, None, ALU.add))
            link(dve.tensor_scalar(fc[s, :], fz[s, :], 0.0, None, ALU.is_equal))
            link(dve.tensor_tensor(fz[s, :], fz[s, :], fc[s, :], ALU.add))
            link(dve.reciprocal(fz[s, :], fz[s, :]))
            dve.wait_ge(S("f_log"), 1)
            link(dve.tensor_tensor(fz[s, :], fl[s, :], fz[s, :], ALU.mult))
            link(dve.tensor_tensor(fz[s, :], fz[s, :], fc[s, :], ALU.add))
            link(dve.tensor_tensor(fz[s, :], fz[s, :], fe[s, :], ALU.mult))
            link(dve.tensor_tensor(fz[s, :], fz[s, :], fm[s, :], ALU.add))
            link(dve.memset(fm[s, :], 0.0))
            dve.tensor_tensor_scan(fc[s, :], fz[s, :], fm[s, :], 0.0, ALU.add, ALU.add).then_inc(S("f_cum"), 1)

            def fox_slot(n):
                if n < N_FOX:
                    b = n % 2
                    dve.wait_ge(S("fsc_full"), n + 1)
                    dve.wait_ge(S("mc"), n + 1)
                    if n >= 2:
                        dve.wait_ge(S("fexp_done"), 2 * (n - 1))
                    dve.tensor_tensor(fat_s[:, b, :], bank[b][:, 0:384], f_mc[:, b, :], ALU.add).then_inc(S("fsc_free"), 1)
                    dve.wait_ge(S("fsc_free"), n + 1)
                    dve.tensor_reduce(neg_max[:, 2 * b:2 * b + 1], fat_s[:, b, 0:P], AX.X, ALU.max)
                    link(dve.tensor_reduce(neg_max[:, 2 * b + 1:2 * b + 2], fat_s[:, b, P:3 * P], AX.X, ALU.max))
                    dve.tensor_scalar(neg_max[:, 2 * b:2 * b + 2], neg_max[:, 2 * b:2 * b + 2], -1.0, None, ALU.mult)\
                       .then_inc(S("fmax_ok"), 1)
                if 1 <= n <= N_FOX:
                    b = (n - 1) % 2
                    dve.wait_ge(S("fexp_done"), 2 * n)
                    inv = inv_sum[:, 2 * b:2 * b + 2]
                    link(dve.reciprocal(inv, row_sum[:, 2 * b:2 * b + 2]))
                    link(dve.tensor_scalar(inv, inv, 0.5, None, ALU.mult))
                    for t, (a, z) in enumerate(((0, P), (P, 3 * P))):
                        ins = dve.tensor_scalar(fat_p[:, b, a:z], fat_p[:, b, a:z], inv[:, t:t + 1], None, ALU.mult)
                    ins.then_inc(S("fp_ok"), 1)
                if n >= 3 and n % 2 == 1:
                    p = (n - 3) // 2
                    dve.wait_ge(S("fpv_done"), 2 * (p + 1))
                    if p == 0:
                        dve.wait_ge(S("proj_free"), GI["c15"] + 1)
                    dve.scalar_tensor_tensor(f_o[:, p, :], f_gate[:, p, :], 1.0, bank[4][:, (p % 2) * T:(p % 2 + 1) * T],
                                             ALU.add, ALU.mult).then_inc(S("fo_free"), 1)

            fox_schedule(fox_slot, lambda j: None)
            add_normed(12, 9, False)
            ffn(3, 13, 1, 4)
            dve.tensor_copy(half_gain, half_gain).then_inc(S("out"), 1)

        @block.tensor
        def _(pe):
            def unit_ready(n, count=None):
                pe.wait_ge(S(f"unit{n % RING}"), 16 * (n // RING + 1) if count is None else count)
                return ring[:, n % RING, :].rearrange("p (k n) -> p k n", k=KD)

            def side_begin(name):
                if SI[name]:
                    pe.wait_ge(S("side_free"), SI[name])
                return bank[7]

            def norm_sums(n, name):
                side_begin(name)
                pe.wait_ge(S("squares"), n + 1)
                for k in range(KD):
                    ins = pe.matmul(bank[7][:, 0:T], C("ones"), SQ[:, k, :], start=(k == 0), stop=(k == KD - 1))
                ins.then_inc(S("side_full"), 1)

            def group_begin(name):
                n = GI[name]
                if n >= 2:
                    pe.wait_ge(S("proj_free"), n - 1)
                return bank[5 + n % 2]

            def project(ps, weights, src=H):
                for k in range(KD):
                    ins = pe.matmul(ps, weights(k), src[:, k, :], start=(k == 0), stop=(k == KD - 1))
                return ins

            def project_tokens(ps, weights, width):
                for t in range(TT):
                    for k in range(KD):
                        ins = pe.matmul(ps[:, t * width:(t + 1) * width], H[:, k, t * P:(t + 1) * P], weights(k),
                                        start=(k == 0), stop=(k == KD - 1))
                return ins

            def unit_channels(ps, w):
                for c in range(2):
                    ins = project(ps[:, c * T:(c + 1) * T], lambda k: w[:, k, c * P:(c + 1) * P])
                ins.then_inc(S("unit_used"), 1)

            pe.wait_ge(S("con"), 16)
            norm_sums(0, "norm0")
            pe.wait_ge(S("normed"), KD)
            for name in ("u0", "u1", "v0", "v1", "ga0", "ga1", "re0", "re1", "q0", "q1", "kvc"):
                ps, w = group_begin(name), unit_ready(FULL[name][1] - 1)
                if name[0] == "v":
                    project_tokens(ps, lambda k: w[:, k, :], UC).then_inc(S("unit_used"), 1)
                else:
                    unit_channels(ps, w)
            for k_name, v_name in (("ks", "vs"), ("kw", "vw")):
                ps, w = group_begin(k_name), unit_ready(FULL[v_name][1] - 1)
                for g in range(2):
                    for half in range(2):
                        ins = project(ps[HD * half:HD * half + HD, g * T:(g + 1) * T],
                                      lambda k: w[:, k, g * HD:(g + 1) * HD])
                ins.then_inc(S("part_full"), 1)
                ps = group_begin(v_name)
                project_tokens(ps, lambda k: w[:, k, P:2 * P], P).then_inc(S("unit_used"), 1)
            pe.wait_ge(S("sm1"), 16)
            w_gate = P1("w_gate").rearrange("p (k n) -> p k n", k=KD)
            project_tokens(group_begin("g24"), lambda k: w_gate[:, k, :], 24).then_inc(S("part_full"), 1)
            for name in ("xd0", "xd1"):
                unit_channels(group_begin(name), unit_ready(FULL[name][1] - 1))

            gm_w = tiles(P1("gm_wT"), 4)
            wa, wx, pool_w = tiles(P1("wa"), MT), tiles(P1("wx"), MT), tiles(P1("pool_w"), MT)
            cw2 = P1("cw2").rearrange("p (c d) -> p c d", c=2)

            def gmlp(pair):
                ps = side_begin(f"gm{pair}")
                pe.wait_ge(S("v_normed"), TT)
                for t in range(2):
                    g = 2 * pair + t
                    for n in range(TT):
                        ins = pe.matmul(ps[:, t * T + n * P:t * T + (n + 1) * P], v1[:, n, g * P:(g + 1) * P],
                                        gm_w[:, g, :], start=True, stop=True)
                ins.then_inc(S("side_full"), 1)

            def compress_hidden():
                ps = side_begin("hid")
                pe.wait_ge(S("kpe"), 1)
                pe.wait_ge(S("cw1"), 16)
                for c in range(2):
                    for g in range(2):
                        h = slice(HD * g, HD * g + HD)
                        for l in range(32):
                            ins = pe.matmul(ps[h, c * 16:c * 16 + N_CMP], cw1[h, c, l, :], kpe[h, c, l, 0:N_CMP],
                                            start=(l == 0), stop=(l == 31))
                ins.then_inc(S("side_full"), 1)

            def compress_out():
                side_begin("kvc2")
                for g in range(2):
                    ps = (bank[7], bank[4])[g]
                    h = slice(HD * g, HD * g + HD)
                    for half in range(2):
                        pe.matmul(ps[HD * half:HD * half + HD, g * 16:g * 16 + N_CMP], cw2[h, 0, :],
                                  hid_c[h, 0, 0:N_CMP], start=True, stop=True)
                    ins = pe.matmul(ps[0:N_CMP, P + g * HD:P + (g + 1) * HD], hid_c[h, 1, 0:N_CMP], cw2[h, 1, :],
                                    start=True, stop=True)
                ins.then_inc(S("side_full"), 1)

            def pairs(name, w, src, ready, count):
                ps = side_begin(name)
                pe.wait_ge(S(ready), count)
                for t in range(2):
                    m = 2 * int(name[-1]) + t
                    ins = pe.matmul(ps[:, t * T:(t + 1) * T], w[:, m, :], src[:, m, :], start=True, stop=True)
                ins.then_inc(S("side_full"), 1)

            def run_mg(j):
                if j in (1, 2):
                    gmlp(j - 1)
                if j == 2:
                    compress_hidden()
                if j == 3:
                    compress_out()
                if j in (7, 8):
                    pairs(f"wa{j - 7}", wa, xc, "xc", MT)
                if j in (9, 10):
                    pairs(f"wx{j - 9}", wx, xc, "xc", MT)
                if j in (11, 12):
                    pairs(f"po{j - 11}", pool_w, xd[:, :, 16:16 + T], "pooled", MT)
                unit_channels(group_begin(f"mg{j}"), unit_ready(FULL[f"mg{j}"][1] - 1))

            def scores(n):
                h, kind = n // 3, n % 3
                hp, g = slice(HD * (h % 2), HD * (h % 2) + HD), h // 4
                ps = bank[n % 2]
                if n == 0:
                    pe.wait_ge(S("side_free"), SI["kvc2"] + 1)
                if n >= 2:
                    pe.wait_ge(S("sc_free"), n - 1)
                for t in range(TT):
                    q = q1[hp, h // 2, t * P:(t + 1) * P]
                    if kind == 0:
                        ins = pe.matmul(ps[:, t * 16:t * 16 + N_CMP], q, k_c[hp, g, 0:N_CMP], start=True, stop=True)
                    else:
                        k = kd[hp, 2 * (kind - 1) + g, :]
                        ins = pe.matmul(ps[:, P * t:P * t + P + P * t], q, k[:, 0:P * (t + 1)], start=True, stop=True)
                ins.then_inc(S("sc_full"), 1)

            def turn(n):
                pe.wait_ge(S("p_ok"), n + 1)
                if n >= 2:
                    pe.wait_ge(S("pt_free"), n - 1)
                ps = bank[2 + n % 2]
                src = p_cmp if n % 3 == 0 else att_p[:, n % 2, :]
                for b in range(2 if n % 3 == 0 else 3):
                    ins = pe.transpose(ps[:, b * P:(b + 1) * P], src[:, b * P:(b + 1) * P], C("ident"))
                ins.then_inc(S("pt_full"), 1)

            def values(n):
                h, kind = n // 3, n % 3
                g, pair = h // 4, h // 2
                pe.wait_ge(S("pt_free"), n + 1)
                if n % 6 == 0 and pair >= 2:
                    pe.wait_ge(S("o_free"), pair - 1)
                o = bank[4][HD * (h % 2):HD * (h % 2) + HD, (pair % 2) * T:(pair % 2) * T + T]
                w = att_t[:, n % 2, :]
                if kind == 0:
                    ins = pe.matmul(o, v_c[:, g * HD:(g + 1) * HD], w[:, 0:T], start=True, stop=False)
                else:
                    v = vn[:, kind - 1, :].rearrange("p (t d) -> p t d", t=TT)[:, :, g * HD:(g + 1) * HD]
                    pe.matmul(o, v[:, 0, :], w[:, 0:T], start=False, stop=False)
                    ins = pe.matmul(o[:, P:T], v[:, 1, :], w[:, T:T + P], start=False, stop=(kind == 2))
                ins.then_inc(S("pv_done"), 1)

            def run_slot(n):
                if n < N_SLOTS:
                    scores(n)
                if 1 <= n <= N_SLOTS:
                    turn(n - 1)
                if n >= 2:
                    values(n - 2)

            schedule(run_slot, run_mg)

            ready = {0: ("zeroed", 1), 1: ("y_b", 1), 2: ("o_free", MT), 3: ("side_free", SI["po1"] + 1)}
            for n, y in ((0, u), (1, gate), (2, yc), (3, yd)):
                pe.wait_ge(S(ready[n][0]), ready[n][1])
                if n == 3:
                    pe.wait_ge(S("side_free"), SI["po1"] + 1)
                src = y
                for half in range(2):
                    unit = 2 * n + half
                    unit_ready(D_UNITS["branch"] + unit)
                    w = ring[:, (D_UNITS["branch"] + unit) % RING, :].rearrange("p (k n) -> p k n", k=MT)
                    if unit >= 2:
                        pe.wait_ge(S("br_free"), 2 * (unit - 1))
                    for d in range(4):
                        ps = bank[2 * half + d // 2][:, (d % 2) * T:(d % 2 + 1) * T]
                        for k in range(MT):
                            ins = pe.matmul(ps, w[:, k, d * P:(d + 1) * P], src[:, k, :], start=(k == 0),
                                            stop=(k == MT - 1))
                    ins.then_inc(S("unit_used"), 1)

            def square(name, src, ready, count):
                pe.wait_ge(S(ready), count)
                for n in range(SQUARE):
                    w = unit_ready(D_UNITS[name] + n)
                    for c in range(2):
                        ins = project(bank[n][:, c * T:(c + 1) * T], lambda k: w[:, k, c * P:(c + 1) * P], src)
                    ins.then_inc(S("unit_used"), 1)

            square("w_out", H, "merged", 1)
            norm_sums(1, "norm1")
            side_begin("route")
            pe.wait_ge(S("normed"), 2 * KD)
            w_route = P1("w_route").rearrange("p (k n) -> p k n", k=KD)
            project_tokens(bank[7], lambda k: w_route[:, k, :], 20).then_inc(S("side_full"), 1)

            def gated(name, steps, last_side):
                u0 = D_UNITS[name]

                def start_sums():
                    for b in range(4):
                        pe.matmul(bank[b][:, :], zeros[:, 0:P], zeros[:, :], start=True, stop=False)

                def gate_up(parity, n, load, s):
                    if s is not None:
                        pe.wait_ge(S("hid_done"), s + 1)
                    for which in range(2):
                        w = unit_ready(n + which, load(which) if load else None)
                        ps = bank[4 + 2 * parity + which]
                        for c in range(2):
                            ins = project(ps[:, c * T:(c + 1) * T], lambda k: w[:, k, c * P:(c + 1) * P])
                        ins.then_inc(S("unit_used"), 1)

                def down(parity, n, load, s, last=False):
                    pe.wait_ge(S("hid_done"), s + 1)
                    unit_ready(n, load)
                    w = ring[:, n % RING, :].rearrange("p (k n) -> p k n", k=2)
                    for k in range(2):
                        for d in range(KD):
                            ins = pe.matmul(bank[d // 2][:, (d % 2) * T:(d % 2 + 1) * T], w[:, k, d * P:(d + 1) * P],
                                            hid[parity][:, k, :], start=False, stop=False, skip_group_check=True)
                    if last:
                        for b in range(4):
                            ins = pe.matmul(bank[b][:, :], zeros[:, 0:P], zeros[:, :], start=False, stop=True)
                    ins.then_inc(S("unit_used"), 1)

                s0 = STEP0[name]
                start_sums()
                gate_up(0, u0, None, None)
                pe.wait_ge(S("side_free"), SI[last_side] + 1)
                trips = (steps - 1) // 2
                n1 = u0 + 2
                with pe.Fori(0, trips) as i:
                    def load_of(n):
                        return i * 16 + 16 * (n // RING + 1)
                    gate_up(1, n1, lambda which: load_of(n1 + which), i * 2 + s0)
                    down(0, n1 + 2, load_of(n1 + 2), i * 2 + (s0 + 1))
                    gate_up(0, n1 + 3, lambda which: load_of(n1 + 3 + which), i * 2 + (s0 + 1))
                    down(1, n1 + 5, load_of(n1 + 5), i * 2 + (s0 + 2))
                n2 = n1 + 6 * trips
                if steps % 2 == 0:
                    gate_up(1, n2, None, s0 + steps - 2)
                    down(0, n2 + 2, None, s0 + steps - 1)
                    n2 += 3
                down((steps - 1) % 2, n2, None, s0 + steps, last=True)

            def spread_weights():
                pe.wait_ge(S("combine"), TT)
                for n in range(8):
                    side_begin(f"comb{n}")
                    for c in range(2):
                        e = 2 * n + c
                        for t in range(TT):
                            w = route_pick[:, t, e:e + 1].to_broadcast([P, P])
                            ins = pe.matmul(bank[7][:, c * T + t * P:c * T + (t + 1) * P], w, C("ident"), start=True,
                                            stop=True)
                    ins.then_inc(S("side_full"), 1)

            spread_weights()
            gated("moe", MOE_STEPS, "comb7")
            norm_sums(2, "norm2")

            ffn_sides = {0: "n3", 1: "n7", 2: "n9", 3: "n13"}

            def pre_norm(n):
                norm_sums(n, f"n{n}")
                pe.wait_ge(S("normed"), (3 + (n - 3) // 2 + 1) * KD)

            def ffn(n, first):
                pre_norm(first)
                gated(f"ffn{n}", FFN_STEPS, f"n{first}")
                norm_sums(first + 1, f"n{first + 1}")

            ffn(0, 3)
            pre_norm(5)

            def ab_unit(n):
                unit_channels(group_begin(f"ab{n}"), unit_ready(FULL[f"ab{n}"][1] - 1))

            for n in (6, 0, 1):
                ab_unit(n)
            pe.wait_ge(S("sm2"), 16)
            pe.wait_ge(S("added"), 1)
            pe.wait_ge(S("lora_in"), 1)
            for half in range(2):
                h = slice(HD * half, HD * half + HD)
                for m in range(MT):
                    ins = pe.matmul(bank[2 * half + m // 2][:, (m % 2) * T:(m % 2 + 1) * T],
                                    P2("lora")[h, m * P:(m + 1) * P], pp[h, 12, :], start=True, stop=True)
            ins.then_inc(S("lora_full"), 1)
            for n in (2, 3, 4, 5):
                ab_unit(n)
            for n in range(2):
                ps = side_begin(f"gu{n}")
                pe.wait_ge(S("gate_in"), 1)
                for c in range(2):
                    m = 2 * n + c
                    ins = pe.matmul(ps[:, c * T:(c + 1) * T], P2("gate_up")[:, m * P:(m + 1) * P], pp[:, 13, :],
                                    start=True, stop=True)
                ins.then_inc(S("side_full"), 1)
            ab_unit(9)

            def head_sums(name, src, ready, count):
                ps = side_begin(name)
                pe.wait_ge(S(ready), count)
                pe.matmul(ps[:, :], C("head1"), src, start=True, stop=True).then_inc(S("side_full"), 1)

            for n in range(2):
                head_sums(f"kk{n}", kkt[:, 2 * n:2 * n + 2, :], "kk_sq", 1)
            for n in (10, 7, 8):
                ab_unit(n)
            for n in range(2):
                head_sums(f"bo{n}", qt[:, 2 * n:2 * n + 2, :], "bonus_in", 1)
            pe.wait_ge(S("lora_out"), 2 * MT)
            pe.wait_ge(S("factors"), 1)
            for b, (src, c) in enumerate(((pp[:, 8:12, :], 0), (pp[:, 8:12, :], 1), (kh, 0), (bh, 0))):
                for m in range(MT):
                    ins = pe.transpose(bank[b][:, m * P:(m + 1) * P], src[:, m, c * P:(c + 1) * P], C("ident"))
            ins.then_inc(S("turned"), 1)
            pe.wait_ge(S("tok_ok"), 1)
            kq = arena[:, 0:2 * MT * T].rearrange("p (a m t) -> p a m t", a=2, m=MT)
            for c in range(TT):
                tok = slice(c * P, (c + 1) * P)
                for p in range(4):
                    for par in range(2):
                        job = 8 * c + 2 * p + par
                        h = slice(HD * par, HD * par + HD)
                        if job >= 4:
                            pe.wait_ge(S("gram_free"), job - 3)
                        ps = bank[par + 2 * (p % 2)]
                        for a, w in enumerate((kh, bh)):
                            ins = pe.matmul(ps[:, 2 * a * P:2 * (a + 1) * P], w[h, p, tok], kq[h, :, p, tok], start=True,
                                            stop=True)
                        ins.then_inc(S("gram_full"), 1)
                for par in range(2):
                    g, h = 2 * c + par, slice(HD * par, HD * par + HD)
                    if g >= 2:
                        pe.wait_ge(S("y_free"), g - 1)
                    else:
                        pe.wait_ge(S("proj_free"), GI["ab8"] + 1)
                    for p in range(4):
                        ins = pe.matmul(bank[5 + g % 2][:, p * P:(p + 1) * P], kkt[h, p, tok], bh[h, p, tok], start=True,
                                        stop=True)
                    ins.then_inc(S("y_full"), 1)

            def q_in(n):
                g = n % 4
                pe.wait_ge(S("mat_ok"), g + 1)
                if n >= 2:
                    pe.wait_ge(S("q_ok"), n - 1)
                if n >= 4:
                    pe.wait_ge(S("mw_ok"), n - 3)
                for i in range(4):
                    ins = pe.matmul(bank[n % 2][:, i * P:(i + 1) * P], mat_y[:, 4 * g + i, :], mat_m[:, 4 * g + i, :],
                                    start=True, stop=True)
                ins.then_inc(S("q_full"), 1)

            def mw_in(n):
                g = n % 4
                pe.wait_ge(S("q_ok"), n + 1)
                if n >= 2:
                    pe.wait_ge(S("mw_ok"), n - 1)
                for i in range(4):
                    q = mat_q[:, n % 2, i * P:(i + 1) * P]
                    ins = pe.matmul(bank[2 + n % 2][:, i * P:(i + 1) * P], mat_w[:, 4 * g + i, :], q, start=True, stop=True)
                    if n < N_INV - 4:
                        ins = pe.matmul(bank[5 + n % 2][:, i * P:(i + 1) * P], q, mat_w[:, 4 * g + i, :], start=True,
                                        stop=True)
                ins.then_inc(S("mw_full"), 1)

            pe.wait_ge(S("gram_free"), N_MAT)
            pe.wait_ge(S("y_free"), 4)
            for n in range(N_INV + 1):
                if n < N_INV:
                    q_in(n)
                if n:
                    mw_in(n - 1)
            pe.wait_ge(S("mw_ok"), N_INV)

            def mat(c, h, what=None):
                i = 8 * c + 4 * (h % 2) + h // 2
                return mat_m[:, i, :] if what is None else gram[:, i, what, :]

            for c in range(TT):
                tok = slice(c * P, (c + 1) * P)
                right, solved, ys = bank[4 * c], bank[4 * c + 1], bank[4 * c + 2]
                if c:
                    pe.wait_ge(S("state"), 1)

                def into(ps, factor, terms, last):
                    for p in range(4):
                        if c:
                            pe.matmul(ps[:, p * P:(p + 1) * P], factor[:, p, tok], state[:, p, :], start=True, stop=False)
                        for par in range(2):
                            h = 2 * p + par
                            cols_h = slice(h * HD, (h + 1) * HD)
                            for n, (which, rhs) in enumerate(terms):
                                ins = pe.matmul(ps[:, cols_h], mat(c, h, which), rhs[:, cols_h],
                                                start=(not c and n == 0), stop=(n == len(terms) - 1 and (not c or par == 1)))
                    return ins
                into(right, kkt, [(0, v_tok[:, c, :])], True).then_inc(S("rw_full"), 1)
                pe.wait_ge(S("rw_r"), c + 1)
                for h in range(N_RW):
                    cols_h = slice(h * HD, (h + 1) * HD)
                    ins = pe.matmul(solved[:, cols_h], mat(c, h), rw_r[:, cols_h], start=True, stop=True)
                ins.then_inc(S("rw_full"), 1)
                pe.wait_ge(S("rw_u"), c + 1)
                ins = into(ys, qt, [(1, v_tok[:, c, :]), (3, rw_u)], True)
                if c == 0:
                    for p in range(4):
                        cols_p = slice(p * P, (p + 1) * P)
                        pe.matmul(bank[3][:, cols_p], kh_tok[:, cols_p], v_tok[:, 0, cols_p], start=True, stop=False)
                        ins = pe.matmul(bank[3][:, cols_p], bh_tok[:, cols_p], rw_u[:, cols_p], start=False, stop=True)
                ins.then_inc(S("rw_full"), 1)
            pe.wait_ge(S("gn_y"), 1)
            for m in range(MT):
                for c in range(TT):
                    ins = pe.transpose(bank[m // 2][:, (m % 2) * T + c * P:(m % 2) * T + (c + 1) * P],
                                       rw_y[:, c, m * P:(m + 1) * P], C("ident"))
            ins.then_inc(S("y_turned"), 1)
            for name, src, ready in (("ln1", cacc, "ln_in"), ("ln2", ctmp, "ln_sq")):
                ps = side_begin(name)
                pe.wait_ge(S(ready), 1)
                for m in range(MT):
                    ins = pe.matmul(ps[:, 0:T], C("ones"), src[:, m, :], start=(m == 0), stop=(m == MT - 1))
                ins.then_inc(S("side_full"), 1)
            pe.wait_ge(S("y_rw"), 1)
            square("ab_out", H, "y_conv", MT)
            norm_sums(6, "n6")
            ffn(1, 7)
            ffn(2, 9)

            pre_norm(11)
            for n in range(8):
                unit_channels(group_begin(f"c{n}"), unit_ready(FULL[f"c{n}"][1] - 1))
                if n:
                    head_sums(f"hs{n - 1}", f_sq[:, (n - 1) % 2, :], "f_sq", n)
            head_sums("hs7", f_sq[:, 1, :], "f_sq", 8)
            ps = side_begin("f")
            w_f = P2("w_f").rearrange("p (k n) -> p k n", k=KD)
            project(ps[0:N_FOX, 0:T], lambda k: w_f[:, k, :]).then_inc(S("side_full"), 1)
            for n in range(8, 12):
                ps, w = group_begin(f"c{n}"), unit_ready(FULL[f"c{n}"][1] - 1)
                project_tokens(ps, lambda k: w[:, k, :], UC).then_inc(S("unit_used"), 1)
            pe.wait_ge(S("f_cum"), 1)
            for n in range(8):
                ps = side_begin(f"cb{n}")
                for c in range(2):
                    h = 2 * n + c
                    pick = C("ident")[0:N_FOX, h:h + 1].to_broadcast([N_FOX, P])
                    ins = pe.matmul(ps[:, c * T:(c + 1) * T], pick, fc[0:N_FOX, :], start=True, stop=True)
                ins.then_inc(S("side_full"), 1)
            pe.wait_ge(S("hn_done"), 8)
            pe.wait_ge(S("proj_free"), GI["c11"] + 1)
            pe.wait_ge(S("added"), 4)

            def fox_slot(n):
                if n < N_FOX:
                    h = slice(HD * (n % 2), HD * (n % 2) + HD)
                    if n >= 2:
                        pe.wait_ge(S("fsc_free"), n - 1)
                    for t in range(TT):
                        ins = pe.matmul(bank[n % 2][:, P * t:P * t + P + P * t], fq[h, n // 2, t * P:(t + 1) * P],
                                        fq[h, KD + n // 2, 0:P * (t + 1)], start=True, stop=True)
                    ins.then_inc(S("fsc_full"), 1)
                if 1 <= n <= N_FOX:
                    b = (n - 1) % 2
                    pe.wait_ge(S("fp_ok"), n)
                    if n >= 3:
                        pe.wait_ge(S("fpt_free"), n - 2)
                    for a in range(3):
                        ins = pe.transpose(bank[2 + b][:, a * P:(a + 1) * P], fat_p[:, b, a * P:(a + 1) * P], C("ident"))
                    ins.then_inc(S("fpt_full"), 1)
                if n >= 2:
                    h, b = n - 2, n % 2
                    pe.wait_ge(S("fpt_free"), n - 1)
                    pair = h // 2
                    if h % 2 == 0 and pair >= 2:
                        pe.wait_ge(S("fo_free"), pair - 1)
                    o = bank[4][HD * (h % 2):HD * (h % 2) + HD, (pair % 2) * T:(pair % 2) * T + T]
                    pe.matmul(o, f_v[:, 0, h * HD:(h + 1) * HD], fat_t[:, b, 0:T], start=True, stop=False)
                    pe.matmul(o[:, P:T], f_v[:, 1, h * HD:(h + 1) * HD], fat_t[:, b, T:T + P], start=False, stop=True)\
                        .then_inc(S("fpv_done"), 1)

            fox_schedule(fox_slot,
                         lambda j: unit_channels(group_begin(f"c{12 + j}"), unit_ready(FULL[f"c{12 + j}"][1] - 1)))
            square("c_out", f_o, "fo_free", KD)
            norm_sums(12, "n12")
            ffn(3, 13)


INPUTS = ["x_t", "stream", "small_1", "cmp_w1", "small_2", "consts"]


def kernel(**inputs):
    import concourse.bacc as bacc
    from concourse.bass_utils import run_bass_kernel_spmd
    nc = bacc.Bacc("TRN2", target_bir_lowering=False, num_devices=1)
    given = lay_out(inputs)
    arrays, args = {}, []
    for name in INPUTS:
        a = given[name]
        arrays[f"in_{name}"] = a
        args.append(nc.dram_tensor(f"in_{name}", a.shape, mybir.dt.from_np(a.dtype), kind="ExternalInput").ap())
    out = nc.dram_tensor("out_x_t", (D, T), FP32, kind="ExternalOutput").ap()
    build(nc, *args, out)
    result = run_bass_kernel_spmd(nc, [arrays], core_ids=[0])
    return np.ascontiguousarray(result.results[0]["out_x_t"].T)[None]
```

```python
import numpy as np
import concourse.bass as bass
from concourse import mybir
from contextlib import ExitStack

FP32 = mybir.dt.float32
BF16 = mybir.dt.bfloat16
F32R = mybir.dt.float32r
ACT = mybir.ActivationFunctionType
ALU = mybir.AluOpType
AX = mybir.AxisListType

P = 128
D = 1024
T = 256
KD = D // P
MIX = 512
MT = MIX // P
TT = T // P
UNIT = 2048
UC = UNIT // KD
SPLIT = 3
GATED_32 = 6144
RING = 6
N_EXP = 16
D_EXP = 512
D_FF = 2816
N_HEADS, N_TYPES = 8, 3
N_CMP = 15
N_FOX = 16
N_RW = 8
HD = 64
CONV_A = 4
CONV_B = 31
WINDOWS = (2, 4, 8, 16)
NEG = -1e30
EPS = 1e-6
GN_EPS = 1e-5 * HD
LN_EPS = 1e-5
ARENA = 26520
SIDES_2 = ["n3", "n4", "n5", "gu0", "gu1", "kk0", "kk1", "bo0", "bo1", "conv", "ln1", "ln2", "n6", "n7", "n8", "n9", "n10", "n11"]\
    + [f"hs{n}" for n in range(8)] + ["f"] + [f"cb{n}" for n in range(8)] + ["n12", "n13", "n14"]
SCALE = HD ** -0.5
MOE_STEPS = N_EXP * D_EXP // UC
FFN_STEPS = D_FF // UC


def offsets(parts):
    at, table = 0, {}
    for name, width in parts:
        table[name] = (at, width)
        at += width
    return table, at


SMALL_1 = [("n1", KD), ("n2", KD), ("nf", KD), ("gm_g", MT), ("conv_w", CONV_A * MT), ("conv_b", MT),
           ("ba", MT), ("bx", MT), ("lam", MT), ("pool_s", MT), ("pe", 64), ("gm_wT", MIX), ("wa", MIX),
           ("wx", MIX), ("pool_w", MIX), ("cw2", 128), ("w_gate", KD * 24), ("w_route", KD * 20),
           ("gm_b", MIX), ("b_route", 20)]
SMALL_2 = [("n", 12 * KD), ("mu", 14), ("d_base", MT), ("i_base", MT), ("k_k", MT), ("k_a", MT),
           ("r_k", MT), ("lnx_g", MT), ("lnx_b", MT), ("conv_w", CONV_B * MT), ("conv_b", MT),
           ("ln_g", MT), ("ln_b", MT), ("qg", 1), ("kg", 1), ("fb", 1), ("lora", MIX), ("gate_up", MIX),
           ("w_f", KD * N_FOX)]
LEVELS = [1 << n for n in range(7)]
N_INV = 4 * (len(LEVELS) - 1)
CONSTS = [("ident", P), ("mask3", 3 * P), ("head1", P), ("cmp_add", 2 * 16), ("cmp_01", 2 * 16),
          ("level", len(LEVELS) * P), ("s_le_t", P), ("gram", 4 * P), ("level_t", P), ("pool_n", 4 * 16),
          ("keep", T), ("ones", P), ("eps", 4)]
OFF_1, W_1 = offsets(SMALL_1)
OFF_2, W_2 = offsets(SMALL_2)
OFF_C, W_C = offsets(CONSTS)


def constants():
    c = np.zeros((P, W_C), np.float32)

    def put(name, value):
        a, w = OFF_C[name]
        c[:, a:a + w] = np.asarray(value, np.float32).reshape(P, w)
    i = np.arange(P)
    put("ident", np.eye(P))
    diag = np.where(i[None, :] <= i[:, None], 0.0, NEG)
    put("mask3", np.concatenate([diag, np.zeros((P, P)), diag], 1))
    put("head1", i[:, None] // HD == i[None, :] // HD)
    t = (np.arange(TT)[None, :, None] * P + i[:, None, None])
    seen = (np.arange(16)[None, None, :] * 16 + 31 <= t) & (np.arange(16) < N_CMP)
    put("cmp_add", np.where(seen, 0.0, NEG))
    put("cmp_01", seen)
    put("level", np.stack([(i[:, None] // (2 * b) == i[None, :] // (2 * b)) & (i[:, None] // b < i[None, :] // b)
                           for b in LEVELS], 1))
    put("s_le_t", i[:, None] <= i[None, :])
    first = (i[:, None] // 2 == i[None, :] // 2) & (i[:, None] < i[None, :])
    put("gram", np.stack([i[:, None] < i[None, :], i[:, None] <= i[None, :], -1.0 * first, -1.0 * (i[:, None] <= i[None, :])], 1))
    put("level_t", -1.0 * first.T)
    put("pool_n", np.broadcast_to(np.stack([1.0 / np.minimum(np.arange(16) + 1, w) for w in WINDOWS])[None], (P, 4, 16)))
    put("keep", np.broadcast_to((np.arange(T) % P != 0)[None], (P, T)))
    put("ones", np.ones((P, P)))
    put("eps", np.broadcast_to(np.array([EPS, GN_EPS, LN_EPS, 0.0])[None], (P, 4)))
    return c


PROJ_SPLIT = 15
C_SPLIT = 12
CONV_V = 2
DIAG_RUNS = [6, 6, 8, 6, 6, 14, 16]
DIAGS = 8
SPLIT_AREA = 2 * SPLIT * UNIT + 2 * KD * T
PROJ_1 = 31
BRANCH = 8
SQUARE = 4
PROJ_AB = 11
PROJ_C = 16
AB_ORDER = [6, 0, 1, 2, 3, 4, 5, 9, 10, 7, 8]


def column_units(w):
    return w.reshape(KD, P, -1, UC).transpose(2, 1, 0, 3).reshape(-1, P, UNIT)


def row_units(w):
    return w.reshape(-1, 2, P, D).transpose(0, 2, 1, 3).reshape(-1, P, UNIT)


def gated_units(gate, up, down):
    g, u, d = column_units(gate), column_units(up), row_units(down)
    order = [g[0], u[0]]
    for n in range(1, len(g)):
        order += [g[n], u[n], d[n - 1]]
    return order + [d[-1]]


def cols(v):
    return v.reshape(-1, P).T


def pack(parts, given):
    out = np.zeros((P, sum(w for _, w in parts)), np.float32)
    table, _ = offsets(parts)
    for name, (a, w) in table.items():
        v = given[name]
        v = v.reshape(v.shape[0], w)
        out[:v.shape[0], a:a + w] = v
    return out


def block_diagonal(w):
    out = np.zeros((P, MT, P), np.float32)
    for b in range(8):
        h = b % 2
        out[HD * h:HD * h + HD, b // 2, HD * h:HD * h + HD] = w[b]
    return out


def lay_out(a):
    a = {k: np.asarray(v) for k, v in a.items()}
    w_in = a["w_in"][0]
    first = np.concatenate([w_in[:, :3328], w_in[:, 3352:]], 1)
    units = list(column_units(first))
    wb = a["w_branch"][0]
    for n in range(4):
        units += list(wb[n].reshape(MT, P, 2, 512).transpose(2, 1, 0, 3).reshape(2, P, UNIT))
    units += list(column_units(a["w_out"][0]))
    gate = np.concatenate(list(a["moe_w_gate"][0]), 1)
    up = np.concatenate(list(a["moe_w_up"][0]), 1)
    down = a["moe_w_down"][0].reshape(-1, D)
    units += gated_units(gate, up, down)
    fg, fu, fd = a["ffn_w_gate_2"], a["ffn_w_up_2"], a["ffn_w_down_2"]
    units += gated_units(fg[0, 0], fu[0, 0], fd[0, 0])
    ab = column_units(a["a_w_in_2"][0])
    units += [ab[n] for n in AB_ORDER]
    units += list(column_units(a["ab_w_out_2"][0]))
    units += gated_units(fg[0, 1], fu[0, 1], fd[0, 1])
    units += gated_units(fg[1, 0], fu[1, 0], fd[1, 0])
    units += list(column_units(a["c_w_in_2"][0][:, :4096]))
    units += list(column_units(a["c_w_out_2"][0]))
    units += gated_units(fg[1, 1], fu[1, 1], fd[1, 1])
    pe = a["cmp_pe"][0].transpose(0, 2, 1)
    rows = lambda w: w.reshape(KD, P, -1).transpose(1, 0, 2)
    every = lambda v: np.broadcast_to(v.reshape(1, -1), (P, v.size))
    small_1 = pack(SMALL_1, {
        "n1": cols(a["norm1_g"][0]), "n2": cols(a["norm2_g"][0]), "nf": cols(a["final_norm_g"]),
        "gm_g": cols(a["gm_norm_g"][0]), "conv_w": cols(a["conv_w"][0].reshape(-1)), "conv_b": cols(a["conv_b"][0]),
        "ba": cols(a["lru_ba"][0]), "bx": cols(a["lru_bx"][0]), "lam": cols(a["lru_lambda"][0]),
        "pool_s": cols(a["pool_scale"][0]), "pe": np.concatenate([pe, pe], 1).transpose(1, 0, 2),
        "gm_wT": a["gm_ws"][0].transpose(2, 0, 1), "wa": block_diagonal(a["lru_wa"][0]),
        "wx": block_diagonal(a["lru_wx"][0]), "pool_w": a["pool_w"][0].transpose(1, 0, 2),
        "cw2": a["cmp_w2"][0].transpose(1, 2, 0, 3).reshape(P, 128), "w_gate": rows(w_in[:, 3328:3352]),
        "w_route": rows(np.concatenate([a["router_w_group"][0], a["router_w_expert"][0]], 1)),
        "gm_b": every(a["gm_b"][0]),
        "b_route": every(np.concatenate([a["router_b_group"][0], a["router_b_expert"][0]]))})
    cmp_w1 = a["cmp_w1"][0].reshape(2, 2, 32, HD, HD).transpose(1, 3, 0, 2, 4).reshape(P, 2 * 32 * HD)
    two = lambda v: np.concatenate([v, v]).reshape(P, 1)
    small_2 = pack(SMALL_2, {
        "n": cols(a["norm_gains_2"].reshape(-1)), "mu": cols(a["a_shift_mu_2"][0]),
        "d_base": cols(a["a_decay_base_2"][0]), "i_base": cols(a["a_iclr_base_2"][0]),
        "k_k": cols(a["a_k_k_2"][0]), "k_a": cols(a["a_k_a_2"][0]), "r_k": cols(a["a_r_k_2"][0].reshape(-1)),
        "lnx_g": cols(a["a_lnx_g_2"][0]), "lnx_b": cols(a["a_lnx_b_2"][0]),
        "conv_w": cols(a["b_conv_w_2"][0].reshape(-1)), "conv_b": cols(a["b_conv_b_2"][0]),
        "ln_g": cols(a["b_ln_g_2"][0]), "ln_b": cols(a["b_ln_b_2"][0]), "qg": two(a["c_q_norm_g_2"][0]),
        "kg": two(a["c_k_norm_g_2"][0]), "fb": a["c_forget_bias_2"][0].reshape(N_FOX, 1),
        "lora": np.concatenate([a["a_decay_up_2"][0], a["a_iclr_up_2"][0]], 0), "gate_up": a["a_gate_up_2"][0],
        "w_f": rows(a["c_w_in_2"][0][:, 4096:])})
    return {"x_t": np.ascontiguousarray(a["x"][0].T), "stream": np.stack(units), "small_1": small_1,
            "cmp_w1": np.ascontiguousarray(cmp_w1), "small_2": small_2, "consts": constants()}


def build(nc, x_t, stream, small_1, cmp_w1, small_2, consts, out):
    n_units = stream.shape[0]
    assert n_units % RING == 0
    with ExitStack() as ctx:
        def sb(name, shape, dt=FP32):
            return ctx.enter_context(nc.sbuf_tensor(name, shape, dt))

        sems = {}

        def S(name):
            if name not in sems:
                sems[name] = ctx.enter_context(nc.semaphore("s_" + name))
            return sems[name]

        ring = sb("ring", [P, RING, UNIT])
        con = sb("con", [P, W_C])
        sm1 = sb("sm1", [P, W_1])
        sm2 = sb("sm2", [P, W_2])
        X = sb("X", [P, KD, T])
        H = sb("H", [P, KD, T])
        SQ = sb("SQ", [P, KD, T])
        rstd = sb("rstd", [P, T])
        zeros = sb("zeros", [P, 512], BF16)
        tiny = sb("tiny", [P, 256])
        with nc.sbuf_tensor("arena", [P, ARENA], FP32) as arena:
            pass
        w_hi = sb("w_hi", [P, SPLIT, UNIT], F32R)
        w_lo = sb("w_lo", [P, SPLIT, UNIT], F32R)
        h_hi = sb("h_hi", [P, KD, T], F32R)
        h_lo = sb("h_lo", [P, KD, T], F32R)
        hid_hi = sb("hid_hi", [P, 2, 2, T], F32R)
        hid_lo = sb("hid_lo", [P, 2, 2, T], F32R)
        gated_32 = sb("gated_32", [P, GATED_32])
        bank = [ctx.enter_context(nc.psum_tensor(f"bank{n}", [P, 512], FP32)) for n in range(8)]

        def C(name, *dims):
            a, w = OFF_C[name]
            return con[:, a:a + w]

        def P1(name):
            a, w = OFF_1[name]
            return sm1[:, a:a + w]

        def P2(name):
            a, w = OFF_2[name]
            return sm2[:, a:a + w]

        def tiles(ap, n):
            return ap.rearrange("p (m t) -> p m t", m=n)

        class Carve:

            def __init__(self, of, size, at=0):
                self.of, self.size, self.at = of, size, at

            def __call__(self, width):
                a = self.at
                self.at += width
                assert self.at <= self.size, self.at
                return self.of[:, a:a + width]

        cut = Carve(arena, ARENA)
        yc = tiles(cut(MT * T), MT)
        yd = tiles(cut(MT * T), MT)
        mg = tiles(cut(4 * KD * T), 4 * KD)
        after_mg = cut.at
        cw1_flat = cut(2 * 32 * HD)
        cw1 = cw1_flat.rearrange("p (c l e) -> p c l e", c=2, l=32)
        xc, th_r, th_i, e_b = (tiles(cw1_flat[:, n * 1024:(n + 1) * 1024], MT) for n in range(4))
        att_t = tiles(cut(2 * 384), 2)
        p_cmp = cut(2 * P)
        late = arena[:, after_mg - 16 * T:after_mg]
        win_a, win_b = (tiles(late[:, n * MT * (16 + T):(n + 1) * MT * (16 + T)], MT) for n in range(2))
        hid_c = cut(2 * 16).rearrange("p (c n) -> p c n", c=2)
        k_c = cut(2 * 16).rearrange("p (g n) -> p g n", g=2)
        v_c = cut(2 * HD)
        first_cols = tiles(cut(4 * 16), 4)
        assert cut.at <= SPLIT_AREA
        cut = Carve(arena, ARENA, SPLIT_AREA)
        u = tiles(cut(MT * T), MT)
        gate = tiles(cut(MT * T), MT)
        q1 = tiles(cut(MT * T), MT)
        xd = tiles(cut(MT * (16 + T)), MT)
        rec = tiles(cut(MT * 260), MT)
        kvc_flat = cut(2 * T)
        kvc = tiles(kvc_flat, 2)
        kd = tiles(cut(4 * T), 4)
        vn = tiles(cut(2 * TT * P), 2)
        v1 = tiles(cut(TT * MIX), TT)
        gates3 = tiles(cut(TT * 24), TT)
        att_sp = cut(4 * 384)
        att_s = tiles(att_sp[:, 0:768], 2)
        att_p = [att_sp[:, 768:1152], att_sp[:, 1152:1536], kvc_flat[:, 0:384]]
        keys_2 = tiles(att_sp[:, 1024:1536], 2)
        kpe = att_sp[:, 0:2 * 32 * 16].rearrange("p (c l n) -> p c l n", c=2, l=32)
        v_junk = SQ[:, 4:8, :].rearrange("p k t -> p (k t)")
        cut = Carve(gated_32, GATED_32)
        sil = [tiles(cut(2 * T), 2) for _ in range(2)]
        hid = tiles(cut(2 * T), 2)
        scratch = (sil[0], sil[1])
        comb_all = tiles(cut(N_EXP * T), N_EXP)
        route = cut(512)
        route_pick = tiles(route[:, 112:144], 2)
        gsum, rt_w2 = route[:, 56:64], route[:, 286:288]

        cut = Carve(arena, ARENA)
        kkt, qt, kh, bh = (tiles(cut(MT * T), MT) for _ in range(4))
        bon, gup = (tiles(cut(MT * T), MT) for _ in range(2))
        glu = tiles(cut(MT * 288), MT)
        cacc, ctmp = (tiles(cut(MT * T), MT) for _ in range(2))
        diag = tiles(ctmp.rearrange("p m t -> p (m t)"), DIAGS)
        phase = cut.at
        pr = tiles(cut(14 * 260), 14)
        pp = tiles(cut(14 * T), 14)
        cv, cg = (tiles(cut(MT * T), MT) for _ in range(2))
        lw, cum_l, rate, e_l, e_p, e_n, kk = (tiles(cut(MT * T), MT) for _ in range(7))
        cut = Carve(arena, ARENA, phase)
        N_MAT = 2 * N_RW
        gram = cut(N_MAT * 4 * P).rearrange("p (i a t) -> p i a t", i=N_MAT, a=4)
        mat_w_at = cut.at + N_MAT * P
        mat_y, mat_w, mat_m = (tiles(cut(N_MAT * P), N_MAT) for _ in range(3))
        mat_q = tiles(cut(2 * 4 * P), 2)
        rw_r, rw_u = mat_q[:, 0, :], mat_q[:, 1, :]
        rw_y = tiles(cut(TT * MIX), TT)
        sq_flat = SQ[:, :, :].rearrange("p k t -> p (k t)")
        v_tok = tiles(sq_flat[:, 0:2 * MIX], TT)
        kh_tok, bh_tok = sq_flat[:, 2 * MIX:3 * MIX], sq_flat[:, 3 * MIX:4 * MIX]
        state = tiles(cut(MIX), MT)
        cut = Carve(arena, ARENA)
        f_gate = tiles(cut(KD * T), KD)
        f_cum = tiles(cut(N_FOX * T), N_FOX)
        f_mc = tiles(cut(2 * 384), 2)
        fat_s, fat_t = (tiles(cut(2 * 384), 2) for _ in range(2))
        fat_p = tiles(cut(3 * 384), 3)
        f_o = tiles(cut(KD * T), KD)
        assert cut.at <= SPLIT_AREA
        cut = Carve(arena, ARENA, SPLIT_AREA)
        fq = tiles(cut(2 * KD * T), 2 * KD)
        f_sq, f_rs = (tiles(cut(2 * 2 * T), 2) for _ in range(2))
        f_v = tiles(cut(TT * D), TT)
        fz, fa, fe, fl, fc, fm = (cut(T) for _ in range(6))

        def small(at, width):
            return tiny[:, at:at + width]
        v_ss, v_rstd = small(0, 2), small(4, 2)
        neg_max, row_sum, inv_sum = small(8, 4), small(12, 4), small(16, 4)
        hb_a, hb_x, lam_t, lam_z, lam_l, lam_c = (small(20 + 4 * n, 4) for n in range(6))
        lam_d, lam_e = small(44, 4), small(48, 4)
        hd_base, hi_base, e_last = small(52, 4), small(56, 4), small(60, 4)
        gn_sum, gn_rs = small(64, 16), small(80, 16)
        e_mean = arena[:, mat_w_at:mat_w_at + T]
        half_gain, qg8 = small(96, KD), small(104, 1)

        GROUPS = (["u0", "u1", "v0", "v1", "ga0", "ga1", "re0", "re1", "q0", "q1", "kvc", "ks", "vs", "kks", "kw", "vw", "kkw",
                   "g24", "xd0", "xd1"] + [f"mg{n}" for n in range(16)])
        GI = {name: n for n, name in enumerate(GROUPS)}
        PARTS = ["ks", "kks", "kw", "kkw", "g24"]
        FULL, unit = {}, 0
        for name in GROUPS:
            if name in PARTS:
                FULL[name] = ("part_full", PARTS.index(name) + 1)
            else:
                unit += 1
                FULL[name] = ("unit_used", unit)
        assert unit == PROJ_1
        for kind, order in (("ab", AB_ORDER), ("c", range(PROJ_C))):
            for place, n in enumerate(order):
                GI[f"{kind}{n}"] = len(GI)
                FULL[f"{kind}{n}"] = (kind, place + 1)
        SIDES = ["norm0", "gm0", "gm1", "hid", "kvc2", "wa0", "wa1", "wx0", "wx1", "po0", "po1",
                 "norm1", "route"] + [f"comb{n}" for n in range(8)] + ["norm2"] + SIDES_2
        SI = {name: n for n, name in enumerate(SIDES)}
        N_SLOTS = N_HEADS * N_TYPES
        D_UNITS = {"proj": 0, "branch": PROJ_1, "w_out": PROJ_1 + BRANCH, "moe": PROJ_1 + BRANCH + SQUARE}
        at = D_UNITS["moe"] + 3 * MOE_STEPS
        for name, size in (("ffn0", 3 * FFN_STEPS), ("ab", PROJ_AB), ("ab_out", SQUARE), ("ffn1", 3 * FFN_STEPS),
                           ("ffn2", 3 * FFN_STEPS), ("c", PROJ_C), ("c_out", SQUARE), ("ffn3", 3 * FFN_STEPS)):
            D_UNITS[name] = at
            at += size
        assert at == n_units
        for name in GI:
            if FULL[name][0] in ("ab", "c"):
                FULL[name] = ("unit_used", D_UNITS[FULL[name][0]] + FULL[name][1])
        STEP0, SPLIT0, NTH, steps, n_split = {}, {}, {}, 0, 0
        for name, phase_steps, units in (("proj", 0, PROJ_SPLIT), ("moe", MOE_STEPS, 3 * MOE_STEPS),
                                         ("ffn0", FFN_STEPS, 3 * FFN_STEPS), ("ffn1", FFN_STEPS, 3 * FFN_STEPS),
                                         ("ffn2", FFN_STEPS, 3 * FFN_STEPS), ("c", 0, C_SPLIT),
                                         ("ffn3", FFN_STEPS, 3 * FFN_STEPS)):
            NTH[name], STEP0[name], SPLIT0[name] = len(NTH), steps, n_split
            steps, n_split = steps + phase_steps, n_split + units
        SQ0 = {"w_out": 0, "ab_out": SQUARE, "c_out": 2 * SQUARE}

        def fox_schedule(run_slot, run_gate):
            for n in range(N_FOX + 3):
                if n < 8:
                    run_gate(n // 2, n % 2)
                run_slot(n)

        def up_count(name, s):
            return s * 3 + (D_UNITS[name] + 1)

        def split_order(name, steps, eng, split, use):
            def trip(used, first, static, i=None, half=None):
                split(first, static, i)
                use(used, static % 2, half)
                split(first + 1, static + 1, i)
                split(first + 2, static + 2, i)
            trip(0, 2, 2)
            trip(1, 5, 5)
            trips = (steps - 3) // 2
            with eng.Fori(0, trips) as i:
                trip(i * 2 + 2, i * 6 + 8, 8, i, i + 1)
                trip(i * 2 + 3, i * 6 + 11, 11, i, i + 1)
            if steps % 2 == 0:
                trip(steps - 2, 3 * steps - 4, 3 * steps - 4)
            use(steps - 1, (steps - 1) % 2)
            split(3 * steps - 1, 3 * steps - 1)

        def schedule(run_slot, run_mg):
            for j in range(16):
                for half in range(2):
                    run_mg(j, half)
                    if j >= 3:
                        run_slot(2 * (j - 3) + half)
            for n in range(26, N_SLOTS + 3):
                run_slot(n)

        block = ctx.enter_context(nc.Block())

        @block.sync
        def _(sp):
            sp.dma_start(X[:, :, :], x_t.rearrange("(k p) t -> p k t", p=P)).then_inc(S("x"), 16)
            def load(s, unit):
                sp.dma_start(ring[:, s, :], unit.rearrange("a p n -> (a p) n")).then_inc(S(f"unit{s}"), 16)
            load(0, stream[0:1, :, :])
            sp.dma_start(con[:, :], consts).then_inc(S("con"), 16)
            sp.dma_start(sm1[:, :], small_1).then_inc(S("sm1"), 16)
            for s in range(1, RING):
                load(s, stream[s:s + 1, :, :])
            sp.dma_start(sm2[:, :], small_2).then_inc(S("sm2"), 16)
            with sp.Fori(0, n_units // RING - 1) as i:
                for s in range(RING):
                    sp.wait_ge(S("unit_used"), i * RING + s + 1)
                    load(s, stream[bass.ds(i * RING + (RING + s), 1), :, :])
            sp.wait_ge(S("out"), 1)
            sp.dma_start(out.rearrange("(k p) t -> p k t", p=P), X[:, :, :]).then_inc(S("stored"), 16)
            sp.wait_ge(S("stored"), 16)

        @block.gpsimd
        def _(pool):
            chain = [0]

            def link(ins):
                chain[0] += 1
                ins.then_inc(S("pool_chain"), 1)
                pool.wait_ge(S("pool_chain"), chain[0])
            link(pool.memset(zeros[:, :], 0.0))
            link(pool.memset(xd[:, :, 0:16], 0.0))
            pool.memset(rec[:, :, 0:3], 0.0).then_inc(S("zeroed"), 1)
            pool.wait_ge(S("unit_used"), PROJ_SPLIT)
            for part in (win_a[:, :, 0:16], win_b[:, :, 0:16], v_c):
                link(pool.memset(part, 0.0))
            pool.memset(p_cmp, 0.0).then_inc(S("zeroed_cmp"), 1)
            pool.wait_ge(S("zeroed"), 1)
            pool.wait_ge(S("con"), 16)
            pool.wait_ge(S("proj_free"), GI["xd1"] + 1)
            link(pool.tensor_tensor(win_a[:, :, 1:16 + T], xd[:, :, 1:16 + T], xd[:, :, 0:15 + T], ALU.add))
            src, dst = win_a, win_b
            for m, w in enumerate(WINDOWS):
                if m < MT - 1:
                    link(pool.tensor_tensor(dst[:, m + 1:, w:16 + T], src[:, m + 1:, w:16 + T],
                                            src[:, m + 1:, 0:16 + T - w], ALU.add))
                first = C("pool_n").rearrange("p (m t) -> p m t", m=4)[:, m, :]
                link(pool.tensor_tensor(first_cols[:, m, :], src[:, m, 16:32], first, ALU.mult))
                link(pool.tensor_scalar(src[:, m, 16:16 + T], src[:, m, 16:16 + T], 1.0 / w, None, ALU.mult))
                link(pool.tensor_copy(src[:, m, 16:32], first_cols[:, m, :]))
                pool.tensor_tensor(xd[:, m, 16:16 + T], src[:, m, 16:16 + T], xd[:, m, 16:16 + T], ALU.subtract)\
                    .then_inc(S("pooled"), 1)
                src, dst = dst, src

            pool.wait_ge(S("added"), 4)
            link(pool.memset(pr[:, :, 0:1], 0.0))
            pool.memset(glu[:, :, 0:CONV_B - 1], 0.0).then_inc(S("zeroed_2"), 1)
            for h in range(N_FOX):
                b = h % 2
                pool.wait_ge(S("side_free"), SI[f"cb{h // 2}"] + 1)
                if h >= 2:
                    pool.wait_ge(S("fsc_free"), h - 1)
                m = C("mask3")
                pool.tensor_tensor(f_mc[:, b, 0:P], m[:, 0:P], f_cum[:, h, 0:P], ALU.add)
                pool.tensor_tensor(f_mc[:, b, P:3 * P], m[:, P:3 * P], f_cum[:, h, :], ALU.add)\
                    .then_inc(S("mc"), 1)

        @block.scalar
        def _(act):
            chain = [0]

            def link(ins):
                chain[0] += 1
                ins.then_inc(S("act_chain"), 1)
                act.wait_ge(S("act_chain"), chain[0])

            def squares(n):
                for b in range(4):
                    act.activation(SQ[:, 2 * b:2 * b + 2, :], X[:, 2 * b:2 * b + 2, :], ACT.Square)\
                       .then_inc(S("squares"), 1)

            def evac(name, dst, func, scale=1.0):
                n = GI[name]
                if name in GROUPS and FULL[name][0] == "unit_used":
                    split_ahead("proj", FULL[name][1] - 1, PROJ_SPLIT)
                act.wait_ge(S(FULL[name][0]), FULL[name][1])
                src = bank[5 + n % 2][:, 0:dst.free_size()]
                if len(dst.shape) == 3:
                    src = tiles(src, dst.shape[1])
                act.activation(dst, src, func, scale=scale).then_inc(S("proj_free"), 1)

            def root_mean(name, scale=1.0 / D, eps=0, width=T):
                act.wait_ge(S("side_full"), SI[name] + 1)
                act.activation(rstd[:, 0:width], bank[7][:, 0:width], ACT.Sqrt, bias=C("eps")[:, eps:eps + 1], scale=scale)\
                   .then_inc(S("side_free"), 1)

            def split(name, n, static, i=None):
                unit = D_UNITS[name] + static
                lap = 16 * (unit // RING + 1)
                act.wait_ge(S(f"unit{unit % RING}"), lap if i is None else i * 16 + lap)
                if unit >= SPLIT:
                    act.wait_ge(S("unit_used"), n + (D_UNITS[name] - SPLIT + 1))
                act.activation(w_hi[:, unit % SPLIT, :], ring[:, unit % RING, :], ACT.Copy).then_inc(S("w_hi"), 1)

            def split_first(name):
                for n in range(2):
                    split(name, n, n)

            def split_ahead(name, n, units):
                if n + 2 < units:
                    split(name, n + 2, n + 2)

            def h_rounded(n):
                for k in range(KD):
                    act.wait_ge(S("normed"), n * KD + k + 1)
                    act.activation(h_hi[:, k, :], H[:, k, :], ACT.Copy).then_inc(S("h_hi"), 1)

            split("proj", 0, 0)
            act.wait_ge(S("x"), 16)
            squares(0)
            split("proj", 1, 1)
            act.wait_ge(S("con"), 16)
            root_mean("norm0")
            h_rounded(0)
            gelu = ACT.Gelu_apprx_tanh
            for n in range(2):
                evac(f"u{n}", u[:, 2 * n:2 * n + 2, :], gelu)
            for n in range(2):
                evac(f"v{n}", v1[:, :, n * UC:(n + 1) * UC], gelu)
            for n in range(2):
                evac(f"ga{n}", gate[:, 2 * n:2 * n + 2, :], gelu)
            act.wait_ge(S("zeroed"), 1)
            for n in range(2):
                evac(f"re{n}", rec[:, 2 * n:2 * n + 2, 3:3 + T], ACT.Copy)
            for n in range(2):
                evac(f"q{n}", q1[:, 2 * n:2 * n + 2, :], ACT.Copy)
            evac("kvc", kvc[:, :, :], ACT.Copy)
            for n, kind in enumerate("sw"):
                evac(f"k{kind}", keys_2[:, n, :], ACT.Copy)
                evac(f"v{kind}", vn[:, n, :].rearrange("p (t d) -> p t d", t=TT), ACT.Copy)
                evac(f"kk{kind}", kd[:, 2 * n:2 * n + 2, :], ACT.Copy)
            evac("g24", gates3[:, :, :], ACT.Tanh, scale=0.5)
            for n in range(2):
                evac(f"xd{n}", xd[:, 2 * n:2 * n + 2, 16:16 + T], ACT.Copy)
            act.dma_start(cw1_flat, cmp_w1).then_inc(S("cw1"), 16)
            act.wait_ge(S("proj_free"), GI["v1"] + 1)
            for t in range(TT):
                link(act.activation(tiles(v_junk, 2)[:, t, :], v1[:, t, :], ACT.Square, accum_out=v_ss[:, t:t + 1]))
            act.wait_ge(S("con"), 16)
            act.activation(v_rstd, v_ss, ACT.Sqrt, bias=C("eps")[:, 0:1], scale=1.0 / MIX).then_inc(S("v_sums"), 1)

            def exp(n):
                act.wait_ge(S("max_ok"), n + 1)
                b = n % 2
                if n >= 3:
                    act.wait_ge(S("pt_full"), n - 2)
                for t in range(TT):
                    if n % 3 == 0:
                        dst, src = p_cmp[:, t * P:t * P + N_CMP], att_s[:, b, t * 16:t * 16 + N_CMP]
                    else:
                        a, z = (0, P) if t == 0 else (P, 3 * P)
                        dst, src = att_p[n % 3][:, a:z], att_s[:, b, a:z]
                    act.activation(dst, src, ACT.Exp, bias=neg_max[:, 2 * b + t:2 * b + t + 1],
                                   accum_out=row_sum[:, 2 * b + t:2 * b + t + 1]).then_inc(S("exp_done"), 1)

            def weights_out(n):
                act.wait_ge(S("pt_full"), n + 1)
                if n >= 2:
                    act.wait_ge(S("pv_done"), n - 1)
                w = 2 * P if n % 3 == 0 else 3 * P
                act.activation(att_t[:, n % 2, 0:w], bank[2 + n % 2][:, 0:w], ACT.Copy).then_inc(S("pt_free"), 1)

            def run_mg(j, half):
                if not half:
                    return
                if j == 8:
                    act.wait_ge(S("pooled"), MT)
                evac(f"mg{j}", mg[:, 2 * j:2 * j + 2, :], ACT.Tanh, scale=0.5)
                if j == 1:
                    act.wait_ge(S("side_full"), SI["hid"] + 1)
                    act.activation(hid_c[:, :, 0:N_CMP], tiles(bank[7][:, 0:32], 2)[:, :, 0:N_CMP], gelu).then_inc(S("side_free"), 1)
                if j == 2:
                    act.wait_ge(S("lam_abs"), 1)
                    act.activation(lam_z, lam_t, ACT.Exp, scale=-1.0).then_inc(S("lam_z"), 1)
                    act.wait_ge(S("lam_u"), 1)
                    act.activation(lam_l, lam_t, ACT.Ln).then_inc(S("lam_l"), 1)
                if j in (7, 8, 9, 10):
                    name, dst, bias = (("wa0", th_r, hb_a), ("wa1", th_r, hb_a), ("wx0", th_i, hb_x),
                                       ("wx1", th_i, hb_x))[j - 7]
                    act.wait_ge(S("side_full"), SI[name] + 1)
                    for t in range(2):
                        m = 2 * (j % 2 == 0) + t
                        ins = act.activation(dst[:, m, :], bank[7][:, t * T:(t + 1) * T], ACT.Tanh,
                                             bias=bias[:, m:m + 1], scale=0.5)
                    ins.then_inc(S("side_free"), 1)
                if j in (11, 12):
                    name = f"po{j - 11}"
                    act.wait_ge(S("side_full"), SI[name] + 1)
                    for t in range(2):
                        m = 2 * (j - 11) + t
                        ins = act.activation(yd[:, m, :], bank[7][:, t * T:(t + 1) * T], ACT.Copy,
                                             scale=P1("pool_s")[:, m:m + 1])
                    ins.then_inc(S("side_free"), 1)
                if j == 13:
                    act.wait_ge(S("log_a"), 1)
                    act.activation(th_i[:, :, :], th_r[:, :, :], ACT.Tanh).then_inc(S("tanh_l"), 1)
                    act.activation(th_r[:, :, :], th_r[:, :, :], ACT.Exp).then_inc(S("decay"), 1)
                if j == 15:
                    act.wait_ge(S("e_ok"), 1)
                    act.activation(e_b[:, :, :], e_b[:, :, :], ACT.Sqrt).then_inc(S("e_root"), 1)

            def run_slot(n):
                if n < N_SLOTS:
                    exp(n)
                if 2 <= n < N_SLOTS + 2:
                    weights_out(n - 2)

            schedule(run_slot, run_mg)

            act.wait_ge(S("merged"), 1)
            split_first("moe")
            act.wait_ge(S("res_done"), SQ0["w_out"] + SQUARE)
            squares(1)
            root_mean("norm1")
            h_rounded(1)

            act.wait_ge(S("rt_1"), 1)
            act.activation(gsum, gsum, ACT.Exp).then_inc(S("rt_e"), 1)
            act.wait_ge(S("rt_2"), 1)
            act.activation(rt_w2, rt_w2, ACT.Exp).then_inc(S("rt_e"), 1)

            def silu_steps(name, steps):
                u0 = D_UNITS[name]

                def use(s, parity, half=None):
                    act.wait_ge(S("unit_used"), u0 + 2 if isinstance(s, int) and s == 0 else s * 3 + (u0 + 1))
                    act.activation(sil[parity], tiles(bank[4 + 2 * parity][:, :], 2), ACT.Silu)\
                       .then_inc(S("silu_done"), 1)

                split_order(name, steps, act, lambda n, static, i=None: split(name, n, static, i), use)

            silu_steps("moe", MOE_STEPS)
            act.wait_ge(S("out_1"), 1)
            squares(2)
            root_mean("norm2")

            def pre_norm(n):
                for b in range(4):
                    if n > 3:
                        act.wait_ge(S("added"), 4 * ((n - 3) // 2 - 1) + b + 1)
                    else:
                        act.wait_ge(S("normed"), 2 * KD + 2 * b + 2)
                    act.activation(SQ[:, 2 * b:2 * b + 2, :], X[:, 2 * b:2 * b + 2, :], ACT.Square)\
                       .then_inc(S("squares"), 1)
                root_mean(f"n{n}")

            def post_norm(n, full):
                for b in range(4):
                    act.wait_ge(S("unit_used"), full[b])
                    act.activation(SQ[:, 2 * b:2 * b + 2, :], tiles(bank[b][:, :], 2), ACT.Square)\
                       .then_inc(S("squares"), 1)
                root_mean(f"n{n}")

            def ffn(n, first, follows=None):
                pre_norm(first)
                h_rounded(3 + (first - 3) // 2)
                silu_steps(f"ffn{n}", FFN_STEPS)
                if follows:
                    split_first(follows)
                post_norm(first + 1, [D_UNITS[f"ffn{n}"] + 3 * FFN_STEPS] * 4)

            def squares_out(name):
                return [D_UNITS[name] + b + 1 for b in range(4)]

            split_first("ffn0")
            ffn(0, 3)
            pre_norm(5)
            act.wait_ge(S("zeroed_2"), 1)
            evac("ab6", pr[:, 12:14, 1:1 + T], ACT.Copy)
            act.wait_ge(S("shifted"), 1)
            act.activation(pp[0:HD, 12, :], pp[0:HD, 12, :], ACT.Tanh).then_inc(S("lora_in"), 1)
            act.activation(pp[:, 13, :], pp[:, 13, :], ACT.Tanh, scale=0.5).then_inc(S("lora_in"), 1)
            for n in range(2):
                evac(f"ab{n}", pr[:, 2 * n:2 * n + 2, 1:1 + T], ACT.Copy)
            act.wait_ge(S("half_bias"), 1)
            act.wait_ge(S("lora_full"), 1)
            for m in range(MT):
                act.activation(lw[:, m, :], bank[m // 2][:, (m % 2) * T:(m % 2 + 1) * T], ACT.Tanh,
                               bias=hd_base[:, m:m + 1], scale=0.5).then_inc(S("lora_out"), 1)
            for m in range(MT):
                act.activation(rate[:, m, :], bank[2 + m // 2][:, (m % 2) * T:(m % 2 + 1) * T], ACT.Tanh,
                               bias=hi_base[:, m:m + 1], scale=0.5).then_inc(S("lora_out"), 1)
            for n in range(2, 6):
                evac(f"ab{n}", pr[:, 2 * n:2 * n + 2, 1:1 + T], ACT.Copy)
            for n in range(2):
                act.wait_ge(S("side_full"), SI[f"gu{n}"] + 1)
                act.activation(gup[:, 2 * n:2 * n + 2, :], tiles(bank[7][:, :], 2), ACT.Copy).then_inc(S("side_free"), 1)
            for n in range(2):
                evac(f"ab{9 + n}", cg[:, 2 * n:2 * n + 2, :], ACT.Tanh, scale=0.5)
            act.wait_ge(S("kk_max"), 1)
            act.activation(e_l[:, :, :], e_l[:, :, :], ACT.Sqrt).then_inc(S("kk_root"), 1)
            act.wait_ge(S("logs"), 1)
            act.activation(e_p[:, :, :], e_p[:, :, :], ACT.Exp).then_inc(S("exps"), 1)
            act.activation(e_n[:, :, :], cum_l[:, :, :], ACT.Exp, scale=-1.0).then_inc(S("exps"), 1)
            act.wait_ge(S("kk_used"), 1)
            act.activation(e_l[:, :, :], cum_l[:, :, :], ACT.Exp).then_inc(S("exps"), 1)
            for n in range(2):
                evac(f"ab{7 + n}", cv[:, 2 * n:2 * n + 2, :], ACT.Copy)
            act.wait_ge(S("turned"), 1)
            for c in range(TT):
                act.activation(v_tok[:, c, :], bank[c][:, :], ACT.Copy)
            act.activation(kh_tok, bank[2][:, :], ACT.Copy)
            act.activation(bh_tok, bank[3][:, :], ACT.Copy, scale=-1.0).then_inc(S("tok_ok"), 1)
            for g in range(4):
                act.wait_ge(S("y_full"), g + 1)
                act.activation(mat_y[:, 4 * g:4 * g + 4, :], tiles(bank[5 + g % 2][:, :], 4), ACT.Copy)\
                   .then_inc(S("y_free"), 1)
            diags_made = [0]

            def make_diags(count):
                for j in range(diags_made[0], min(diags_made[0] + count, (MT - CONV_V) * CONV_B)):
                    m, k = CONV_V + j // CONV_B, j % CONV_B
                    if j >= DIAGS:
                        act.wait_ge(S("diag_used"), j - DIAGS + 1)
                    act.activation(diag[:, j % DIAGS, :], C("ident"), ACT.Copy, scale=P2("conv_w")[:, MT * k + m:MT * k + m + 1])\
                       .then_inc(S("diag_ok"), 1)
                    diags_made[0] = j + 1

            make_diags(DIAGS)
            for c in range(TT):
                act.wait_ge(S("rw_full"), 3 * c + 1)
                act.activation(rw_r, bank[4 * c][:, :], ACT.Copy).then_inc(S("rw_r"), 1)
                make_diags(DIAG_RUNS[3 * c])
                act.wait_ge(S("rw_full"), 3 * c + 2)
                act.activation(rw_u, bank[4 * c + 1][:, :], ACT.Copy).then_inc(S("rw_u"), 1)
                make_diags(DIAG_RUNS[3 * c + 1])
                if c == 0:
                    make_diags(DIAG_RUNS[2])
            make_diags(DIAG_RUNS[5])
            act.wait_ge(S("gn_var"), 1)
            act.activation(gn_rs, gn_sum, ACT.Sqrt, bias=C("eps")[:, 1:2], scale=1.0 / HD).then_inc(S("gn_root"), 1)
            make_diags(DIAG_RUNS[6])
            act.wait_ge(S("y_turned"), 1)
            for m in range(MT):
                act.activation(H[:, m, :], bank[m // 2][:, (m % 2) * T:(m % 2 + 1) * T], ACT.Identity,
                               bias=P2("lnx_b")[:, m:m + 1], scale=P2("lnx_g")[:, m:m + 1]).then_inc(S("gn_out"), 1)
            act.wait_ge(S("side_full"), SI["ln1"] + 1)
            act.activation(e_mean, bank[7][:, 0:T], ACT.Copy, scale=1.0 / MIX).then_inc(S("side_free"), 1)
            act.wait_ge(S("ln_centered"), 1)
            act.activation(ctmp[:, :, :], cacc[:, :, :], ACT.Square).then_inc(S("ln_sq"), 1)
            root_mean("ln2", scale=1.0 / MIX, eps=2)
            act.wait_ge(S("ln_scaled"), 1)
            for m in range(MT):
                act.activation(H[:, MT + m, :], cacc[:, m, :], ACT.Silu, bias=P2("ln_b")[:, m:m + 1],
                               scale=P2("ln_g")[:, m:m + 1]).then_inc(S("y_conv"), 1)
            act.wait_ge(S("unit_used"), D_UNITS["ab_out"] + 1)
            split_first("ffn1")
            post_norm(6, squares_out("ab_out"))
            ffn(1, 7, "ffn2")
            ffn(2, 9, "c")
            pre_norm(11)
            h_rounded(7)

            def head_norm(n):
                act.wait_ge(S("side_full"), SI[f"hs{n}"] + 1)
                if n >= 2:
                    act.wait_ge(S("hn_done"), n - 1)
                act.activation(f_rs[:, n % 2, :], bank[7][:, :], ACT.Sqrt, bias=C("eps")[:, 0:1], scale=1.0 / HD)\
                   .then_inc(S("side_free"), 1)

            for n in range(8):
                split_ahead("c", n, C_SPLIT)
                act.wait_ge(S(FULL[f"c{n}"][0]), FULL[f"c{n}"][1])
                if n >= 2:
                    act.wait_ge(S("side_full"), SI[f"hs{n - 2}"] + 1)
                act.activation(f_sq[:, n % 2, :], bank[5 + GI[f"c{n}"] % 2][:, :], ACT.Square).then_inc(S("f_sq"), 1)
                evac(f"c{n}", fq[:, 2 * n:2 * n + 2, :], ACT.Copy)
                if n:
                    head_norm(n - 1)
            head_norm(7)
            for n in range(4):
                split_ahead("c", 8 + n, C_SPLIT)
                evac(f"c{8 + n}", f_v[:, :, n * UC:(n + 1) * UC], ACT.Copy)
            act.wait_ge(S("f_abs"), 1)
            act.activation(fe[0:N_FOX, :], fa[0:N_FOX, :], ACT.Exp, scale=-1.0).then_inc(S("f_exp"), 1)
            act.wait_ge(S("f_one"), 1)
            act.activation(fl[0:N_FOX, :], fa[0:N_FOX, :], ACT.Ln).then_inc(S("f_log"), 1)
            for n in range(8):
                act.wait_ge(S("side_full"), SI[f"cb{n}"] + 1)
                act.activation(f_cum[:, 2 * n:2 * n + 2, :], tiles(bank[7][:, :], 2), ACT.Copy).then_inc(S("side_free"), 1)

            def fox_slot(n):
                if n < N_FOX:
                    b = n % 2
                    act.wait_ge(S("fmax_ok"), n + 1)
                    if n >= 3:
                        act.wait_ge(S("fpt_full"), n - 2)
                    for t, (a, z) in enumerate(((0, P), (P, 3 * P))):
                        act.activation(fat_p[:, n % 3, a:z], fat_s[:, b, a:z], ACT.Exp,
                                       bias=neg_max[:, 2 * b + t:2 * b + t + 1],
                                       accum_out=row_sum[:, 2 * b + t:2 * b + t + 1]).then_inc(S("fexp_done"), 1)
                if 2 <= n < N_FOX + 2:
                    act.wait_ge(S("fpt_full"), n - 1)
                    if n >= 4:
                        act.wait_ge(S("fpv_done"), n - 3)
                    act.activation(fat_t[:, n % 2, :], bank[2 + n % 2][:, 0:384], ACT.Copy)\
                       .then_inc(S("fpt_free"), 1)

            fox_schedule(fox_slot, lambda j, half: half and evac(f"c{12 + j}", f_gate[:, 2 * j:2 * j + 2, :], ACT.Tanh,
                                                                 scale=0.5))
            act.wait_ge(S("unit_used"), D_UNITS["ffn3"])
            split_first("ffn3")
            post_norm(12, squares_out("c_out"))
            ffn(3, 13)

        @block.vector
        def _(dve):
            chain = [0]

            def link(ins):
                chain[0] += 1
                ins.then_inc(S("dve_chain"), 1)
                dve.wait_ge(S("dve_chain"), chain[0])

            def h_left(name):
                nth = NTH[name]
                for half in range(2):
                    ks = slice(4 * half, 4 * half + 4)
                    dve.wait_ge(S("h_hi"), nth * KD + 4 * half + 4)
                    dve.tensor_tensor(h_lo[:, ks, :], H[:, ks, :], h_hi[:, ks, :].bitcast(FP32), ALU.subtract)\
                       .then_inc(S("h_lo"), 1)

            def split(name, n, static, i=None):
                unit = D_UNITS[name] + static
                dve.wait_ge(S("w_hi"), n + (SPLIT0[name] + 1))
                dve.tensor_tensor(w_lo[:, unit % SPLIT, :], ring[:, unit % RING, :], w_hi[:, unit % SPLIT, :].bitcast(FP32),
                                  ALU.subtract).then_inc(S("w_lo"), 1)

            def split_first(name):
                for n in range(2):
                    split(name, n, n)

            def norm(n, side, gain, dst):
                dve.wait_ge(S("side_free"), SI[side] + 1)
                link(dve.reciprocal(rstd[:, :], rstd[:, :]))
                for k in range(KD):
                    dve.scalar_tensor_tensor(dst[:, k, :], X[:, k, :], gain[:, k:k + 1], rstd[:, :], ALU.mult,
                                             ALU.mult).then_inc(S("normed"), 1)

            dve.memset(small(110, 1), 0.0).then_inc(S("hid_done"), 1)
            dve.wait_ge(S("con"), 16)
            dve.wait_ge(S("sm1"), 16)
            dve.wait_ge(S("x"), 16)
            split_first("proj")
            norm(0, "norm0", P1("n1"), H)
            h_left("proj")
            gm_w = tiles(P1("gm_wT"), 4)
            link(dve.tensor_tensor(gm_w, gm_w, C("s_le_t").unsqueeze(1).to_broadcast([P, 4, P]), ALU.mult))
            link(dve.tensor_scalar(hb_a, P1("ba"), 0.5, None, ALU.mult))
            link(dve.tensor_scalar(hb_x, P1("bx"), 0.5, None, ALU.mult))
            link(dve.tensor_scalar(lam_d, P1("lam"), -1.0, None, ALU.mult))
            dve.tensor_tensor(lam_t, lam_d, P1("lam"), ALU.max).then_inc(S("lam_abs"), 1)
            for n in range(2, PROJ_SPLIT):
                split("proj", n, n)
            dve.wait_ge(S("proj_free"), GI["kvc"] + 1)
            for c in range(2):
                by16 = kvc[:, c, :].rearrange("p (n l) -> p l n", l=16)
                for half in range(2):
                    pe_c = P1("pe")[:, c * 32 + half * 16:c * 32 + half * 16 + 16]
                    ins = dve.tensor_tensor(kpe[:, c, half * 16:half * 16 + 16, 0:N_CMP],
                                            by16[:, :, half:half + N_CMP],
                                            pe_c.unsqueeze(2).to_broadcast([P, 16, N_CMP]), ALU.add)
            ins.then_inc(S("kpe"), 1)
            dve.wait_ge(S("v_sums"), 1)
            link(dve.reciprocal(v_rstd, v_rstd))
            for t in range(TT):
                dve.tensor_scalar(v1[:, t, :], v1[:, t, :], v_rstd[:, t:t + 1], None, ALU.mult)\
                   .then_inc(S("v_normed"), 1)
            dve.wait_ge(S("proj_free"), GI["g24"] + 1)
            link(dve.tensor_scalar(gates3[:, :, :], gates3[:, :, :], 0.5, 0.5, ALU.mult, ALU.add))

            def gmlp(pair):
                dve.wait_ge(S("side_full"), SI[f"gm{pair}"] + 1)
                for t in range(2):
                    g = 2 * pair + t
                    bias = P1("gm_b")[:, g * P:(g + 1) * P].unsqueeze(1).to_broadcast([P, 2, P])
                    link(dve.scalar_tensor_tensor(tiles(SQ[:, 2 + t, :], 2), tiles(bank[7][:, t * T:(t + 1) * T], 2),
                                                  P1("gm_g")[:, g:g + 1], bias, ALU.mult, ALU.add))
                    ins = dve.tensor_tensor(u[:, g, :], u[:, g, :], SQ[:, 2 + t, :], ALU.mult)
                    if t == 0:
                        link(ins)
                ins.then_inc(S("side_free"), 1)

            def compressed():
                dve.wait_ge(S("side_full"), SI["kvc2"] + 1)
                dve.wait_ge(S("zeroed_cmp"), 1)
                for g, ps in enumerate((bank[7], bank[4])):
                    dve.tensor_copy(k_c[:, g, 0:N_CMP], ps[:, g * 16:g * 16 + N_CMP])
                    ins = dve.tensor_copy(v_c[0:N_CMP, g * HD:(g + 1) * HD], ps[0:N_CMP, P + g * HD:P + (g + 1) * HD])
                ins.then_inc(S("side_free"), 1)

            def soft_1(n):
                b = n % 2
                dve.wait_ge(S("sc_full"), n + 1)
                if n >= 2:
                    dve.wait_ge(S("exp_done"), 2 * (n - 1))
                if n % 3 == 0:
                    s = tiles(att_s[:, b, 0:32], 2)[:, :, 0:N_CMP]
                    ins = dve.scalar_tensor_tensor(s, tiles(bank[b][:, 0:32], 2)[:, :, 0:N_CMP], SCALE,
                                                   tiles(C("cmp_add"), 2)[:, :, 0:N_CMP], ALU.mult, ALU.add)
                    ins.then_inc(S("sc_free"), 1)
                    dve.wait_ge(S("sc_free"), n + 1)
                    link(dve.tensor_reduce(neg_max[:, 2 * b:2 * b + 2], s, AX.X, ALU.max))
                else:
                    dve.scalar_tensor_tensor(att_s[:, b, :], bank[b][:, 0:384], SCALE, C("mask3"), ALU.mult, ALU.add)\
                       .then_inc(S("sc_free"), 1)
                    dve.wait_ge(S("sc_free"), n + 1)
                    dve.tensor_reduce(neg_max[:, 2 * b:2 * b + 1], att_s[:, b, 0:P], AX.X, ALU.max)
                    link(dve.tensor_reduce(neg_max[:, 2 * b + 1:2 * b + 2], att_s[:, b, P:3 * P], AX.X, ALU.max))
                dve.tensor_scalar(neg_max[:, 2 * b:2 * b + 2], neg_max[:, 2 * b:2 * b + 2], -1.0, None, ALU.mult)\
                   .then_inc(S("max_ok"), 1)

            def soft_2(n):
                b, h, kind = n % 2, n // 3, n % 3
                dve.wait_ge(S("exp_done"), 2 * (n + 1))
                inv = inv_sum[:, 2 * b:2 * b + 2]
                link(dve.reciprocal(inv, row_sum[:, 2 * b:2 * b + 2]))
                link(dve.tensor_tensor(inv, inv, gates3[:, :, 3 * h + kind], ALU.mult))
                for t in range(TT):
                    i = inv[:, t:t + 1]
                    if kind == 0:
                        w = p_cmp[:, t * P:t * P + N_CMP]
                        ins = dve.scalar_tensor_tensor(w, w, i, tiles(C("cmp_01"), 2)[:, t, 0:N_CMP], ALU.mult, ALU.mult)
                    else:
                        a, z = (0, P) if t == 0 else (P, 3 * P)
                        ins = dve.tensor_scalar(att_p[n % 3][:, a:z], att_p[n % 3][:, a:z], i, None, ALU.mult)
                ins.then_inc(S("p_ok"), 1)

            def conv(m):
                w = P1("conv_w")
                link(dve.tensor_scalar(xc[:, m, :], rec[:, m, 0:T], w[:, m:m + 1], P1("conv_b")[:, m:m + 1],
                                       ALU.mult, ALU.add))
                for k in range(1, CONV_A):
                    ins = dve.scalar_tensor_tensor(xc[:, m, :], rec[:, m, k:k + T], w[:, MT * k + m:MT * k + m + 1],
                                                   xc[:, m, :], ALU.mult, ALU.add)
                    if k < CONV_A - 1:
                        link(ins)
                ins.then_inc(S("xc"), 1)

            def lam_1():
                dve.wait_ge(S("lam_z"), 1)
                dve.tensor_scalar(lam_t, lam_z, 1.0, None, ALU.add).then_inc(S("lam_u"), 1)

            def lam_2():
                dve.wait_ge(S("lam_l"), 1)
                link(dve.tensor_scalar(lam_d, lam_t, -1.0, None, ALU.add))
                link(dve.tensor_scalar(lam_e, lam_d, 0.0, None, ALU.is_equal))
                link(dve.tensor_tensor(lam_d, lam_d, lam_e, ALU.add))
                link(dve.reciprocal(lam_d, lam_d))
                link(dve.tensor_tensor(lam_c, lam_l, lam_d, ALU.mult))
                link(dve.tensor_tensor(lam_c, lam_c, lam_e, ALU.add))
                link(dve.tensor_tensor(lam_c, lam_c, lam_z, ALU.mult))
                link(dve.tensor_scalar(lam_d, P1("lam"), -1.0, 0.0, ALU.mult, ALU.max))
                link(dve.tensor_tensor(lam_c, lam_c, lam_d, ALU.add))
                link(dve.tensor_scalar(lam_c, lam_c, -4.0, None, ALU.mult))

            def recur_1():
                dve.wait_ge(S("side_free"), SI["wx1"] + 1)
                link(dve.scalar_tensor_tensor(xc[:, :, :], th_i[:, :, :], 1.0, xc[:, :, :], ALU.add, ALU.mult))
                for m in range(MT):
                    ins = dve.tensor_scalar(th_r[:, m, :], th_r[:, m, :], 1.0, lam_c[:, m:m + 1], ALU.add, ALU.mult)
                ins.then_inc(S("log_a"), 1)

            def recur_2():
                dve.wait_ge(S("decay"), 1)
                link(dve.tensor_scalar(e_b[:, :, :], th_i[:, :, :], -1.0, 1.0, ALU.mult, ALU.add))
                link(dve.reciprocal(e_b[:, :, :], e_b[:, :, :]))
                dve.scalar_tensor_tensor(e_b[:, :, :], th_i[:, :, :], -2.0, e_b[:, :, :], ALU.mult, ALU.mult)\
                   .then_inc(S("e_ok"), 1)

            def recur_3():
                dve.wait_ge(S("e_root"), 1)
                link(dve.scalar_tensor_tensor(xc[:, :, :], e_b[:, :, :], 0.5, xc[:, :, :], ALU.mult, ALU.mult))
                for m in range(MT):
                    ins = dve.tensor_tensor_scan(e_b[:, m, :], th_r[:, m, :], xc[:, m, :], 0.0, ALU.mult, ALU.add)
                link(ins)
                dve.tensor_tensor(gate[:, :, :], gate[:, :, :], e_b[:, :, :], ALU.mult).then_inc(S("y_b"), 1)

            def run_mg(j, half):
                if not half:
                    return
                if j < 2:
                    gmlp(j)
                if j == 2:
                    compressed()
                    lam_1()
                if j == 3:
                    lam_2()
                if 3 <= j <= 6:
                    conv(j - 3)
                if j == 12:
                    recur_1()
                if j == 14:
                    recur_2()
                if j == 15:
                    recur_3()

            def run_slot(n):
                if n < N_SLOTS:
                    soft_1(n)
                if 1 <= n <= N_SLOTS:
                    soft_2(n - 1)
                if n >= 3 and (n - 3) % 6 == 5:
                    p = (n - 3) // 6
                    dve.wait_ge(S("pv_done"), 6 * (p + 1))
                    dve.tensor_copy(yc[:, p, :], bank[4][:, (p % 2) * T:(p % 2) * T + T]).then_inc(S("o_free"), 1)

            schedule(run_slot, run_mg)

            for n in range(4):
                for half in range(2):
                    unit = 2 * n + half
                    dve.wait_ge(S("unit_used"), D_UNITS["branch"] + unit + 1)
                    for b in range(2):
                        d0 = 4 * half + 2 * b
                        dst = SQ if n == 0 else H
                        ins = dve.scalar_tensor_tensor(dst[:, d0:d0 + 2, :], mg[:, KD * n + d0:KD * n + d0 + 2, :], 1.0,
                                                       tiles(bank[2 * half + b][:, :], 2), ALU.add, ALU.mult)
                        ins.then_inc(S("br_free"), 1)
                        if n:
                            dve.wait_ge(S("br_free"), 2 * unit + b + 1)
                            link(dve.tensor_tensor(SQ[:, d0:d0 + 2, :], SQ[:, d0:d0 + 2, :], H[:, d0:d0 + 2, :], ALU.add))
            dve.tensor_scalar(H[:, :, :], SQ[:, :, :], 0.5, None, ALU.mult).then_inc(S("merged"), 1)

            def add_square(name, dst, src=None):
                for n in range(SQUARE):
                    dve.wait_ge(S("unit_used"), D_UNITS[name] + n + 1)
                    d = dst[:, 2 * n:2 * n + 2, :]
                    ps = tiles(bank[n][:, :], 2)
                    ins = dve.tensor_tensor(d, ps, src[:, 2 * n:2 * n + 2, :], ALU.add) if src is not None \
                        else dve.tensor_copy(d, ps)
                    ins.then_inc(S("res_done"), 1)

            dve.wait_ge(S("merged"), 1)
            split_first("moe")
            add_square("w_out", X, X)
            norm(1, "norm1", P1("n2"), H)
            h_left("moe")

            dve.wait_ge(S("side_full"), SI["route"] + 1)
            lg = tiles(route[:, 0:40], 2)
            dve.tensor_tensor(lg, tiles(bank[7][:, 0:40], 2), P1("b_route").unsqueeze(1).to_broadcast([P, 2, 20]),
                              ALU.add).then_inc(S("side_free"), 1)
            dve.wait_ge(S("side_free"), SI["route"] + 1)
            gl, el = lg[:, :, 0:4], lg[:, :, 4:20]
            gmax, ge, gw = route[:, 40:42], route[:, 48:56], route[:, 64:66]
            one_g, pick, in_g, o1, o2, rest = (tiles(route[:, 80 + 32 * n:80 + 32 * n + w], 2) for n, w in
                                               enumerate((8, 32, 8, 8, 8, 8)))
            m1, m2, w1, w2 = route[:, 280:282], route[:, 282:284], route[:, 284:286], rt_w2

            def bc(x, n):
                return x.unsqueeze(2).to_broadcast([P, 2, n])

            def first_of(dst, src, top, tmp):
                link(dve.tensor_tensor(dst, src, bc(top, 4), ALU.is_equal))
                for k in range(1, 4):
                    link(dve.tensor_reduce(tmp, dst[:, :, 0:k], AX.X, ALU.max))
                    link(dve.tensor_scalar(tmp, tmp, -1.0, 1.0, ALU.mult, ALU.add))
                    link(dve.tensor_tensor(dst[:, :, k], dst[:, :, k], tmp, ALU.mult))
            t2 = route[:, 290:292]
            link(dve.tensor_reduce(gmax, gl, AX.X, ALU.max))
            link(dve.tensor_tensor(tiles(ge, 2), gl, bc(gmax, 4), ALU.subtract))
            first_of(one_g, gl, gmax, t2)
            dve.tensor_copy(gsum, ge).then_inc(S("rt_1"), 1)
            dve.wait_ge(S("rt_1"), 1)
            el4 = route[:, 0:40].rearrange("p (t c) -> p t c", t=2)[:, :, 4:20]
            for t in range(2):
                e_t = el4[:, t, :].rearrange("p (g e) -> p g e", g=4)
                link(dve.tensor_tensor(pick[:, t, :].rearrange("p (g e) -> p g e", g=4), e_t,
                                       one_g[:, t, :].unsqueeze(2).to_broadcast([P, 4, 4]), ALU.mult))
                link(dve.tensor_reduce(in_g[:, t, :], pick[:, t, :].rearrange("p (g e) -> p e g", g=4), AX.X, ALU.add))
            link(dve.tensor_reduce(m1, in_g, AX.X, ALU.max))
            first_of(o1, in_g, m1, t2)
            link(dve.scalar_tensor_tensor(rest, o1, 2.0 * NEG, in_g, ALU.mult, ALU.add))
            link(dve.tensor_reduce(m2, rest, AX.X, ALU.max))
            first_of(o2, rest, m2, t2)
            dve.tensor_tensor(w2, m2, m1, ALU.subtract).then_inc(S("rt_2"), 1)
            dve.wait_ge(S("rt_e"), 2)
            link(dve.tensor_reduce(gw, tiles(gsum, 2), AX.X, ALU.add))
            link(dve.tensor_scalar(w1, w2, 1.0, None, ALU.add))
            link(dve.tensor_tensor(w1, w1, gw, ALU.mult))
            link(dve.reciprocal(w1, w1))
            link(dve.tensor_tensor(w2, w2, w1, ALU.mult))
            link(dve.tensor_tensor(o1, o1, bc(w1, 4), ALU.mult))
            link(dve.tensor_tensor(o2, o2, bc(w2, 4), ALU.mult))
            link(dve.tensor_tensor(o1, o1, o2, ALU.add))
            for t in range(2):
                ins = dve.tensor_tensor(pick[:, t, :].rearrange("p (g e) -> p g e", g=4),
                                        one_g[:, t, :].unsqueeze(2).to_broadcast([P, 4, 4]),
                                        o1[:, t, :].unsqueeze(1).to_broadcast([P, 4, 4]), ALU.mult)
                ins.then_inc(S("combine"), 1)
            for n in range(8):
                dve.wait_ge(S("side_full"), SI[f"comb{n}"] + 1)
                dve.tensor_copy(comb_all[:, 2 * n:2 * n + 2, :], tiles(bank[7][:, :], 2)).then_inc(S("side_free"), 1)
            dve.wait_ge(S("side_free"), SI["comb7"] + 1)

            def hid_steps(name, steps, experts=False):
                s0 = STEP0[name]

                def use(s, parity, half=None):
                    dve.wait_ge(S("silu_done"), s + (s0 + 1))
                    up = tiles(bank[5 + 2 * parity][:, :], 2)
                    dve.tensor_tensor(hid, sil[parity], up, ALU.mult).then_inc(S("hid_32"), 1)
                    if experts:
                        expert = slice(s // 2, s // 2 + 1) if half is None else bass.ds(half, 1)
                        dve.wait_ge(S("hid_32"), s * 2 + 1)
                        dve.tensor_tensor(hid, hid, comb_all[:, expert, :].to_broadcast([P, 2, T]), ALU.mult)\
                           .then_inc(S("hid_32"), 1)
                        dve.wait_ge(S("hid_32"), s * 2 + 2)
                    else:
                        dve.wait_ge(S("hid_32"), s + (s0 + MOE_STEPS + 1))
                    dve.tensor_copy(hid_hi[:, parity, :, :], hid).then_inc(S("hid_hi"), 1)
                    dve.wait_ge(S("hid_hi"), s + (s0 + 1))
                    dve.tensor_tensor(hid_lo[:, parity, :, :], hid, hid_hi[:, parity, :, :].bitcast(FP32), ALU.subtract)\
                       .then_inc(S("hid_done"), 1)

                split_order(name, steps, dve, lambda n, static, i=None: split(name, n, static, i), use)

            hid_steps("moe", MOE_STEPS, experts=True)
            dve.wait_ge(S("unit_used"), D_UNITS["moe"] + 3 * MOE_STEPS)
            for b in range(4):
                ins = dve.tensor_tensor(X[:, 2 * b:2 * b + 2, :], tiles(bank[b][:, :], 2), X[:, 2 * b:2 * b + 2, :], ALU.add)
            ins.then_inc(S("out_1"), 1)
            dve.wait_ge(S("out_1"), 1)
            norm(2, "norm2", P1("nf"), X)

            def add_normed(n, gain_index, half):
                gain = P2("n")[:, gain_index * KD:(gain_index + 1) * KD]
                if half:
                    link(dve.tensor_scalar(half_gain, gain, 0.5, None, ALU.mult))
                    gain = half_gain
                dve.wait_ge(S("side_free"), SI[f"n{n}"] + 1)
                link(dve.reciprocal(rstd[:, :], rstd[:, :]))
                for b in range(4):
                    two = scratch[b % 2]
                    for c in range(2):
                        k = 2 * b + c
                        ins = dve.scalar_tensor_tensor(two[:, c, :], bank[b][:, c * T:(c + 1) * T], gain[:, k:k + 1],
                                                       rstd[:, :], ALU.mult, ALU.mult)
                    link(ins)
                    dve.tensor_tensor(X[:, 2 * b:2 * b + 2, :], X[:, 2 * b:2 * b + 2, :], two, ALU.add)\
                       .then_inc(S("added"), 1)
                dve.wait_ge(S("added"), 4 * ((n - 2) // 2))

            def pre_norm(n, gain_index):
                norm(n, f"n{n}", P2("n")[:, gain_index * KD:(gain_index + 1) * KD], H)

            def ffn(n, first, layer, place, follows=None):
                pre_norm(first, 6 * layer + place)
                h_left(f"ffn{n}")
                hid_steps(f"ffn{n}", FFN_STEPS)
                if follows:
                    split_first(follows)
                add_normed(first + 1, 6 * layer + place + 1, True)

            dve.wait_ge(S("normed"), 3 * KD)
            dve.wait_ge(S("sm2"), 16)
            split_first("ffn0")
            ffn(0, 3, 0, 0)
            pre_norm(5, 2)

            def shift(n):
                dve.wait_ge(S("proj_free"), GI[f"ab{n}"] + 1)
                two = slice(2 * n, 2 * n + 2)
                link(dve.tensor_tensor(pp[:, two, :], pr[:, two, 0:T], pr[:, two, 1:1 + T], ALU.subtract))
                for m in range(2 * n, 2 * n + 2):
                    ins = dve.scalar_tensor_tensor(pp[:, m, :], pp[:, m, :], P2("mu")[:, m:m + 1], pr[:, m, 1:1 + T],
                                                   ALU.mult, ALU.add)
                return ins

            link(dve.tensor_scalar(hd_base, P2("d_base"), 0.5, None, ALU.mult))
            dve.tensor_scalar(hi_base, P2("i_base"), 0.5, None, ALU.mult).then_inc(S("half_bias"), 1)
            shift(6).then_inc(S("shifted"), 1)
            dve.wait_ge(S("lora_in"), 2)
            dve.tensor_scalar(pp[:, 13, :], pp[:, 13, :], 0.5, 0.5, ALU.mult, ALU.add).then_inc(S("gate_in"), 1)
            for n in range(2):
                link(shift(n))
            dve.wait_ge(S("lora_out"), MT)
            c_log = -0.5 * float(np.exp(-0.5))
            link(dve.tensor_scalar(lw[:, :, :], lw[:, :, :], 1.0, c_log, ALU.add, ALU.mult))
            for m in range(MT):
                ins = dve.tensor_tensor_scan(cum_l[:, m, :], C("keep"), lw[:, m, :], 0.0, ALU.mult, ALU.add)
            link(ins)
            dve.tensor_tensor(e_p[:, :, :], cum_l[:, :, :], lw[:, :, :], ALU.subtract).then_inc(S("logs"), 1)
            dve.wait_ge(S("lora_out"), 2 * MT)
            link(dve.tensor_scalar(rate[:, :, :], rate[:, :, :], 0.5, 0.5, ALU.mult, ALU.add))
            for n in range(2, 4):
                link(shift(n))
            r, k, v = pp[:, 0:4, :], pp[:, 4:8, :], pp[:, 8:12, :]
            for m in range(MT):
                ins = dve.tensor_scalar(kk[:, m, :], k[:, m, :], P2("k_k")[:, m:m + 1], None, ALU.mult)
            link(ins)
            dve.tensor_tensor(kkt[:, :, :], kk[:, :, :], kk[:, :, :], ALU.mult).then_inc(S("kk_sq"), 1)
            for m in range(MT):
                ins = dve.tensor_scalar(bh[:, m, :], rate[:, m, :], 1.0, P2("k_a")[:, m:m + 1], ALU.subtract, ALU.mult)
            link(ins)
            link(dve.scalar_tensor_tensor(k, bh[:, :, :], 1.0, k, ALU.add, ALU.mult))
            for m in range(MT):
                ins = dve.scalar_tensor_tensor(qt[:, m, :], r[:, m, :], P2("r_k")[:, m:m + 1], k[:, m, :], ALU.mult,
                                               ALU.mult)
            ins.then_inc(S("bonus_in"), 1)
            for n in range(4, 6):
                link(shift(n))
            for n in range(2):
                dve.wait_ge(S("side_full"), SI[f"kk{n}"] + 1)
                dve.tensor_scalar(e_l[:, 2 * n:2 * n + 2, :], tiles(bank[7][:, :], 2), 1e-24, None, ALU.max)\
                   .then_inc(S("side_free"), 1)
            dve.wait_ge(S("side_free"), SI["kk1"] + 1)
            dve.tensor_copy(half_gain, half_gain).then_inc(S("kk_max"), 1)
            dve.wait_ge(S("kk_root"), 1)
            link(dve.reciprocal(e_l[:, :, :], e_l[:, :, :]))
            dve.tensor_tensor(kk[:, :, :], kk[:, :, :], e_l[:, :, :], ALU.mult).then_inc(S("kk_used"), 1)
            dve.wait_ge(S("kk_used"), 1)
            for n in range(2):
                dve.wait_ge(S("side_full"), SI[f"bo{n}"] + 1)
                dve.tensor_tensor(bon[:, 2 * n:2 * n + 2, :], tiles(bank[7][:, :], 2), v[:, 2 * n:2 * n + 2, :], ALU.mult)\
                   .then_inc(S("side_free"), 1)
            dve.wait_ge(S("exps"), 2)
            link(dve.tensor_tensor(kkt[:, :, :], kk[:, :, :], e_p[:, :, :], ALU.mult))
            link(dve.tensor_tensor(kh[:, :, :], k, e_n[:, :, :], ALU.mult))
            link(dve.tensor_tensor(bh[:, :, :], kk[:, :, :], rate[:, :, :], ALU.mult))
            link(dve.tensor_tensor(bh[:, :, :], bh[:, :, :], e_n[:, :, :], ALU.mult))
            dve.wait_ge(S("exps"), 3)
            link(dve.tensor_copy(e_last, e_l[:, :, P - 1]))
            dve.tensor_tensor(qt[:, :, :], r, e_l[:, :, :], ALU.mult).then_inc(S("factors"), 1)
            dve.wait_ge(S("zeroed_2"), 1)
            dve.wait_ge(S("proj_free"), GI["ab8"] + 1)
            for m in range(MT):
                dve.scalar_tensor_tensor(glu[:, m, CONV_B - 1:CONV_B - 1 + T], cg[:, m, :], 1.0, cv[:, m, :], ALU.add,
                                         ALU.mult).then_inc(S("glu"), 1)
            taps_done = [0]

            def conv_taps(count):
                for k in range(taps_done[0], min(taps_done[0] + count, CONV_B)):
                    for m in range(CONV_V):
                        w = P2("conv_w")[:, MT * k + m:MT * k + m + 1]
                        src = glu[:, m, k:k + T]
                        if k == 0:
                            ins = dve.tensor_scalar(cacc[:, m, :], src, w, None, ALU.mult)
                        else:
                            ins = dve.scalar_tensor_tensor(cacc[:, m, :], src, w, cacc[:, m, :], ALU.mult, ALU.add)
                    link(ins)
                    taps_done[0] = k + 1

            dve.wait_ge(S("glu"), MT)
            dve.wait_ge(S("tok_ok"), 1)
            for c in range(TT):
                for p in range(4):
                    for par in range(2):
                        job = 8 * c + 2 * p + par
                        dve.wait_ge(S("gram_full"), job + 1)
                        dve.tensor_tensor(gram[:, 8 * c + 4 * par + p, :, :], tiles(bank[par + 2 * (p % 2)][:, :], 4),
                                          tiles(C("gram"), 4), ALU.mult).then_inc(S("gram_free"), 1)
            dve.wait_ge(S("gram_free"), N_MAT)
            ident4 = C("ident").unsqueeze(1).to_broadcast([P, 4, P])
            for g in range(4):
                four = slice(4 * g, 4 * g + 4)
                dve.wait_ge(S("y_free"), g + 1)
                link(dve.tensor_tensor(mat_w[:, four, :], mat_y[:, four, :],
                                       C("level_t").unsqueeze(1).to_broadcast([P, 4, P]), ALU.mult))
                link(dve.tensor_tensor(mat_w[:, four, :], mat_w[:, four, :], ident4, ALU.add))
                dve.tensor_tensor(mat_m[:, four, :], gram[:, four, 2, :], ident4, ALU.add).then_inc(S("mat_ok"), 1)
            dve.wait_ge(S("mat_ok"), 4)

            def q_out(n):
                level = C("level")[:, (n // 4 + 1) * P:(n // 4 + 2) * P].unsqueeze(1).to_broadcast([P, 4, P])
                dve.wait_ge(S("q_full"), n + 1)
                if n >= 2:
                    dve.wait_ge(S("mw_full"), n - 1)
                dve.tensor_tensor(tiles(mat_q[:, n % 2, :], 4), tiles(bank[n % 2][:, :], 4), level, ALU.mult)\
                   .then_inc(S("q_ok"), 1)

            def mw_out(n):
                four = slice(4 * (n % 4), 4 * (n % 4) + 4)
                dve.wait_ge(S("mw_full"), n + 1)
                if n < N_INV - 4:
                    dve.tensor_tensor(mat_w[:, four, :], mat_w[:, four, :], tiles(bank[5 + n % 2][:, :], 4), ALU.subtract)
                dve.tensor_tensor(mat_m[:, four, :], mat_m[:, four, :], tiles(bank[2 + n % 2][:, :], 4), ALU.subtract)\
                   .then_inc(S("mw_ok"), 1)

            for n in range(N_INV + 1):
                if n < N_INV:
                    q_out(n)
                if n:
                    mw_out(n - 1)
                conv_taps(1)
            dve.wait_ge(S("mw_ok"), N_INV)
            conv_taps(6)
            dve.wait_ge(S("rw_full"), 3)
            for m in range(MT):
                ins = dve.scalar_tensor_tensor(state[:, m, :], bank[3][:, m * P:(m + 1) * P], e_last[:, m:m + 1],
                                               C("head1"), ALU.mult, ALU.mult)
            ins.then_inc(S("state"), 1)
            dve.tensor_copy(rw_y[:, 0, :], bank[2][:, :]).then_inc(S("gn_in"), 1)
            conv_taps(6)
            dve.wait_ge(S("rw_full"), 6)
            dve.tensor_copy(rw_y[:, 1, :], bank[6][:, :]).then_inc(S("gn_in"), 1)
            dve.wait_ge(S("gn_in"), 2)
            yh = rw_y[:, :, :].rearrange("p c (h v) -> p (c h) v", v=HD)
            ysq = arena[:, phase:phase + TT * MIX].rearrange("p (h v) -> p h v", v=HD)
            link(dve.tensor_reduce(gn_sum, yh, AX.X, ALU.add))
            link(dve.tensor_scalar(gn_sum, gn_sum, 1.0 / HD, None, ALU.mult))
            link(dve.tensor_tensor(yh, yh, gn_sum.unsqueeze(2).to_broadcast([P, 16, HD]), ALU.subtract))
            link(dve.tensor_tensor(ysq, yh, yh, ALU.mult))
            dve.tensor_reduce(gn_sum, ysq, AX.X, ALU.add).then_inc(S("gn_var"), 1)
            dve.wait_ge(S("gn_root"), 1)
            link(dve.reciprocal(gn_rs, gn_rs))
            dve.tensor_tensor(yh, yh, gn_rs.unsqueeze(2).to_broadcast([P, 16, HD]), ALU.mult).then_inc(S("gn_y"), 1)
            conv_taps(CONV_B)
            for m in range(CONV_V):
                dve.tensor_scalar(cacc[:, m, :], cacc[:, m, :], 0.5, P2("conv_b")[:, m:m + 1], ALU.mult, ALU.add)
            dve.wait_ge(S("side_full"), SI["conv"] + 1)
            for m in range(CONV_V, MT):
                ins = dve.tensor_scalar(cacc[:, m, :], bank[7][:, (m - CONV_V) * T:(m - CONV_V + 1) * T], 0.5,
                                        P2("conv_b")[:, m:m + 1], ALU.mult, ALU.add)
            ins.then_inc(S("side_free"), 1)
            dve.wait_ge(S("gn_out"), MT)
            link(dve.tensor_tensor(H[:, 0:MT, :], H[:, 0:MT, :], bon[:, :, :], ALU.add))
            dve.tensor_tensor(H[:, 0:MT, :], H[:, 0:MT, :], gup[:, :, :], ALU.mult).then_inc(S("y_rw"), 1)
            dve.wait_ge(S("side_free"), SI["ln1"] + 1)
            dve.tensor_tensor(cacc[:, :, :], cacc[:, :, :], e_mean.unsqueeze(1).to_broadcast([P, MT, T]), ALU.subtract)\
               .then_inc(S("ln_centered"), 1)
            dve.wait_ge(S("side_free"), SI["ln2"] + 1)
            link(dve.reciprocal(rstd[:, :], rstd[:, :]))
            dve.tensor_tensor(cacc[:, :, :], cacc[:, :, :], rstd[:, :].unsqueeze(1).to_broadcast([P, MT, T]), ALU.mult)\
               .then_inc(S("ln_scaled"), 1)
            split_first("ffn1")
            add_normed(6, 3, False)
            ffn(1, 7, 0, 4, "ffn2")
            ffn(2, 9, 1, 0, "c")

            pre_norm(11, 8)
            h_left("c")
            link(dve.tensor_scalar(qg8, P2("qg"), SCALE, None, ALU.mult))

            def head_norm(n):
                dve.wait_ge(S("side_free"), SI[f"hs{n}"] + 1)
                link(dve.reciprocal(f_rs[:, n % 2, :], f_rs[:, n % 2, :]))
                gain = qg8 if n < 4 else P2("kg")
                dve.wait_ge(S("proj_free"), GI[f"c{n}"] + 1)
                dve.scalar_tensor_tensor(fq[:, 2 * n:2 * n + 2, :], fq[:, 2 * n:2 * n + 2, :], gain[:, 0:1],
                                         tiles(f_rs[:, n % 2, :], 2), ALU.mult, ALU.mult).then_inc(S("hn_done"), 1)

            for n in range(2, C_SPLIT):
                split("c", n, n)
                if 3 <= n < 11:
                    head_norm(n - 3)
            s = slice(0, N_FOX)
            dve.wait_ge(S("side_full"), SI["f"] + 1)
            dve.tensor_scalar(fz[s, :], bank[7][s, 0:T], P2("fb")[s, :], None, ALU.add).then_inc(S("side_free"), 1)
            dve.wait_ge(S("side_free"), SI["f"] + 1)
            link(dve.tensor_scalar(fa[s, :], fz[s, :], -1.0, None, ALU.mult))
            dve.tensor_tensor(fa[s, :], fa[s, :], fz[s, :], ALU.max).then_inc(S("f_abs"), 1)
            link(dve.tensor_scalar(fm[s, :], fz[s, :], -1.0, 0.0, ALU.mult, ALU.max))
            dve.wait_ge(S("f_exp"), 1)
            dve.tensor_scalar(fa[s, :], fe[s, :], 1.0, None, ALU.add).then_inc(S("f_one"), 1)
            dve.wait_ge(S("f_one"), 1)
            link(dve.tensor_scalar(fz[s, :], fa[s, :], -1.0, None, ALU.add))
            link(dve.tensor_scalar(fc[s, :], fz[s, :], 0.0, None, ALU.is_equal))
            link(dve.tensor_tensor(fz[s, :], fz[s, :], fc[s, :], ALU.add))
            link(dve.reciprocal(fz[s, :], fz[s, :]))
            dve.wait_ge(S("f_log"), 1)
            link(dve.tensor_tensor(fz[s, :], fl[s, :], fz[s, :], ALU.mult))
            link(dve.tensor_tensor(fz[s, :], fz[s, :], fc[s, :], ALU.add))
            link(dve.tensor_tensor(fz[s, :], fz[s, :], fe[s, :], ALU.mult))
            link(dve.tensor_tensor(fz[s, :], fz[s, :], fm[s, :], ALU.add))
            link(dve.memset(fm[s, :], 0.0))
            dve.tensor_tensor_scan(fc[s, :], fz[s, :], fm[s, :], 0.0, ALU.add, ALU.add).then_inc(S("f_cum"), 1)

            def fox_slot(n):
                if n < N_FOX:
                    b = n % 2
                    dve.wait_ge(S("fsc_full"), n + 1)
                    dve.wait_ge(S("mc"), n + 1)
                    if n >= 2:
                        dve.wait_ge(S("fexp_done"), 2 * (n - 1))
                    dve.tensor_tensor(fat_s[:, b, :], bank[b][:, 0:384], f_mc[:, b, :], ALU.add).then_inc(S("fsc_free"), 1)
                    dve.wait_ge(S("fsc_free"), n + 1)
                    dve.tensor_reduce(neg_max[:, 2 * b:2 * b + 1], fat_s[:, b, 0:P], AX.X, ALU.max)
                    link(dve.tensor_reduce(neg_max[:, 2 * b + 1:2 * b + 2], fat_s[:, b, P:3 * P], AX.X, ALU.max))
                    dve.tensor_scalar(neg_max[:, 2 * b:2 * b + 2], neg_max[:, 2 * b:2 * b + 2], -1.0, None, ALU.mult)\
                       .then_inc(S("fmax_ok"), 1)
                if 1 <= n <= N_FOX:
                    b = (n - 1) % 2
                    dve.wait_ge(S("fexp_done"), 2 * n)
                    inv = inv_sum[:, 2 * b:2 * b + 2]
                    link(dve.reciprocal(inv, row_sum[:, 2 * b:2 * b + 2]))
                    link(dve.tensor_scalar(inv, inv, 0.5, None, ALU.mult))
                    p3 = fat_p[:, (n - 1) % 3, :]
                    for t, (a, z) in enumerate(((0, P), (P, 3 * P))):
                        ins = dve.tensor_scalar(p3[:, a:z], p3[:, a:z], inv[:, t:t + 1], None, ALU.mult)
                    ins.then_inc(S("fp_ok"), 1)
                if n >= 4 and n % 2 == 0:
                    p = (n - 4) // 2
                    dve.wait_ge(S("fpv_done"), 2 * (p + 1))
                    dve.wait_ge(S("proj_free"), GI[f"c{12 + p // 2}"] + 1)
                    dve.scalar_tensor_tensor(f_o[:, p, :], f_gate[:, p, :], 1.0, bank[4][:, (p % 2) * T:(p % 2 + 1) * T],
                                             ALU.add, ALU.mult).then_inc(S("fo_free"), 1)

            fox_schedule(fox_slot, lambda j, half: None)
            split_first("ffn3")
            add_normed(12, 9, False)
            ffn(3, 13, 1, 4)
            dve.tensor_copy(half_gain, half_gain).then_inc(S("out"), 1)

        @block.tensor
        def _(pe):
            def unit_ready(n, count=None):
                pe.wait_ge(S(f"unit{n % RING}"), 16 * (n // RING + 1) if count is None else count)
                return ring[:, n % RING, :].rearrange("p (k n) -> p k n", k=KD)

            def side_begin(name):
                if SI[name]:
                    pe.wait_ge(S("side_free"), SI[name])
                return bank[7]

            def norm_sums(n, name):
                side_begin(name)
                for k in range(KD):
                    if k % 2 == 0:
                        pe.wait_ge(S("squares"), 4 * n + k // 2 + 1)
                    ins = pe.matmul(bank[7][:, 0:T], C("ones"), SQ[:, k, :], start=(k == 0), stop=(k == KD - 1))
                ins.then_inc(S("side_full"), 1)

            def halves(ps, w, x_hi, x_lo, terms, first, h_ready=None):
                for a, (wp, xp) in enumerate(((0, x_hi), (1, x_hi), (0, x_lo))):
                    for k in range(terms):
                        if h_ready is not None and a == 0:
                            pe.wait_ge(S("h_hi"), h_ready * KD + k + 1)
                        if h_ready is not None and a == 2 and k % 4 == 0:
                            pe.wait_ge(S("h_lo"), h_ready * 2 + k // 4 + 1)
                        ins = pe.matmul(ps, w(wp, k), xp[:, k, :], start=first and a == 0 and k == 0,
                                        stop=first and a == 2 and k == terms - 1, skip_group_check=not first)
                return ins

            def parts(unit, wide):
                return [x[:, unit % SPLIT, :].rearrange("p (k n) -> p k n", k=wide) for x in (w_hi, w_lo)]

            def split_ready(name, n):
                pe.wait_ge(S("w_lo"), SPLIT0[name] + n + 1)
                return parts(D_UNITS[name] + n, KD)

            def split_channels(ps, name, n):
                w = split_ready(name, n)
                for c in range(2):
                    ins = halves(ps[:, c * T:(c + 1) * T], lambda a, k: w[a][:, k, c * P:(c + 1) * P], h_hi, h_lo, KD, True,
                                 NTH[name] if n == 0 and c == 0 else None)
                ins.then_inc(S("unit_used"), 1)

            def split_tokens(ps, name, n):
                w = split_ready(name, n)
                for t in range(TT):
                    for a, (wp, x) in enumerate(((0, h_hi), (1, h_hi), (0, h_lo))):
                        for k in range(KD):
                            ins = pe.matmul(ps[:, t * UC:(t + 1) * UC], x[:, k, t * P:(t + 1) * P], w[wp][:, k, :],
                                            start=(a == 0 and k == 0), stop=(a == 2 and k == KD - 1))
                ins.then_inc(S("unit_used"), 1)

            def group_begin(name):
                n = GI[name]
                if n >= 2:
                    pe.wait_ge(S("proj_free"), n - 1)
                return bank[5 + n % 2]

            def project(ps, weights, src=H):
                for k in range(KD):
                    ins = pe.matmul(ps, weights(k), src[:, k, :], start=(k == 0), stop=(k == KD - 1))
                return ins

            def project_tokens(ps, weights, width):
                for t in range(TT):
                    for k in range(KD):
                        ins = pe.matmul(ps[:, t * width:(t + 1) * width], H[:, k, t * P:(t + 1) * P], weights(k),
                                        start=(k == 0), stop=(k == KD - 1))
                return ins

            def unit_channels(ps, w, halves=(0, 1)):
                for c in halves:
                    ins = project(ps[:, c * T:(c + 1) * T], lambda k: w[:, k, c * P:(c + 1) * P])
                if c == 1:
                    ins.then_inc(S("unit_used"), 1)

            def half_unit(name, half):
                n = FULL[name][1] - 1
                if half == 0:
                    unit_channels(group_begin(name), unit_ready(n), (0,))
                else:
                    unit_channels(bank[5 + GI[name] % 2], ring[:, n % RING, :].rearrange("p (k n) -> p k n", k=KD), (1,))

            pe.wait_ge(S("con"), 16)
            norm_sums(0, "norm0")
            for name in ("u0", "u1", "v0", "v1", "ga0", "ga1", "re0", "re1", "q0", "q1", "kvc"):
                (split_tokens if name[0] == "v" else split_channels)(group_begin(name), "proj", FULL[name][1] - 1)
            for c, kind in enumerate("sw"):
                n = FULL[f"v{kind}"][1] - 1
                ps, w = group_begin(f"k{kind}"), split_ready("proj", n)
                halves(ps[:, 0:T], lambda a, k: w[a][:, k, 0:P], h_hi, h_lo, KD, True).then_inc(S("part_full"), 1)
                ps, w = group_begin(f"v{kind}"), unit_ready(n)
                project_tokens(ps, lambda k: w[:, k, P:2 * P], P).then_inc(S("unit_used"), 1)
                ps = group_begin(f"kk{kind}")
                pe.wait_ge(S("proj_free"), GI[f"k{kind}"] + 1)
                for g in range(2):
                    for half in range(2):
                        ins = pe.matmul(ps[HD * half:HD * half + HD, g * T:(g + 1) * T], C("ident")[:, g * HD:(g + 1) * HD],
                                        keys_2[:, c, :], start=True, stop=True)
                ins.then_inc(S("part_full"), 1)
            pe.wait_ge(S("sm1"), 16)
            w_gate = P1("w_gate").rearrange("p (k n) -> p k n", k=KD)
            project_tokens(group_begin("g24"), lambda k: w_gate[:, k, :], 24).then_inc(S("part_full"), 1)
            for name in ("xd0", "xd1"):
                split_channels(group_begin(name), "proj", FULL[name][1] - 1)

            gm_w = tiles(P1("gm_wT"), 4)
            wa, wx, pool_w = tiles(P1("wa"), MT), tiles(P1("wx"), MT), tiles(P1("pool_w"), MT)
            cw2 = P1("cw2").rearrange("p (c d) -> p c d", c=2)

            def gmlp(pair):
                ps = side_begin(f"gm{pair}")
                pe.wait_ge(S("v_normed"), TT)
                for t in range(2):
                    g = 2 * pair + t
                    for n in range(TT):
                        ins = pe.matmul(ps[:, t * T + n * P:t * T + (n + 1) * P], v1[:, n, g * P:(g + 1) * P],
                                        gm_w[:, g, :], start=True, stop=True)
                ins.then_inc(S("side_full"), 1)

            def compress_hidden():
                ps = side_begin("hid")
                pe.wait_ge(S("kpe"), 1)
                pe.wait_ge(S("cw1"), 16)
                for c in range(2):
                    for g in range(2):
                        h = slice(HD * g, HD * g + HD)
                        for l in range(32):
                            ins = pe.matmul(ps[h, c * 16:c * 16 + N_CMP], cw1[h, c, l, :], kpe[h, c, l, 0:N_CMP],
                                            start=(l == 0), stop=(l == 31))
                ins.then_inc(S("side_full"), 1)

            def compress_out():
                side_begin("kvc2")
                for g in range(2):
                    ps = (bank[7], bank[4])[g]
                    h = slice(HD * g, HD * g + HD)
                    for half in range(2):
                        pe.matmul(ps[HD * half:HD * half + HD, g * 16:g * 16 + N_CMP], cw2[h, 0, :],
                                  hid_c[h, 0, 0:N_CMP], start=True, stop=True)
                    ins = pe.matmul(ps[0:N_CMP, P + g * HD:P + (g + 1) * HD], hid_c[h, 1, 0:N_CMP], cw2[h, 1, :],
                                    start=True, stop=True)
                ins.then_inc(S("side_full"), 1)

            def pairs(name, w, src, ready, count):
                ps = side_begin(name)
                pe.wait_ge(S(ready), count)
                for t in range(2):
                    m = 2 * int(name[-1]) + t
                    ins = pe.matmul(ps[:, t * T:(t + 1) * T], w[:, m, :], src[:, m, :], start=True, stop=True)
                ins.then_inc(S("side_full"), 1)

            def run_mg(j, half):
                if half:
                    half_unit(f"mg{j}", 1)
                    return
                if j in (1, 2):
                    gmlp(j - 1)
                if j == 2:
                    compress_hidden()
                if j == 3:
                    compress_out()
                if j in (7, 8):
                    pairs(f"wa{j - 7}", wa, xc, "xc", MT)
                if j in (9, 10):
                    pairs(f"wx{j - 9}", wx, xc, "xc", MT)
                if j in (11, 12):
                    pairs(f"po{j - 11}", pool_w, xd[:, :, 16:16 + T], "pooled", MT)
                half_unit(f"mg{j}", 0)

            def scores(n):
                h, kind = n // 3, n % 3
                hp, g = slice(HD * (h % 2), HD * (h % 2) + HD), h // 4
                ps = bank[n % 2]
                if n == 0:
                    pe.wait_ge(S("side_free"), SI["kvc2"] + 1)
                if n >= 2:
                    pe.wait_ge(S("sc_free"), n - 1)
                for t in range(TT):
                    q = q1[hp, h // 2, t * P:(t + 1) * P]
                    if kind == 0:
                        ins = pe.matmul(ps[:, t * 16:t * 16 + N_CMP], q, k_c[hp, g, 0:N_CMP], start=True, stop=True)
                    else:
                        k = kd[hp, 2 * (kind - 1) + g, :]
                        ins = pe.matmul(ps[:, P * t:P * t + P + P * t], q, k[:, 0:P * (t + 1)], start=True, stop=True)
                ins.then_inc(S("sc_full"), 1)

            def turn(n):
                pe.wait_ge(S("p_ok"), n + 1)
                if n >= 2:
                    pe.wait_ge(S("pt_free"), n - 1)
                ps = bank[2 + n % 2]
                src = p_cmp if n % 3 == 0 else att_p[n % 3]
                for b in range(2 if n % 3 == 0 else 3):
                    ins = pe.transpose(ps[:, b * P:(b + 1) * P], src[:, b * P:(b + 1) * P], C("ident"))
                ins.then_inc(S("pt_full"), 1)

            def values(n):
                h, kind = n // 3, n % 3
                g, pair = h // 4, h // 2
                pe.wait_ge(S("pt_free"), n + 1)
                if n % 6 == 0 and pair >= 1:
                    pe.wait_ge(S("o_free"), pair)
                o = bank[4][HD * (h % 2):HD * (h % 2) + HD, (pair % 2) * T:(pair % 2) * T + T]
                w = att_t[:, n % 2, :]
                if kind == 0:
                    ins = pe.matmul(o, v_c[:, g * HD:(g + 1) * HD], w[:, 0:T], start=True, stop=False)
                else:
                    v = vn[:, kind - 1, :].rearrange("p (t d) -> p t d", t=TT)[:, :, g * HD:(g + 1) * HD]
                    pe.matmul(o, v[:, 0, :], w[:, 0:T], start=False, stop=False)
                    ins = pe.matmul(o[:, P:T], v[:, 1, :], w[:, T:T + P], start=False, stop=(kind == 2))
                ins.then_inc(S("pv_done"), 1)

            def run_slot(n):
                if n < N_SLOTS:
                    scores(n)
                if 2 <= n < N_SLOTS + 2:
                    turn(n - 2)
                if n >= 3:
                    values(n - 3)

            schedule(run_slot, run_mg)

            ready = {0: ("zeroed", 1), 1: ("y_b", 1), 2: ("o_free", MT), 3: ("side_free", SI["po1"] + 1)}
            for n, y in ((0, u), (1, gate), (2, yc), (3, yd)):
                pe.wait_ge(S(ready[n][0]), ready[n][1])
                if n == 3:
                    pe.wait_ge(S("side_free"), SI["po1"] + 1)
                src = y
                for half in range(2):
                    unit = 2 * n + half
                    unit_ready(D_UNITS["branch"] + unit)
                    w = ring[:, (D_UNITS["branch"] + unit) % RING, :].rearrange("p (k n) -> p k n", k=MT)
                    if unit >= 2:
                        pe.wait_ge(S("br_free"), 2 * (unit - 1))
                    for d in range(4):
                        ps = bank[2 * half + d // 2][:, (d % 2) * T:(d % 2 + 1) * T]
                        for k in range(MT):
                            ins = pe.matmul(ps, w[:, k, d * P:(d + 1) * P], src[:, k, :], start=(k == 0),
                                            stop=(k == MT - 1))
                    ins.then_inc(S("unit_used"), 1)

            def square(name, src, ready, count):
                pe.wait_ge(S(ready), count)
                for n in range(SQUARE):
                    w = unit_ready(D_UNITS[name] + n)
                    for c in range(2):
                        ins = project(bank[n][:, c * T:(c + 1) * T], lambda k: w[:, k, c * P:(c + 1) * P], src)
                    ins.then_inc(S("unit_used"), 1)

            square("w_out", H, "merged", 1)
            norm_sums(1, "norm1")
            side_begin("route")
            pe.wait_ge(S("normed"), 2 * KD)
            w_route = P1("w_route").rearrange("p (k n) -> p k n", k=KD)
            project_tokens(bank[7], lambda k: w_route[:, k, :], 20).then_inc(S("side_full"), 1)

            def gated(name, steps, last_side):
                u0 = D_UNITS[name]

                def start_sums():
                    for b in range(4):
                        pe.matmul(bank[b][:, :], zeros[:, 0:P], zeros[:, :], start=True, stop=False)

                def gate_up(parity, n, static, s, h_ready=None):
                    if s is not None:
                        pe.wait_ge(S("hid_done"), s + 1)
                    for which in range(2):
                        pe.wait_ge(S("w_lo"), n + (n0 + which + 1))
                        w = parts(u0 + static + which, KD)
                        ps = bank[4 + 2 * parity + which]
                        for c in range(2):
                            ins = halves(ps[:, c * T:(c + 1) * T], lambda a, k: w[a][:, k, c * P:(c + 1) * P], h_hi, h_lo,
                                         KD, True, h_ready if which == 0 and c == 0 else None)
                        ins.then_inc(S("unit_used"), 1)

                def down(parity, n, static, s, last=False):
                    pe.wait_ge(S("hid_done"), s + 1)
                    pe.wait_ge(S("w_lo"), n + (n0 + 1))
                    w = parts(u0 + static, 2)
                    for d in range(KD):
                        ins = halves(bank[d // 2][:, (d % 2) * T:(d % 2 + 1) * T],
                                     lambda a, k: w[a][:, k, d * P:(d + 1) * P], hid_hi[:, parity, :, :],
                                     hid_lo[:, parity, :, :], 2, False)
                    if last:
                        for b in range(4):
                            ins = pe.matmul(bank[b][:, :], zeros[:, 0:P], zeros[:, :], start=False, stop=True)
                    ins.then_inc(S("unit_used"), 1)

                s0, n0 = STEP0[name], SPLIT0[name]
                start_sums()
                gate_up(0, 0, 0, None, NTH[name])
                pe.wait_ge(S("side_free"), SI[last_side] + 1)
                trips = (steps - 1) // 2
                with pe.Fori(0, trips) as i:
                    gate_up(1, i * 6 + 2, 2, i * 2 + s0)
                    down(0, i * 6 + 4, 4, i * 2 + (s0 + 1))
                    gate_up(0, i * 6 + 5, 5, i * 2 + (s0 + 1))
                    down(1, i * 6 + 7, 7, i * 2 + (s0 + 2))
                n2 = 6 * trips + 2
                if steps % 2 == 0:
                    gate_up(1, n2, n2, s0 + steps - 2)
                    down(0, n2 + 2, n2 + 2, s0 + steps - 1)
                    n2 += 3
                down((steps - 1) % 2, n2, n2, s0 + steps, last=True)

            def spread_weights():
                pe.wait_ge(S("combine"), TT)
                for n in range(8):
                    side_begin(f"comb{n}")
                    for c in range(2):
                        e = 2 * n + c
                        for t in range(TT):
                            w = route_pick[:, t, e:e + 1].to_broadcast([P, P])
                            ins = pe.matmul(bank[7][:, c * T + t * P:c * T + (t + 1) * P], w, C("ident"), start=True,
                                            stop=True)
                    ins.then_inc(S("side_full"), 1)

            spread_weights()
            gated("moe", MOE_STEPS, "comb7")
            norm_sums(2, "norm2")

            def pre_norm(n):
                norm_sums(n, f"n{n}")
                pe.wait_ge(S("normed"), (3 + (n - 3) // 2 + 1) * KD)

            def ffn(n, first):
                norm_sums(first, f"n{first}")
                gated(f"ffn{n}", FFN_STEPS, f"n{first}")
                norm_sums(first + 1, f"n{first + 1}")

            ffn(0, 3)
            pre_norm(5)

            def ab_unit(n):
                unit_channels(group_begin(f"ab{n}"), unit_ready(FULL[f"ab{n}"][1] - 1))

            for n in (6, 0, 1):
                ab_unit(n)
            pe.wait_ge(S("sm2"), 16)
            pe.wait_ge(S("added"), 4)
            pe.wait_ge(S("lora_in"), 1)
            for half in range(2):
                h = slice(HD * half, HD * half + HD)
                for m in range(MT):
                    ins = pe.matmul(bank[2 * half + m // 2][:, (m % 2) * T:(m % 2 + 1) * T],
                                    P2("lora")[h, m * P:(m + 1) * P], pp[h, 12, :], start=True, stop=True)
            ins.then_inc(S("lora_full"), 1)
            for n in (2, 3, 4, 5):
                ab_unit(n)
            for n in range(2):
                ps = side_begin(f"gu{n}")
                pe.wait_ge(S("gate_in"), 1)
                for c in range(2):
                    m = 2 * n + c
                    ins = pe.matmul(ps[:, c * T:(c + 1) * T], P2("gate_up")[:, m * P:(m + 1) * P], pp[:, 13, :],
                                    start=True, stop=True)
                ins.then_inc(S("side_full"), 1)
            ab_unit(9)

            def head_sums(name, src, ready, count):
                ps = side_begin(name)
                pe.wait_ge(S(ready), count)
                pe.matmul(ps[:, :], C("head1"), src, start=True, stop=True).then_inc(S("side_full"), 1)

            for n in range(2):
                head_sums(f"kk{n}", kkt[:, 2 * n:2 * n + 2, :], "kk_sq", 1)
            for n in (10, 7, 8):
                ab_unit(n)
            for n in range(2):
                head_sums(f"bo{n}", qt[:, 2 * n:2 * n + 2, :], "bonus_in", 1)
            pe.wait_ge(S("lora_out"), 2 * MT)
            pe.wait_ge(S("factors"), 1)
            for b, (src, c) in enumerate(((pp[:, 8:12, :], 0), (pp[:, 8:12, :], 1), (kh, 0), (bh, 0))):
                for m in range(MT):
                    ins = pe.transpose(bank[b][:, m * P:(m + 1) * P], src[:, m, c * P:(c + 1) * P], C("ident"))
            ins.then_inc(S("turned"), 1)
            pe.wait_ge(S("tok_ok"), 1)
            kq = arena[:, 0:2 * MT * T].rearrange("p (a m t) -> p a m t", a=2, m=MT)
            for c in range(TT):
                tok = slice(c * P, (c + 1) * P)
                for p in range(4):
                    for par in range(2):
                        job = 8 * c + 2 * p + par
                        h = slice(HD * par, HD * par + HD)
                        if job >= 4:
                            pe.wait_ge(S("gram_free"), job - 3)
                        ps = bank[par + 2 * (p % 2)]
                        for a, w in enumerate((kh, bh)):
                            ins = pe.matmul(ps[:, 2 * a * P:2 * (a + 1) * P], w[h, p, tok], kq[h, :, p, tok], start=True,
                                            stop=True)
                        ins.then_inc(S("gram_full"), 1)
                for par in range(2):
                    g, h = 2 * c + par, slice(HD * par, HD * par + HD)
                    if g >= 2:
                        pe.wait_ge(S("y_free"), g - 1)
                    else:
                        pe.wait_ge(S("proj_free"), GI["ab8"] + 1)
                    for p in range(4):
                        ins = pe.matmul(bank[5 + g % 2][:, p * P:(p + 1) * P], kkt[h, p, tok], bh[h, p, tok], start=True,
                                        stop=True)
                    ins.then_inc(S("y_full"), 1)

            def q_in(n):
                g = n % 4
                pe.wait_ge(S("mat_ok"), g + 1)
                if n >= 2:
                    pe.wait_ge(S("q_ok"), n - 1)
                if n >= 4:
                    pe.wait_ge(S("mw_ok"), n - 3)
                for i in range(4):
                    ins = pe.matmul(bank[n % 2][:, i * P:(i + 1) * P], mat_y[:, 4 * g + i, :], mat_m[:, 4 * g + i, :],
                                    start=True, stop=True)
                ins.then_inc(S("q_full"), 1)

            def mw_in(n):
                g = n % 4
                pe.wait_ge(S("q_ok"), n + 1)
                if n >= 2:
                    pe.wait_ge(S("mw_ok"), n - 1)
                for i in range(4):
                    q = mat_q[:, n % 2, i * P:(i + 1) * P]
                    ins = pe.matmul(bank[2 + n % 2][:, i * P:(i + 1) * P], mat_w[:, 4 * g + i, :], q, start=True, stop=True)
                    if n < N_INV - 4:
                        ins = pe.matmul(bank[5 + n % 2][:, i * P:(i + 1) * P], q, mat_w[:, 4 * g + i, :], start=True,
                                        stop=True)
                ins.then_inc(S("mw_full"), 1)

            pe.wait_ge(S("gram_free"), N_MAT)
            pe.wait_ge(S("y_free"), 4)
            for n in range(N_INV + 1):
                if n < N_INV:
                    q_in(n)
                if n:
                    mw_in(n - 1)
            pe.wait_ge(S("mw_ok"), N_INV)

            def mat(c, h, what=None):
                i = 8 * c + 4 * (h % 2) + h // 2
                return mat_m[:, i, :] if what is None else gram[:, i, what, :]

            diag_at = [0, 0]

            def conv_run():
                first = diag_at[1]
                if first == 0:
                    side_begin("conv")
                    pe.wait_ge(S("glu"), MT)
                for j in range(first, first + DIAG_RUNS[diag_at[0]]):
                    m, k = j // CONV_B, j % CONV_B
                    pe.wait_ge(S("diag_ok"), j + 1)
                    ins = pe.matmul(bank[7][:, m * T:(m + 1) * T], diag[:, j % DIAGS, :], glu[:, CONV_V + m, k:k + T],
                                    start=(k == 0), stop=(k == CONV_B - 1))
                    last = j + 1 == sum(DIAG_RUNS)
                    ins.then_inc(S("side_full" if last else "diag_used"), 1)
                diag_at[0], diag_at[1] = diag_at[0] + 1, j + 1

            for c in range(TT):
                tok = slice(c * P, (c + 1) * P)
                right, solved, ys = bank[4 * c], bank[4 * c + 1], bank[4 * c + 2]
                if c:
                    pe.wait_ge(S("state"), 1)

                def into(ps, factor, terms, last):
                    for p in range(4):
                        if c:
                            pe.matmul(ps[:, p * P:(p + 1) * P], factor[:, p, tok], state[:, p, :], start=True, stop=False)
                        for par in range(2):
                            h = 2 * p + par
                            cols_h = slice(h * HD, (h + 1) * HD)
                            for n, (which, rhs) in enumerate(terms):
                                ins = pe.matmul(ps[:, cols_h], mat(c, h, which), rhs[:, cols_h],
                                                start=(not c and n == 0), stop=(n == len(terms) - 1 and (not c or par == 1)))
                    return ins
                into(right, kkt, [(0, v_tok[:, c, :])], True).then_inc(S("rw_full"), 1)
                conv_run()
                pe.wait_ge(S("rw_r"), c + 1)
                for h in range(N_RW):
                    cols_h = slice(h * HD, (h + 1) * HD)
                    ins = pe.matmul(solved[:, cols_h], mat(c, h), rw_r[:, cols_h], start=True, stop=True)
                ins.then_inc(S("rw_full"), 1)
                conv_run()
                pe.wait_ge(S("rw_u"), c + 1)
                ins = into(ys, qt, [(1, v_tok[:, c, :]), (3, rw_u)], True)
                if c == 0:
                    for p in range(4):
                        cols_p = slice(p * P, (p + 1) * P)
                        pe.matmul(bank[3][:, cols_p], kh_tok[:, cols_p], v_tok[:, 0, cols_p], start=True, stop=False)
                        ins = pe.matmul(bank[3][:, cols_p], bh_tok[:, cols_p], rw_u[:, cols_p], start=False, stop=True)
                ins.then_inc(S("rw_full"), 1)
                conv_run()
            conv_run()
            pe.wait_ge(S("gn_y"), 1)
            for m in range(MT):
                for c in range(TT):
                    ins = pe.transpose(bank[m // 2][:, (m % 2) * T + c * P:(m % 2) * T + (c + 1) * P],
                                       rw_y[:, c, m * P:(m + 1) * P], C("ident"))
            ins.then_inc(S("y_turned"), 1)
            for name, src in (("ln1", cacc), ("ln2", ctmp)):
                ps = side_begin(name)
                if name == "ln2":
                    pe.wait_ge(S("ln_sq"), 1)
                for m in range(MT):
                    ins = pe.matmul(ps[:, 0:T], C("ones"), src[:, m, :], start=(m == 0), stop=(m == MT - 1))
                ins.then_inc(S("side_full"), 1)
            pe.wait_ge(S("y_rw"), 1)
            square("ab_out", H, "y_conv", MT)
            norm_sums(6, "n6")
            ffn(1, 7)
            ffn(2, 9)

            norm_sums(11, "n11")
            for n in range(8):
                split_channels(group_begin(f"c{n}"), "c", n)
                if n:
                    head_sums(f"hs{n - 1}", f_sq[:, (n - 1) % 2, :], "f_sq", n)
            head_sums("hs7", f_sq[:, 1, :], "f_sq", 8)
            ps = side_begin("f")
            w_f = P2("w_f").rearrange("p (k n) -> p k n", k=KD)
            project(ps[0:N_FOX, 0:T], lambda k: w_f[:, k, :]).then_inc(S("side_full"), 1)
            for n in range(8, 12):
                split_tokens(group_begin(f"c{n}"), "c", n)
            pe.wait_ge(S("f_cum"), 1)
            for n in range(8):
                ps = side_begin(f"cb{n}")
                for c in range(2):
                    h = 2 * n + c
                    pick = C("ident")[0:N_FOX, h:h + 1].to_broadcast([N_FOX, P])
                    ins = pe.matmul(ps[:, c * T:(c + 1) * T], pick, fc[0:N_FOX, :], start=True, stop=True)
                ins.then_inc(S("side_full"), 1)
            pe.wait_ge(S("hn_done"), 8)
            pe.wait_ge(S("proj_free"), GI["c11"] + 1)
            pe.wait_ge(S("added"), 16)

            def fox_slot(n):
                if n < N_FOX:
                    h = slice(HD * (n % 2), HD * (n % 2) + HD)
                    if n >= 2:
                        pe.wait_ge(S("fsc_free"), n - 1)
                    for t in range(TT):
                        ins = pe.matmul(bank[n % 2][:, P * t:P * t + P + P * t], fq[h, n // 2, t * P:(t + 1) * P],
                                        fq[h, KD + n // 2, 0:P * (t + 1)], start=True, stop=True)
                    ins.then_inc(S("fsc_full"), 1)
                if 2 <= n < N_FOX + 2:
                    b = n % 2
                    pe.wait_ge(S("fp_ok"), n - 1)
                    if n >= 4:
                        pe.wait_ge(S("fpt_free"), n - 3)
                    for a in range(3):
                        ins = pe.transpose(bank[2 + b][:, a * P:(a + 1) * P], fat_p[:, (n - 2) % 3, a * P:(a + 1) * P],
                                           C("ident"))
                    ins.then_inc(S("fpt_full"), 1)
                if n >= 3:
                    h, b = n - 3, (n - 3) % 2
                    pe.wait_ge(S("fpt_free"), n - 2)
                    pair = h // 2
                    if h % 2 == 0 and pair >= 1:
                        pe.wait_ge(S("fo_free"), pair)
                    o = bank[4][HD * (h % 2):HD * (h % 2) + HD, (pair % 2) * T:(pair % 2) * T + T]
                    pe.matmul(o, f_v[:, 0, h * HD:(h + 1) * HD], fat_t[:, b, 0:T], start=True, stop=False)
                    pe.matmul(o[:, P:T], f_v[:, 1, h * HD:(h + 1) * HD], fat_t[:, b, T:T + P], start=False, stop=True)\
                        .then_inc(S("fpv_done"), 1)

            fox_schedule(fox_slot, lambda j, half: half_unit(f"c{12 + j}", half))
            square("c_out", f_o, "fo_free", KD)
            norm_sums(12, "n12")
            ffn(3, 13)


INPUTS = ["x_t", "stream", "small_1", "cmp_w1", "small_2", "consts"]


def kernel(**inputs):
    import concourse.bacc as bacc
    from concourse.bass_utils import run_bass_kernel_spmd
    nc = bacc.Bacc("TRN2", target_bir_lowering=False, num_devices=1)
    given = lay_out(inputs)
    arrays, args = {}, []
    for name in INPUTS:
        a = given[name]
        arrays[f"in_{name}"] = a
        args.append(nc.dram_tensor(f"in_{name}", a.shape, mybir.dt.from_np(a.dtype), kind="ExternalInput").ap())
    out = nc.dram_tensor("out_x_t", (D, T), FP32, kind="ExternalOutput").ap()
    build(nc, *args, out)
    result = run_bass_kernel_spmd(nc, [arrays], core_ids=[0])
    return np.ascontiguousarray(result.results[0]["out_x_t"].T)[None]
```
